# Optimizing a Trainium2 kernel written in Bass

```python
import jax, jax.numpy as jnp
from jax import lax
import numpy as np

D_MODEL = 1024
BATCH = 1
SEQ = 512
DEPTH = 1

NSA_HEADS = 8
NSA_KV_GROUPS = 2
NSA_HEAD_DIM = 64
CMP_LEN = 32
CMP_STRIDE = 16
CMP_HIDDEN = 256
SEL_BLOCK = 64
SEL_TOPK = 16
WINDOW = 512
MLA_HEADS = 8
MLA_NOPE = 64
MLA_ROPE = 32
MLA_V = 64
MLA_Q_RANK = 384
MLA_KV_RANK = 256
ROPE_THETA = 10000.0
D_FF = 4 * D_MODEL
Q_BLOCK = 128
EPS = 1e-6
FORCE_BONUS = 1000.0

NSA_HG = NSA_HEADS // NSA_KV_GROUPS
NSA_Q_DIM = NSA_HEADS * NSA_HEAD_DIM
NSA_KV_DIM = NSA_KV_GROUPS * NSA_HEAD_DIM
IN_SPLITS = (NSA_Q_DIM, NSA_KV_DIM, NSA_KV_DIM, NSA_KV_DIM, NSA_KV_DIM, NSA_KV_DIM, NSA_KV_DIM,
             3 * NSA_HEADS, MLA_Q_RANK, MLA_KV_RANK, MLA_ROPE, D_MODEL, D_MODEL)
IN_DIM = sum(IN_SPLITS)


def rmsnorm(x, g):
    xf = x.astype(jnp.float32)
    y = xf * lax.rsqrt(jnp.mean(xf * xf, axis=-1, keepdims=True) + EPS)
    return (y * g.astype(jnp.float32)).astype(x.dtype)

def modulate(h, shift, scale):
    return h * (1.0 + scale[:, None, :]) + shift[:, None, :]

def masked_softmax(s, mask):
    s = jnp.where(mask, s, -jnp.inf)
    m = jnp.max(s, axis=-1, keepdims=True)
    m = jnp.where(jnp.isfinite(m), m, 0.0)
    e = jnp.exp(s - m)
    return e / jnp.maximum(jnp.sum(e, axis=-1, keepdims=True), 1e-30)

def alibi_slopes(n):
    return 2.0 ** (-8.0 * jnp.arange(1, n + 1, dtype=jnp.float32) / n)

def rope(x, cos, sin):
    half = x.shape[-1] // 2
    x1, x2 = x[..., :half], x[..., half:]
    return jnp.concatenate([x1 * cos - x2 * sin, x2 * cos + x1 * sin], axis=-1).astype(x.dtype)

def compress(kv, pe, w1, w2):
    B, S, G, dh = kv.shape
    r = CMP_LEN // CMP_STRIDE
    n_chunks = S // CMP_STRIDE
    nc = n_chunks - r + 1
    chunks = kv.reshape(B, n_chunks, CMP_STRIDE, G, dh)
    blocks = jnp.concatenate([chunks[:, i:i + nc] for i in range(r)], axis=2)
    blocks = blocks + pe[None, None, :, None, :]
    flat = blocks.transpose(0, 3, 1, 2, 4).reshape(B, G, nc, CMP_LEN * dh)
    return jax.nn.silu(flat @ w1) @ w2

def nsa_attention(q, kc, vc, ks, vs, kw, vw, gates):
    B, G, Hg, S, dh = q.shape
    nc = kc.shape[2]
    ns = S // SEL_BLOCK
    n_sel = min(SEL_TOPK, ns)
    n_key_sel = n_sel * SEL_BLOCK
    scale = dh ** -0.5
    slopes = alibi_slopes(G * Hg).reshape(1, G, Hg, 1, 1)
    c_start = jnp.arange(nc) * CMP_STRIDE
    c_end = c_start + CMP_LEN - 1
    s_start = jnp.arange(ns) * SEL_BLOCK
    overlap = ((c_start[:, None] < s_start[None, :] + SEL_BLOCK)
               & (c_end[:, None] >= s_start[None, :])).astype(jnp.float32)
    ks_blocks = ks.reshape(B, G, ns, SEL_BLOCK, dh)
    vs_blocks = vs.reshape(B, G, ns, SEL_BLOCK, dh)
    kw_pad = jnp.pad(kw, ((0, 0), (0, 0), (WINDOW, 0), (0, 0)))
    vw_pad = jnp.pad(vw, ((0, 0), (0, 0), (WINDOW, 0), (0, 0)))
    blk = jnp.arange(ns)
    in_blk = jnp.arange(SEL_BLOCK)
    win_off = jnp.arange(Q_BLOCK + WINDOW) - WINDOW
    gather = jax.vmap(jax.vmap(lambda kb, ix: kb[ix]))

    def block(qb):
        t0 = qb * Q_BLOCK
        t = t0 + jnp.arange(Q_BLOCK)
        qq = lax.dynamic_slice_in_dim(q, t0, Q_BLOCK, axis=3)
        g = lax.dynamic_slice_in_dim(gates, t0, Q_BLOCK, axis=4)
        dist_c = (t[:, None] - c_end[None, :]).astype(jnp.float32)
        s = jnp.einsum('bghqd,bgkd->bghqk', qq, kc).astype(jnp.float32) * scale - slopes * dist_c
        p_cmp = masked_softmax(s, dist_c >= 0)
        o_cmp = jnp.einsum('bghqk,bgkd->bghqd', p_cmp.astype(vc.dtype), vc)
        p_slc = jnp.einsum('bghqk,ks->bgqs', p_cmp, overlap)
        cur = t // SEL_BLOCK
        valid = blk[None, :] <= cur[:, None]
        forced = (blk[None, :] == 0) | (blk[None, :] >= cur[:, None] - 1)
        score = jnp.where(valid, p_slc + FORCE_BONUS * forced.astype(jnp.float32), -jnp.inf)
        _, idx = lax.top_k(score, n_sel)
        spos = idx[..., None] * SEL_BLOCK + in_blk
        smask = (spos <= t[:, None, None]).reshape(B, G, Q_BLOCK, n_key_sel)
        dist_s = (t[:, None, None] - spos).reshape(B, G, Q_BLOCK, n_key_sel).astype(jnp.float32)
        k_sel = gather(ks_blocks, idx).reshape(B, G, Q_BLOCK, n_key_sel, dh)
        v_sel = gather(vs_blocks, idx).reshape(B, G, Q_BLOCK, n_key_sel, dh)
        s = jnp.einsum('bghqd,bgqkd->bghqk', qq, k_sel).astype(jnp.float32) * scale - slopes * dist_s[:, :, None]
        p = masked_softmax(s, smask[:, :, None])
        o_sel = jnp.einsum('bghqk,bgqkd->bghqd', p.astype(vs.dtype), v_sel)
        k_win = lax.dynamic_slice_in_dim(kw_pad, t0, Q_BLOCK + WINDOW, axis=2)
        v_win = lax.dynamic_slice_in_dim(vw_pad, t0, Q_BLOCK + WINDOW, axis=2)
        wpos = t0 + win_off
        dist_w = t[:, None] - wpos[None, :]
        wmask = (dist_w >= 0) & (dist_w < WINDOW) & (wpos[None, :] >= 0)
        s = jnp.einsum('bghqd,bgkd->bghqk', qq, k_win).astype(jnp.float32) * scale - slopes * dist_w.astype(jnp.float32)
        p = masked_softmax(s, wmask)
        o_win = jnp.einsum('bghqk,bgkd->bghqd', p.astype(vw.dtype), v_win)
        o = g[0] * o_cmp + g[1] * o_sel + g[2] * o_win
        return o.transpose(0, 3, 1, 2, 4).reshape(B, Q_BLOCK, G * Hg * dh)

    out = lax.map(block, jnp.arange(S // Q_BLOCK))
    return out.transpose(1, 0, 2, 3).reshape(B, S, G * Hg * dh)

def mla_attention(q, k, v):
    B, H, S, dqk = q.shape
    dv = v.shape[-1]
    scale = dqk ** -0.5
    kpos = jnp.arange(S)

    def block(qb):
        t0 = qb * Q_BLOCK
        t = t0 + jnp.arange(Q_BLOCK)
        qq = lax.dynamic_slice_in_dim(q, t0, Q_BLOCK, axis=2)
        s = jnp.einsum('bhqd,bhkd->bhqk', qq, k).astype(jnp.float32) * scale
        p = masked_softmax(s, kpos[None, :] <= t[:, None])
        o = jnp.einsum('bhqk,bhkd->bhqd', p.astype(v.dtype), v)
        return o.transpose(0, 2, 1, 3).reshape(B, Q_BLOCK, H * dv)

    out = lax.map(block, jnp.arange(S // Q_BLOCK))
    return out.transpose(1, 0, 2, 3).reshape(B, S, H * dv)

def first_inputs(seed: int = 0) -> dict:
    key = jax.random.key(seed)
    ks = jax.random.split(key, 24)
    f32 = jnp.float32

    def nrm(k, shape, scale):
        return jax.random.normal(k, (DEPTH,) + shape, f32) * scale

    def gain(k, n):
        return 1.0 + 0.05 * jax.random.normal(k, (DEPTH, n), f32)

    dqk = MLA_NOPE + MLA_ROPE
    return {
        'x': jax.random.normal(ks[0], (BATCH, SEQ, D_MODEL), f32),
        'c': jax.random.normal(ks[1], (BATCH, D_MODEL), f32),
        'w_ada': nrm(ks[2], (D_MODEL, 6 * D_MODEL), 0.5 * D_MODEL ** -0.5),
        'b_ada': nrm(ks[3], (6 * D_MODEL,), 0.01),
        'g_mix': gain(ks[4], D_MODEL),
        'w_in': nrm(ks[5], (D_MODEL, IN_DIM), D_MODEL ** -0.5),
        'pe_ck': nrm(ks[6], (CMP_LEN, NSA_HEAD_DIM), 0.1),
        'w_ck1': nrm(ks[7], (CMP_LEN * NSA_HEAD_DIM, CMP_HIDDEN), (CMP_LEN * NSA_HEAD_DIM) ** -0.5),
        'w_ck2': nrm(ks[8], (CMP_HIDDEN, NSA_HEAD_DIM), CMP_HIDDEN ** -0.5),
        'pe_cv': nrm(ks[9], (CMP_LEN, NSA_HEAD_DIM), 0.1),
        'w_cv1': nrm(ks[10], (CMP_LEN * NSA_HEAD_DIM, CMP_HIDDEN), (CMP_LEN * NSA_HEAD_DIM) ** -0.5),
        'w_cv2': nrm(ks[11], (CMP_HIDDEN, NSA_HEAD_DIM), CMP_HIDDEN ** -0.5),
        'g_cq': gain(ks[12], MLA_Q_RANK),
        'w_uq': nrm(ks[13], (MLA_Q_RANK, MLA_HEADS * dqk), MLA_Q_RANK ** -0.5),
        'g_ckv': gain(ks[14], MLA_KV_RANK),
        'w_uk': nrm(ks[15], (MLA_KV_RANK, MLA_HEADS * MLA_NOPE), MLA_KV_RANK ** -0.5),
        'w_uv': nrm(ks[16], (MLA_KV_RANK, MLA_HEADS * MLA_V), MLA_KV_RANK ** -0.5),
        'w_o_nsa': nrm(ks[17], (NSA_Q_DIM, D_MODEL), NSA_Q_DIM ** -0.5),
        'w_o_mla': nrm(ks[18], (MLA_HEADS * MLA_V, D_MODEL), (MLA_HEADS * MLA_V) ** -0.5),
        'w_out': nrm(ks[19], (D_MODEL, D_MODEL), D_MODEL ** -0.5),
        'g_mlp': gain(ks[20], D_MODEL),
        'w_fc1': nrm(ks[21], (D_MODEL, D_FF), D_MODEL ** -0.5),
        'w_fc2': nrm(ks[22], (D_FF, D_MODEL), D_FF ** -0.5),
        'g_final': 1.0 + 0.05 * jax.random.normal(ks[23], (D_MODEL,), f32),
    }

def first_block(x, c, w_ada, b_ada, g_mix, w_in, pe_ck, w_ck1, w_ck2, pe_cv, w_cv1, w_cv2,
              g_cq, w_uq, g_ckv, w_uk, w_uv, w_o_nsa, w_o_mla, w_out, g_mlp, w_fc1, w_fc2, g_final):
    B, S, _ = x.shape
    G, Hg, dh = NSA_KV_GROUPS, NSA_HG, NSA_HEAD_DIM
    split_points = np.cumsum(IN_SPLITS)[:-1].tolist()
    half = MLA_ROPE // 2
    pos = jnp.arange(S, dtype=jnp.float32)
    inv_freq = ROPE_THETA ** (-jnp.arange(half, dtype=jnp.float32) / half)
    ang = pos[:, None] * inv_freq[None, :]
    cos, sin = jnp.cos(ang), jnp.sin(ang)

    def kv_groups(t):
        return t.reshape(B, S, G, dh)

    for layer in range(DEPTH):
        mod = c @ w_ada[layer] + b_ada[layer]
        sh_a, sc_a, gt_a, sh_m, sc_m, gt_m = jnp.split(mod, 6, axis=-1)

        h = modulate(rmsnorm(x, g_mix[layer]), sh_a, sc_a)
        z = h @ w_in[layer]
        (zq, zkc, zvc, zks, zvs, zkw, zvw, zg, zqd, zkvd, zkr, zga, zgb) = jnp.split(z, split_points, axis=-1)

        q_nsa = zq.reshape(B, S, G, Hg, dh).transpose(0, 2, 3, 1, 4)
        kc = compress(kv_groups(zkc), pe_ck[layer], w_ck1[layer], w_ck2[layer])
        vc = compress(kv_groups(zvc), pe_cv[layer], w_cv1[layer], w_cv2[layer])
        k_s = kv_groups(zks).transpose(0, 2, 1, 3)
        v_s = kv_groups(zvs).transpose(0, 2, 1, 3)
        k_w = kv_groups(zkw).transpose(0, 2, 1, 3)
        v_w = kv_groups(zvw).transpose(0, 2, 1, 3)
        nsa_gates = jax.nn.sigmoid(zg).reshape(B, S, 3, G, Hg).transpose(2, 0, 3, 4, 1)[..., None]
        o_nsa = nsa_attention(q_nsa, kc, vc, k_s, v_s, k_w, v_w, nsa_gates)

        cq = rmsnorm(zqd, g_cq[layer])
        qm = (cq @ w_uq[layer]).reshape(B, S, MLA_HEADS, MLA_NOPE + MLA_ROPE)
        q_rot = rope(qm[..., MLA_NOPE:], cos[:, None, :], sin[:, None, :])
        q_mla = jnp.concatenate([qm[..., :MLA_NOPE], q_rot], axis=-1)
        ckv = rmsnorm(zkvd, g_ckv[layer])
        k_nope = (ckv @ w_uk[layer]).reshape(B, S, MLA_HEADS, MLA_NOPE)
        v_mla = (ckv @ w_uv[layer]).reshape(B, S, MLA_HEADS, MLA_V)
        k_rot = rope(zkr, cos, sin)
        k_mla = jnp.concatenate(
            [k_nope, jnp.broadcast_to(k_rot[:, :, None, :], (B, S, MLA_HEADS, MLA_ROPE))], axis=-1)
        o_mla = mla_attention(q_mla.transpose(0, 2, 1, 3), k_mla.transpose(0, 2, 1, 3),
                              v_mla.transpose(0, 2, 1, 3))

        y = jax.nn.sigmoid(zga) * (o_nsa @ w_o_nsa[layer]) + jax.nn.sigmoid(zgb) * (o_mla @ w_o_mla[layer])
        x = x + gt_a[:, None, :] * (y @ w_out[layer])

        h = modulate(rmsnorm(x, g_mlp[layer]), sh_m, sc_m)
        x = x + gt_m[:, None, :] * (jnp.square(jax.nn.relu(h @ w_fc1[layer])) @ w_fc2[layer])

    return rmsnorm(x, g_final)


CHUNK = 64
HEAD_SIZE = 64
D_RWKV = D_MODEL
N_RWKV_HEADS = D_RWKV // HEAD_SIZE
D_CONV = D_MODEL
CONV_WIDTH = 31
D_DECAY_LORA = 64
D_AAA_LORA = 64
D_GATE_LORA = 128
D_FF_2 = 4 * D_MODEL
N_BRANCHES = 2
RMS_EPS = 1e-6
LN_EPS = 1e-5
GN_EPS = 64e-5
DECAY_OFFSET = 0.5
COL_RKV = 3 * D_RWKV
COL_GLU = 2 * D_CONV
COL_GATE = N_BRANCHES * D_MODEL
IN_COLS = COL_RKV + COL_GLU + COL_GATE


def _rmsnorm(x, g):
    xf = x.astype(jnp.float32)
    y = xf * lax.rsqrt(jnp.mean(xf * xf, axis=-1, keepdims=True) + RMS_EPS)
    return (y * g.astype(jnp.float32)).astype(x.dtype)

def _layernorm(x, g, b):
    xf = x.astype(jnp.float32)
    mu = jnp.mean(xf, axis=-1, keepdims=True)
    var = jnp.mean(jnp.square(xf - mu), axis=-1, keepdims=True)
    y = (xf - mu) * lax.rsqrt(var + LN_EPS)
    return (y * g.astype(jnp.float32) + b.astype(jnp.float32)).astype(x.dtype)

def _token_shift(z):
    return jnp.pad(z, ((0, 0), (1, 0), (0, 0)))[:, :-1]

def _heads(z):
    b, t, _ = z.shape
    return z.reshape(b, t, N_RWKV_HEADS, HEAD_SIZE)

def _wkv7_scan(r, w, k, v, kk, a):
    b, t, h, n = r.shape
    n_chunks = t // CHUNK

    def to_chunks(z):
        return jnp.moveaxis(z.astype(jnp.float32).reshape(b, n_chunks, CHUNK, h, n), (1, 2), (0, 1))

    def frame_step(S, inp):
        r_t, w_t, k_t, v_t, kk_t, a_t = inp
        sa = jnp.einsum('bhvk,bhk->bhv', S, -kk_t)
        S = (S * w_t[:, :, None, :]
             + sa[..., None] * (kk_t * a_t)[:, :, None, :]
             + v_t[..., None] * k_t[:, :, None, :])
        o_t = jnp.einsum('bhvk,bhk->bhv', S, r_t)
        return S, o_t

    def chunk_step(S, chunk_inp):
        return lax.scan(frame_step, S, chunk_inp)

    S0 = jnp.zeros((b, h, n, n), jnp.float32)
    inputs = (to_chunks(r), to_chunks(w), to_chunks(k), to_chunks(v), to_chunks(kk), to_chunks(a))
    _, o = lax.scan(chunk_step, S0, inputs)
    return jnp.moveaxis(o, (0, 1), (1, 2)).reshape(b, t, h, n)

def _rwkv7_mixer(h, r, k, v, mu_lora, w0, w1, w2, a0, a1, a2, g1, g2, k_k, k_a, r_k, ln_g, ln_b):
    dh = _token_shift(h) - h
    xw = h + dh * mu_lora[0]
    xa = h + dh * mu_lora[1]
    xg = h + dh * mu_lora[2]
    w_log = -jax.nn.softplus(-(w0 + jnp.tanh(xw @ w1) @ w2)) - DECAY_OFFSET
    decay = jnp.exp(-jnp.exp(w_log.astype(jnp.float32)))
    a = jax.nn.sigmoid(a0 + (xa @ a1) @ a2)
    g = jax.nn.sigmoid(xg @ g1) @ g2
    kk = _heads(k * k_k).astype(jnp.float32)
    kk = kk / jnp.maximum(jnp.linalg.norm(kk, axis=-1, keepdims=True), 1e-12)
    k = k * (1.0 + (a - 1.0) * k_a)
    rh, kh, vh, ah = _heads(r), _heads(k), _heads(v), _heads(a)
    o = _wkv7_scan(rh, _heads(decay), kh, vh, kk, ah)
    mu = jnp.mean(o, axis=-1, keepdims=True)
    var = jnp.mean(jnp.square(o - mu), axis=-1, keepdims=True)
    o = ((o - mu) * lax.rsqrt(var + GN_EPS)).reshape(h.shape[0], h.shape[1], D_RWKV)
    o = (o * ln_g.astype(jnp.float32) + ln_b.astype(jnp.float32)).astype(h.dtype)
    bonus = jnp.sum(rh * kh * r_k, axis=-1, keepdims=True) * vh
    o = o + bonus.reshape(o.shape)
    return o * g

def _conformer_conv_mixer(glu_in, conv_w, conv_b, ln_g, ln_b):
    u = glu_in[..., :D_CONV] * jax.nn.sigmoid(glu_in[..., D_CONV:])
    u = lax.conv_general_dilated(
        u, conv_w[:, None, :], window_strides=(1,), padding=((CONV_WIDTH - 1, 0),),
        dimension_numbers=('NWC', 'WIO', 'NWC'), feature_group_count=D_CONV) + conv_b
    u = _layernorm(u, ln_g, ln_b)
    return jax.nn.silu(u)

def second_inputs(seed: int = 0) -> dict:
    key = jax.random.key(seed)
    ks = iter(jax.random.split(key, 40))
    L = DEPTH
    f32 = jnp.float32

    def nrm(shape, scale):
        return jax.random.normal(next(ks), shape, f32) * scale

    def unif(shape, lo, hi):
        return jax.random.uniform(next(ks), shape, f32, minval=lo, maxval=hi)

    return {
        "x": nrm((BATCH, SEQ, D_MODEL), 1.0),
        "norm_mix_g": 1.0 + nrm((L, D_MODEL), 0.05),
        "w_in": nrm((L, D_MODEL, IN_COLS), D_MODEL ** -0.5),
        "b_gate": nrm((L, COL_GATE), 0.1),
        "mu_rkv": unif((L, COL_RKV), 0.0, 1.0),
        "mu_lora": unif((L, 3, D_MODEL), 0.0, 1.0),
        "decay_w0": unif((L, D_RWKV), -3.0, 2.0),
        "decay_w1": nrm((L, D_MODEL, D_DECAY_LORA), D_MODEL ** -0.5),
        "decay_w2": nrm((L, D_DECAY_LORA, D_RWKV), 0.1),
        "aaa_a0": nrm((L, D_RWKV), 0.1),
        "aaa_a1": nrm((L, D_MODEL, D_AAA_LORA), D_MODEL ** -0.5),
        "aaa_a2": nrm((L, D_AAA_LORA, D_RWKV), 0.5 * D_AAA_LORA ** -0.5),
        "gate_g1": nrm((L, D_MODEL, D_GATE_LORA), D_MODEL ** -0.5),
        "gate_g2": nrm((L, D_GATE_LORA, D_RWKV), D_GATE_LORA ** -0.5),
        "k_k": 0.85 + nrm((L, D_RWKV), 0.05),
        "k_a": 1.0 + nrm((L, D_RWKV), 0.05),
        "r_k": nrm((L, N_RWKV_HEADS, HEAD_SIZE), 0.1),
        "ln_x_g": 1.0 + nrm((L, D_RWKV), 0.05),
        "ln_x_b": nrm((L, D_RWKV), 0.02),
        "w_rwkv_proj": nrm((L, D_RWKV, D_MODEL), D_RWKV ** -0.5),
        "conv_w": nrm((L, CONV_WIDTH, D_CONV), CONV_WIDTH ** -0.5),
        "conv_b": nrm((L, D_CONV), 0.02),
        "conv_ln_g": 1.0 + nrm((L, D_CONV), 0.05),
        "conv_ln_b": nrm((L, D_CONV), 0.02),
        "w_conv_proj": nrm((L, D_CONV, D_MODEL), D_CONV ** -0.5),
        "w_out": nrm((L, D_MODEL, D_MODEL), D_MODEL ** -0.5),
        "norm_ff_g": 1.0 + nrm((L, D_MODEL), 0.05),
        "w_ff1": nrm((L, D_MODEL, D_FF_2), D_MODEL ** -0.5),
        "w_ff2": nrm((L, D_FF_2, D_MODEL), 0.5 * D_FF_2 ** -0.5),
        "norm_final_g": 1.0 + nrm((D_MODEL,), 0.05),
    }

def second_block(x, norm_mix_g, w_in, b_gate, mu_rkv, mu_lora, decay_w0, decay_w1, decay_w2,
              aaa_a0, aaa_a1, aaa_a2, gate_g1, gate_g2, k_k, k_a, r_k, ln_x_g, ln_x_b,
              w_rwkv_proj, conv_w, conv_b, conv_ln_g, conv_ln_b, w_conv_proj, w_out,
              norm_ff_g, w_ff1, w_ff2, norm_final_g):
    b, t, _ = x.shape
    for l in range(DEPTH):
        h = _rmsnorm(x, norm_mix_g[l])
        proj = h @ w_in[l]
        rkv = proj[..., :COL_RKV]
        glu_in = proj[..., COL_RKV:COL_RKV + COL_GLU]
        gate_logits = proj[..., COL_RKV + COL_GLU:] + b_gate[l]
        rkv = rkv + (_token_shift(rkv) - rkv) * mu_rkv[l]
        r = rkv[..., :D_RWKV]
        k = rkv[..., D_RWKV:2 * D_RWKV]
        v = rkv[..., 2 * D_RWKV:]
        a_out = _rwkv7_mixer(h, r, k, v, mu_lora[l], decay_w0[l], decay_w1[l], decay_w2[l],
                             aaa_a0[l], aaa_a1[l], aaa_a2[l], gate_g1[l], gate_g2[l],
                             k_k[l], k_a[l], r_k[l], ln_x_g[l], ln_x_b[l])
        c_out = _conformer_conv_mixer(glu_in, conv_w[l], conv_b[l], conv_ln_g[l], conv_ln_b[l])
        gates = jax.nn.sigmoid(gate_logits).reshape(b, t, N_BRANCHES, D_MODEL)
        merged = gates[:, :, 0] * (a_out @ w_rwkv_proj[l]) + gates[:, :, 1] * (c_out @ w_conv_proj[l])
        x = x + merged @ w_out[l]
        h2 = _rmsnorm(x, norm_ff_g[l])
        x = x + jnp.square(jax.nn.relu(h2 @ w_ff1[l])) @ w_ff2[l]
    return _rmsnorm(x, norm_final_g)


def setup_inputs(seed=0):
    out = dict(first_inputs(seed))
    for name, value in second_inputs(seed + 1).items():
        if name != "x":
            out[name + "_2"] = value
    return out


def reference(
    x, c, w_ada, b_ada, g_mix, w_in, pe_ck, w_ck1, w_ck2, pe_cv, w_cv1, w_cv2, g_cq, w_uq,
    g_ckv, w_uk, w_uv, w_o_nsa, w_o_mla, w_out, g_mlp, w_fc1, w_fc2, g_final, norm_mix_g_2,
    w_in_2, b_gate_2, mu_rkv_2, mu_lora_2, decay_w0_2, decay_w1_2, decay_w2_2, aaa_a0_2,
    aaa_a1_2, aaa_a2_2, gate_g1_2, gate_g2_2, k_k_2, k_a_2, r_k_2, ln_x_g_2, ln_x_b_2,
    w_rwkv_proj_2, conv_w_2, conv_b_2, conv_ln_g_2, conv_ln_b_2, w_conv_proj_2, w_out_2,
    norm_ff_g_2, w_ff1_2, w_ff2_2, norm_final_g_2,
):
    x = first_block(
        x, c, w_ada, b_ada, g_mix, w_in, pe_ck, w_ck1, w_ck2, pe_cv, w_cv1, w_cv2, g_cq, w_uq,
        g_ckv, w_uk, w_uv, w_o_nsa, w_o_mla, w_out, g_mlp, w_fc1, w_fc2, g_final,
    )
    return second_block(
        x, norm_mix_g_2, w_in_2, b_gate_2, mu_rkv_2, mu_lora_2, decay_w0_2, decay_w1_2,
        decay_w2_2, aaa_a0_2, aaa_a1_2, aaa_a2_2, gate_g1_2, gate_g2_2, k_k_2, k_a_2, r_k_2,
        ln_x_g_2, ln_x_b_2, w_rwkv_proj_2, conv_w_2, conv_b_2, conv_ln_g_2, conv_ln_b_2,
        w_conv_proj_2, w_out_2, norm_ff_g_2, w_ff1_2, w_ff2_2, norm_final_g_2,
    )


_drawn_inputs = setup_inputs


def setup_inputs(seed=0):
    import zlib

    import numpy as np

    out = dict(_drawn_inputs(seed))
    spreads = {}
    factors = {'b_ada': 2.791,
     'g_mix': 4.188,
     'pe_ck': 8.0,
     'pe_cv': 5.324,
     'g_cq': 8.0,
     'g_ckv': 7.805,
     'b_gate_2': 3.369,
     'aaa_a0_2': 3.689,
     'k_k_2': 28.258,
     'ln_x_g_2': 3.965,
     'ln_x_b_2': 8.0,
     'conv_b_2': 4.483,
     'conv_ln_g_2': 3.225,
     'conv_ln_b_2': 8.0,
     'norm_ff_g_2': 3.212}
    for name, (base, spread) in spreads.items():
        noise = np.random.default_rng([zlib.crc32(name.encode()), seed]).standard_normal(out[name].shape)
        drawn = base * np.exp(spread * noise) if base else spread * noise
        out[name] = __import__('jax').numpy.asarray(drawn.astype(out[name].dtype))
    for name, factor in factors.items():
        out[name] = (out[name] * factor).astype(out[name].dtype)
    return out
```

```python
from contextlib import ExitStack

import numpy as np
import concourse.bass as bass
from concourse import mybir

F32 = mybir.dt.float32
F32R = mybir.dt.float32r
ACT = mybir.ActivationFunctionType
ALU = mybir.AluOpType

P = 128
S = 512
D = 1024
KT = D // P
TT = S // P
DFF = 4 * D
NCH = DFF // D
H, G, DH = 8, 2, 64
HG = H // G
CL, CS, CHID = 32, 16, 256
NC = S // CS - CL // CS + 1
LP = CL * DH // P
MH, NOPE, ROPE, MV = 8, 64, 32, 64
DQK = NOPE + ROPE
QR, KVR = 384, 256
EPS = 1e-6
BIG = 1e30
RH, RN = 16, 64
CH = 64
NCK = S // CH
LEVELS = 5
CONV = 31
LORA = 64
LN_EPS, GN_EPS = 1e-5, 64e-5
DECAY = float(np.exp(np.float32(-0.5)))

NBANK = 7
OBANK = 7
NRAW, NHL = 4, 2


def vec_columns():
    names = [("c", 8), ("b_ada", 48), ("g_mix", 8), ("g_cq", 3), ("g_ckv", 2), ("g_mlp", 8), ("g_final", 8),
             ("pe_ck", LP), ("pe_cv", LP), ("w_ck2", 256), ("w_cv2", 128), ("norm_mix_g_2", 8), ("b_gate_2", 16), ("mu_rkv_2", 24),
             ("mu_lora_2", 24), ("decay_w0_2", 8), ("aaa_a0_2", 8), ("k_k_2", 8), ("k_a_2", 8), ("r_k_2", 8), ("ln_x_g_2", 8),
             ("ln_x_b_2", 8), ("conv_w_2", CONV * 8), ("conv_b_2", 8), ("conv_ln_g_2", 8), ("conv_ln_b_2", 8),
             ("norm_ff_g_2", 8), ("norm_final_g_2", 8)]
    at, n = {}, 0
    for name, w in names:
        at[name] = n
        n += w
    return at, n


VEC, NVEC = vec_columns()


def weight_blocks():
    out = [("raw", ("ada", n)) for n in range(16)]
    for m in range(16):
        out.append(("split", ("z", m)))
        out += [("raw", ("ada", 16 + 2 * m)), ("raw", ("ada", 17 + 2 * m))]
    out += [("raw", ("ck", kv, q)) for kv in range(2) for q in range(LP // 4)]
    out += [("split", ("uq", i)) for i in range(MH // 2)] + [("split", ("uk",)), ("split", ("uv",))]
    out += [("split", ("gate", m)) for m in range(16)]
    out += [("split", ("nm", m)) for m in range(KT)]
    out += [("split", ("wo", m)) for m in range(KT)]
    out += mlp_blocks(1)
    out += [("raw", ("lora", 0)), ("raw", ("lora", 1))]
    out += [("split", f) for f in rwkv_order() if f[0] in ("rkv", "glu")]
    out += [("split", ("gate2", m)) for m in range(16)]
    out += [("split", (n, m)) for m in range(KT) for n in ("pr", "pc")]
    out += [("split", ("wo2", m)) for m in range(KT)]
    return out + mlp_blocks(2)


def mlp_order():
    order = [(1, 0)]
    for c in range(1, NCH):
        order += [(1, c), (2, c - 1)]
    return order + [(2, NCH - 1)]


def mlp_blocks(n):
    return [("split", (f"fc{half}", n, c, m)) for half, c in mlp_order() for m in range(KT)]


def rwkv_order():
    inputs = [[("rkv", j, 1), ("rkv", j, 0), ("rkv", j, 2), ("lw2", j), ("la2", j), ("lg2", j)] for j in range(KT)]
    features = [[("kkss", j), ("bonus", j)] for j in range(KT)]
    glu = [[("glu", j, 1), ("glu", j, 0)] for j in range(KT)]
    turned = [[("tok", j, i) for i in range(4)] for j in range(KT)]
    out = inputs[0] + features[0] + glu[0] + turned[0]
    for j in range(KT):
        between = list(inputs[j + 1]) if j + 1 < KT else []
        for hh in range(2):
            out += [("mb", j, hh, 0), ("mb", j, hh, 1), ("mk", j, hh, 0), ("mk", j, hh, 1), ("inv", j, hh, 0), ("akv", j, hh)]
            for lv in range(1, LEVELS + 1):
                out.append(("ip", j, hh, lv))
                if lv <= 3 and between:
                    out.append(between.pop(0))
                out.append(("iy", j, hh, lv))
                if lv < LEVELS:
                    out.append(("inv", j, hh, lv))
            out += [("tav", j, hh), ("rr", j, hh), ("opart", j, hh)]
        out += [("pt", j, 0), ("pt", j, 1), ("qq", j, 0), ("qq", j, 1)]
        between = []
        if j + 1 < KT:
            out += features[j + 1]
            between = list(glu[j + 1])
        for c in range(1, NCK - 1):
            out.append(("st", j, c))
            if c in (1, 4) and between:
                out.append(between.pop(0))
        out += [("ost", j), ("gnm", j), ("gnv", j)]
        if j + 1 < KT:
            out += turned[j + 1]
    return out


POOL_F = 11
NO_BANK = ("opart", "ost")

BLOCKS = weight_blocks()
BLOCK_AT = {what: b for b, (_, what) in enumerate(BLOCKS)}
SPLIT_AT = {}
for _b, (_kind, _what) in enumerate(BLOCKS):
    if _kind == "split":
        SPLIT_AT[_what] = len(SPLIT_AT)
SPLITS = list(SPLIT_AT)


NSA_UNITS = [(h, qt, br) for h in range(H) for qt in range(TT) for br in range(3)]
MLA_UNITS = [(h, qt, None) for h in range(MH) for qt in range(TT)]
LAG_T, LAG_O = 2, 3


def attention_order(units):
    for i in range(len(units) + LAG_O):
        if i < len(units):
            yield "S", i
        if 0 <= i - LAG_T < len(units):
            yield "PT", i - LAG_T
        if i >= LAG_O:
            yield "O", i - LAG_O


def bank_order():
    out = [("ada", n) for n in range(16)] + [("ss", "mix")]
    for m in range(16):
        out += [("z", m), ("ada", 16 + 2 * m), ("ada", 17 + 2 * m)]
    out += [("vt", 0), ("vt", 1), ("gt",)]
    out += [("ck", kv, ht) for kv in range(2) for ht in range(2)] + [("kc",), ("vc",)]
    out += [("ss", "cq"), ("ss", "ckv")]
    out += [(k, "nsa", u) for k, u in attention_order(NSA_UNITS) if k != "O"]
    out += [("uq", h) for h in range(MH)] + [("uk", i) for i in range(MH // 2)] + [("uv", t) for t in range(TT)]
    out += [(k, "mla", u) for k, u in attention_order(MLA_UNITS) if k != "O"]
    out += [("gate", m) for m in range(16)]
    for m in range(KT):
        out += [("on", m), ("om", m)]
    out += [("wo", m) for m in range(KT)]
    out += [("ss", "mlp")] + [(f"fc{half}", 1, c, m) for half, c in mlp_order() for m in range(KT)]
    out += [("ss", "final"), ("ss", "mix2"), ("lh", 0), ("lh", 1), ("lh", 2)]
    out += [f for f in rwkv_order() if f[0] not in NO_BANK]
    out += [("convmean",), ("ss", "conv")]
    out += [("gate2", m) for m in range(16)]
    for m in range(KT):
        out += [("pr", m), ("pc", m)]
    out += [("wo2", m) for m in range(KT)]
    out += [("ss", "ff2")] + [(f"fc{half}", 2, c, m) for half, c in mlp_order() for m in range(KT)]
    return out + [("ss", "final2")]


BANK_ORDER = bank_order()
FILL = {name: n for n, name in enumerate(BANK_ORDER)}
BLOCK_LAST = {}
for _what in SPLITS:
    BLOCK_LAST[_what] = FILL[{"uq": lambda w: ("uq", 2 * w[1] + 1), "uk": lambda w: ("uk", MH // 2 - 1),
                              "uv": lambda w: ("uv", TT - 1), "nm": lambda w: ("om", w[1])}.get(_what[0], lambda w: w)(_what)]

NORMS = [("mix", KT), ("cq", 3), ("ckv", 2), ("mlp", KT), ("final", KT), ("mix2", KT), ("conv", KT), ("ff2", KT),
         ("final2", KT)]
SQ_AT = {}
for _name, _n in NORMS:
    for _k in range(_n):
        SQ_AT[_name, _k] = len(SQ_AT)

def split_order():
    out = [("mix", k) for k in range(KT)] + [("cq", k) for k in range(3)] + [("ckv", k) for k in range(2)]
    out += [("y", m) for m in range(KT)] + [("mlp", k) for k in range(KT)]
    out += [("hid", 1, c, m) for c in range(NCH) for m in range(KT)]
    out += [("mix2", k) for k in range(KT)] + [("conv", k) for k in range(KT)]
    out += [("y2", m) for m in range(KT)] + [("ff2", k) for k in range(KT)]
    return out + [("hid", 2, c, m) for c in range(NCH) for m in range(KT)]


SPLIT_EVENTS = split_order()
EVENT = {name: n for n, name in enumerate(SPLIT_EVENTS)}
NTMP = 3


def block1_constants():
    f = np.float32
    i = np.arange(P)[:, None]
    off = np.arange(S)[None, :] - (S - P)
    dist = (i - off).astype(f)
    slopes = (2.0 ** (-8.0 * np.arange(1, H + 1) / H)).astype(f)
    seen = off <= i
    alibi = np.where(seen[:, None], slopes[None, :, None] * dist[:, None], f(BIG)).astype(f)
    t = np.arange(S).reshape(TT, P).T[:, :, None, None]
    dc = (t - (np.arange(NC) * CS + CL - 1)).astype(f)
    cmpb = np.where(dc >= 0, slopes[None, None, :, None] * dc, f(BIG)).astype(f)
    causal = np.where(seen, f(0), f(BIG)).astype(f)
    half = ROPE // 2
    inv = (f(10000.0) ** (-np.arange(half, dtype=f) / f(half))).astype(f)
    ang = (np.arange(S, dtype=f)[:, None] * inv[None, :]).astype(f)
    cos, sin = np.cos(ang).T.astype(f), np.sin(ang).T.astype(f)
    rope = np.zeros((P, S), f)
    rope[64:96] = np.concatenate([cos, cos])
    rope[96:128] = np.concatenate([-sin, sin])
    return {"eye_ones": np.concatenate([np.eye(P, dtype=f), np.ones((P, P), f)], 1), "alibi": alibi.reshape(P, H * S),
            "cmpb": cmpb.reshape(P, TT * H * NC), "causal": causal, "rope": rope}


def rwkv_constants():
    i, t = np.arange(P)[:, None], np.arange(P)[None, :]
    same = i // CH == t // CH
    out = [same & (i < t), same & (i <= t)]
    for lv in range(LEVELS + 1):
        b = 1 << lv
        joins = (i // (2 * b) == t // (2 * b)) & (i // b % 2 == 0) & (t // b % 2 == 1)
        out.append(joins if lv == 0 else joins.T)
    out.append(i // RN == t // RN)
    return np.concatenate(out, 1).astype(np.float32)


CONSTS = {"rw": (2 + LEVELS + 1 + 1) * P, "eye_ones": 2 * P, "alibi": H * S, "cmpb": TT * H * NC, "causal": S, "rope": S}


def build_program(nc, io):
    x_in, vec_in, w_in, out = io["x"], io["vec"], io["w"], io["out"]
    ctx = ExitStack()
    with ctx:
        def sb(name, shape, dt=F32, at=ctx):
            return at.enter_context(nc.sbuf_tensor(name, shape, dt))

        def sem(name):
            return ctx.enter_context(nc.semaphore(name))

        x = sb("x", [P, KT, S])
        vec = sb("vec", [P, NVEC])
        eye_ones = sb("eye_ones", [P, 2 * P])
        eye, ones = eye_ones[:, 0:P], eye_ones[:, P:2 * P]
        raw = sb("raw", [P, NRAW, D])
        whi = sb("whi", [P, NHL, D], F32R)
        wlo = sb("wlo", [P, NHL, D], F32R)
        ah = sb("ah", [P, 2, KT, S], F32R)
        tmp = sb("tmp", [P, NTMP, S])
        sq = sb("sq", [P, 2, S])
        rstd = sb("rstd", [P, S])
        mod = sb("mod", [P, 48])
        modg = sb("modg", [P, 2 * KT])
        psum = ctx.enter_context(nc.psum_tensor("psum", [P, 8, S], F32))

        mixer = ExitStack()
        oh = sb("oh", [P, 2, KT, S], F32R, mixer)
        with ExitStack() as at:
            cqh = sb("cqh", [P, 2, 5, S], F32R, at)
            zkr = sb("zkr", [P, S], F32, at)
            rope = sb("rope", [P, S], F32, at)
            causal = sb("causal", [P, S], F32, at)
            with ExitStack() as nsa:
                qT = sb("qT", [P, H // 2, S], F32, nsa)
                ksd = sb("ksd", [P, G, S], F32, nsa)
                kwd = sb("kwd", [P, G, S], F32, nsa)
                vtok = sb("vtok", [P, 2, TT, P], F32, nsa)
                kcT = sb("kcT", [P, G * NC], F32, nsa)
                vc = sb("vc", [P, G * DH], F32, nsa)
                gates = sb("gates", [P, TT, 32], F32, nsa)
                alibi = sb("alibi", [P, H, S], F32, nsa)
                cmpb = sb("cmpb", [P, TT, H, NC], F32, nsa)
                sm = sb("sm", [P, 3, S], F32, nsa)
                pt = sb("pt", [P, 2, S], F32, nsa)
                gT = zkr[0:32, :]
                stat = sb("stat", [P, 3, 4], F32, nsa)
            with ExitStack() as mla:
                qcat = sb("qcat", [P, MH, S], F32, mla)
                kcat = sb("kcat", [P, MH, S], F32, mla)
                vm = sb("vm", [P, TT, MH * MV], F32, mla)
                rtmp = sb("rtmp", [P, S], F32, mla)
                sm2 = sb("sm2", [P, 3, S], F32, mla)
                pt2 = sb("pt2", [P, 2, S], F32, mla)
                stat2 = sb("stat2", [P, 3, 4], F32, mla)
        with ExitStack() as at:
            yh = sb("yh", [P, 2, KT, S], F32R, at)
            sg = sb("sg", [P, 16, S], F32, at)
        mixer.close()
        with ExitStack() as at:
            kcd = sb("kcd", [P, 2, G, S], F32, at)
            bkv = sb("bkv", [P, 2, LP, G * NC], F32, at)
            hid = sb("hid", [P, 2, 2, G * NC], F32, at)
            vT = sb("vT", [P, 2, S], F32, at)
            zd = sb("zd", [P, 5, S], F32, at)
        with ExitStack() as at:
            def work(name, cols):
                return sb(name, [P, cols], F32, at)

            rw = work("rw", CONSTS["rw"])
            rkvp = work("rkvp", 3 * (S + 1))[:, :].rearrange("p (i s) -> p i s", i=3)
            rkv = work("rkv", 3 * S)[:, :].rearrange("p (i s) -> p i s", i=3)
            lh = work("lh", 2 * S)[:, :].rearrange("p (i s) -> p i s", i=2)
            lwt = work("lwt", 4 * P)[:, :].rearrange("p (i n) -> p i n", i=2)
            upad = work("upad", S + CONV - 1)
            arow = work("arow", 2 * S)[:, :].rearrange("p (t a n) -> p t a n", t=TT, a=2)
            bh, kh = work("bh", S), work("kh", S)
            ew, ewi, ewp = work("ew", S), work("ewi", S), work("ewp", S)
            sw, cw, rate, kk = work("sw", S), work("cw", S), work("rate", S), work("kk", S)
            bv = work("bv", 2 * S)[:, :].rearrange("p (i s) -> p i s", i=2)
            gate = work("gate", 2 * S)[:, :].rearrange("p (i s) -> p i s", i=2)
            wc = work("wc", 2 * NCK)[:, :].rearrange("p (i c) -> p i c", i=2)
            ao = work("ao", KT * S)[:, :].rearrange("p (k s) -> p k s", k=KT)
            mb = work("mb", 4 * 2 * P)[:, :].rearrange("p (t n) -> p t n", t=TT)
            mk = work("mk", 4 * 2 * P)[:, :].rearrange("p (t n) -> p t n", t=TT)
            ix, iy, ip = (work(n, S)[:, :].rearrange("p (t n) -> p t n", t=TT) for n in ("ix", "iy", "ip"))
            ftok = work("ftok", 2 * S)[:, :].rearrange("p (t h a n) -> p t h a n", t=TT, h=2, a=2)
            tav = work("tav", 2 * S)[:, :].rearrange("p (t a h n) -> p t a h n", t=TT, a=2, h=2)
            btok, ktok, vtk = (work(n, S)[:, :].rearrange("p (t n) -> p t n", t=TT) for n in ("btok", "ktok", "vtk"))
            rp = work("rp", S)
            pts = work("pts", NCK * P)[:, :].rearrange("p (c n) -> p c n", c=NCK)
            qs = work("qs", NCK * RN)[:, :].rearrange("p (c n) -> p c n", c=NCK)
            st = work("st", NCK * RN)[:, :].rearrange("p (c n) -> p c n", c=NCK)
        usig, og, tf, nrm = tmp[:, 0, :], tmp[:, 1, :], tmp[:, 2, :], rstd[:, :]
        strict_incl = rw[:, 0:2 * P]
        level = [rw[:, (2 + lv) * P:(3 + lv) * P] for lv in range(LEVELS + 1)]
        heads = rw[:, (3 + LEVELS) * P:(4 + LEVELS) * P]
        with ExitStack() as at:
            aoh = sb("aoh", [P, 2, KT, S], F32R, at)
            coh = sb("coh", [P, 2, KT, S], F32R, at)
            sg2 = sb("sg2", [P, 16, S], F32, at)
        x_kept = nc.dram_tensor("x_kept", (P, KT * S), F32, kind="Internal").ap()
        with ExitStack() as at:
            hidden = [sb(f"hidden{i}", [P, 2, KT, S], F32R, at) for i in range(2)]

        x_loaded, vec_loaded = sem("x_loaded"), sem("vec_loaded")
        const_loaded = {n: sem(f"{n}_loaded") for n in CONSTS}
        w_loaded = [sem(f"w_loaded{i}") for i in range(NRAW)]
        raw_used = sem("raw_used")
        hi_done, lo_done = sem("hi_done"), sem("lo_done")
        filled = sem("filled")
        emptied = [sem(f"emptied{i}") for i in range(NBANK)]
        dve_step, act_step = sem("dve_step"), sem("act_step")
        sq_ready, sq_used = sem("sq_ready"), sem("sq_used")
        root_done = sem("root_done")
        pre_split, hi_ready, hl_ready = sem("pre_split"), sem("hi_ready"), sem("hl_ready")
        modg_ready = sem("modg_ready")
        bkv_ready = sem("bkv_ready")
        exp_done, p_ready, o_done = sem("exp_done"), sem("p_ready"), sem("o_done")
        o_hi, o_empty = sem("o_hi"), sem("o_empty")
        nope_done, rope_done, krot_done = sem("nope_done"), sem("rope_done"), sem("krot_done")
        xn_ready = sem("xn_ready")
        zeros_done = sem("zeros_done")
        hp_ready, xm_ready, xm_used = sem("hp_ready"), sem("xm_ready"), sem("xm_used")
        lw_loaded = [sem(f"lw_loaded{i}") for i in range(2)]
        pool_f = sem("pool_f")
        mix_done = sem("mix_done")
        cw_ready, exp_ready = sem("cw_ready"), sem("exp_ready")
        kk0_ready, kksq_ready, nrm_ready = sem("kk0_ready"), sem("kksq_ready"), sem("nrm_ready")
        kmod_ready, rk_ready, at_ready = sem("kmod_ready"), sem("rk_ready"), sem("at_ready")
        iy0_done, pool_step = sem("iy0_done"), sem("pool_step")
        opart_done, ost_done, og_ready = sem("opart_done"), sem("ost_done"), sem("og_ready")
        st_ready, gnsq_ready, gnroot_done, ao_done = sem("st_ready"), sem("gnsq_ready"), sem("gnroot_done"), sem("ao_done")
        conv_done, cen_ready, convn_ready = sem("conv_done"), sem("cen_ready"), sem("convn_ready")
        ao_hi, ao_ready = sem("ao_hi"), sem("ao_ready")
        x_put, x_back = sem("x_put"), sem("x_back")
        stored = sem("stored")

        def bank(name):
            return psum[:, FILL[name] % NBANK, :]

        def wait_filled(eng, name):
            eng.wait_ge(filled, FILL[name] + 1)

        def wait_emptied(eng, name):
            eng.wait_ge(emptied[FILL[name] % NBANK], FILL[name] // NBANK + 1)

        def emptied_by(ins, name):
            ins.then_inc(emptied[FILL[name] % NBANK], 1)

        def vcol(name, k=0, n=1):
            return vec[:, VEC[name] + k:VEC[name] + k + n]

        def wait_loaded(eng, what):
            b = BLOCK_AT[what]
            eng.wait_ge(w_loaded[b % NRAW], 16 * (b // NRAW + 1))

        def raw_of(what):
            return raw[:, BLOCK_AT[what] % NRAW, :]

        def xm(i, k):
            t = (mb, mk)[k % 2][:, :, :].rearrange("p t n -> p (t n)")
            return t[:, i * S:i * S + S] if i < 2 else (ix, iy)[k % 2][:, :, :].rearrange("p t n -> p (t n)")

        def state(c):
            return qs[:, 0, :] if c == 1 else st[:, c, :]

        block = ctx.enter_context(nc.Block())

        @block.sync
        def _(sp):
            sp.dma_start(vec[:, :], vec_in).then_inc(vec_loaded, 16)
            sp.dma_start(x[:, :, :], x_in.rearrange("p (k s) -> p k s", k=KT)).then_inc(x_loaded, 16)
            sp.dma_start(eye_ones[:, :], io["eye_ones"]).then_inc(const_loaded["eye_ones"], 16)
            raws = 0
            for b, (kind, what) in enumerate(BLOCKS):
                if b >= NRAW:
                    old_kind, old = BLOCKS[b - NRAW]
                    if old_kind == "split":
                        sp.wait_ge(lo_done, SPLIT_AT[old] + 1)
                    elif old[0] == "ck" and old[2] < LP // 4 - 1:
                        raws += 1
                        sp.wait_ge(raw_used, raws)
                    elif old[0] == "lora":
                        wait_filled(sp, ("lh", 2))
                    else:
                        wait_filled(sp, old if old[0] != "ck" else ("ck", old[1], 1))
                sp.dma_start(raw[:, b % NRAW, :], w_in[b]).then_inc(w_loaded[b % NRAW], 16)
                if what == ("ada", 15):
                    for n, t in (("rope", rope), ("causal", causal), ("cmpb", cmpb), ("alibi", alibi)):
                        dst = {"cmpb": "p a b c -> p (a b c)", "alibi": "p a b -> p (a b)"}.get(n)
                        sp.dma_start(t.rearrange(dst) if dst else t[:, :], io[n]).then_inc(const_loaded[n], 16)
            sp.wait_ge(xn_ready, 2 * KT)
            sp.dma_start(out.rearrange("p (k s) -> p k s", k=KT), x[:, :, :]).then_inc(stored, 16)
            sp.wait_ge(stored, 16)

        @block.gpsimd
        def _(pool):
            low = [0]

            def weights_ahead(n):
                while low[0] <= min(n, len(SPLITS) - 1):
                    s = low[0]
                    pool.wait_ge(hi_done, s + 1)
                    pool.tensor_tensor(wlo[:, s % NHL, :], raw_of(SPLITS[s]), whi[:, s % NHL, :].bitcast(F32),
                                       ALU.subtract).then_inc(lo_done, 1)
                    low[0] += 1

            weights_ahead(SPLIT_AT["rkv", 0, 1] - 1)
            wait_filled(pool, ("fc2", 1, NCH - 1, KT - 1))
            pool.memset(rkvp[:, :, 0:1], 0.0).then_inc(zeros_done, 1)
            pool.memset(upad[:, 0:CONV - 1], 0.0).then_inc(zeros_done, 1)
            weights_ahead(SPLIT_AT["rkv", 0, 1])
            pool.wait_ge(zeros_done, 2)
            for k in range(KT):
                pool.wait_ge(hl_ready, EVENT["mix2", k] + 1)
                if k >= 2:
                    pool.wait_ge(xm_ready, 3 * (k - 1))
                hp = rkvp[:, k % 2, :]
                pool.tensor_tensor(hp[:, 1:S + 1], ah[:, 0, k, :].bitcast(F32), ah[:, 1, k, :].bitcast(F32), ALU.add).then_inc(hp_ready, 1)
                pool.wait_ge(hp_ready, 2 * k + 1)
                pool.tensor_tensor(rkv[:, k % 2, :], hp[:, 0:S], hp[:, 1:S + 1], ALU.subtract).then_inc(hp_ready, 1)
            psteps = 0
            for f in rwkv_order():
                kind, j = f[0], f[1]
                if kind in ("rkv", "glu"):
                    weights_ahead(SPLIT_AT[f] + 1)
                if kind == "rkv":
                    i = f[2]
                    wait_emptied(pool, f)
                    if j:
                        pool.wait_ge(rk_ready, j)
                        wait_emptied(pool, ("bonus", j - 1))
                        wait_filled(pool, ("tok", j - 1, 3))
                    else:
                        pool.wait_ge(xm_ready, 3 * KT)
                    pool.tensor_tensor(rkv[:, i, :], rkvp[:, i, 0:S], rkvp[:, i, 1:S + 1], ALU.subtract).then_inc(pool_f, 1)
                elif kind == "kkss":
                    n = POOL_F * j
                    pool.wait_ge(cw_ready, j + 1)
                    pool.tensor_tensor(sw[:, :], cw[:, :], sw[:, :], ALU.subtract).then_inc(pool_f, 1)
                    pool.wait_ge(nrm_ready, j + 1)
                    pool.tensor_tensor(kk[:, :], kk[:, :], nrm, ALU.mult).then_inc(pool_f, 1)
                    pool.wait_ge(mix_done, 3 * j + 2)
                    pool.wait_ge(exp_ready, 3 * j + 2)
                    if j:
                        wait_filled(pool, ("mk", j - 1, 1, 1))
                        wait_emptied(pool, ("rr", j - 1, 1))
                    pool.tensor_tensor(arow[:, :, 1, :], rkv[:, 0, :].rearrange("p (t n) -> p t n", t=TT),
                                       ew[:, :].rearrange("p (t n) -> p t n", t=TT), ALU.mult).then_inc(pool_f, 1)
                    pool.wait_ge(pool_f, n + 5)
                    wait_emptied(pool, ("la2", j))
                    pool.wait_ge(kmod_ready, j + 1)
                    pool.tensor_tensor(rate[:, :], kk[:, :], rate[:, :], ALU.mult).then_inc(pool_f, 1)
                    pool.wait_ge(pool_f, n + 7)
                    pool.tensor_tensor(bh[:, :], rate[:, :], ewi[:, :], ALU.mult).then_inc(pool_f, 1)
                    pool.tensor_tensor(kh[:, :], rkv[:, 1, :], ewi[:, :], ALU.mult).then_inc(pool_f, 1)
                    pool.wait_ge(exp_ready, 3 * j + 3)
                    end = ew[:, :].rearrange("p (c n) -> p c n", c=NCK)[:, :, CH - 1:CH].to_broadcast([P, NCK, CH])
                    for dst, src, done in ((sw, bh, 8), (cw, kh, 9)):
                        pool.wait_ge(pool_f, n + done)
                        pool.tensor_tensor(dst[:, :].rearrange("p (c n) -> p c n", c=NCK),
                                           src[:, :].rearrange("p (c n) -> p c n", c=NCK), end, ALU.mult).then_inc(pool_f, 1)
                elif kind == "inv" and f[3] == 0:
                    wait_emptied(pool, ("mb", j, f[2], 0))
                    wait_emptied(pool, ("mb", j, f[2], 1))
                    if (j, f[2]) != (0, 0):
                        wait_filled(pool, ("tav", j - 1 if f[2] == 0 else j, 1 - f[2]))
                    pool.tensor_tensor(iy[:, :, :], mb[:, :, 0:P], level[0].unsqueeze(1).to_broadcast([P, TT, P]),
                                       ALU.mult).then_inc(pool_step, 1)
                    psteps += 1
                    pool.wait_ge(pool_step, psteps)
                    pool.tensor_tensor(iy[:, :, :], iy[:, :, :], eye.unsqueeze(1).to_broadcast([P, TT, P]),
                                       ALU.add).then_inc(iy0_done, 1)
            weights_ahead(len(SPLITS))

        @block.tensor
        def _(pe):
            fills = [0]

            def begin(name):
                n = FILL[name]
                assert n == fills[0], (name, BANK_ORDER[fills[0]])
                fills[0] += 1
                if n >= NBANK:
                    pe.wait_ge(emptied[n % NBANK], n // NBANK)

            def three(dst, w, wcols, a, k, first, last, a_moving=True):
                wh, wl = whi[:, w, wcols], wlo[:, w, wcols]
                h_, l_ = a[:, 0, k], a[:, 1, k]
                if a_moving:
                    pe.matmul(dst, wh, h_, start=first, stop=False)
                    pe.matmul(dst, wh, l_, start=False, stop=False)
                    return pe.matmul(dst, wl, h_, start=False, stop=last)
                pe.matmul(dst, h_, wh, start=first, stop=False)
                pe.matmul(dst, l_, wh, start=False, stop=False)
                return pe.matmul(dst, h_, wl, start=False, stop=last)

            def product(name, what, a, kts, col0=0, event=None):
                s = SPLIT_AT[what]
                pe.wait_ge(lo_done, s + 1)
                begin(name)
                for i, k in enumerate(kts):
                    if event is not None:
                        pe.wait_ge(hl_ready, EVENT[event + (i,)] + 1)
                    mm = three(bank(name), s % NHL, slice(col0 + i * P, col0 + i * P + P), a, k, i == 0, i == len(kts) - 1)
                mm.then_inc(filled, 1)

            def ada(n):
                what = ("ada", n)
                wait_loaded(pe, what)
                begin(what)
                for k in range(KT):
                    mm = pe.matmul(bank(what)[:, 0:1], raw_of(what)[:, k * P:k * P + P], vcol("c", k),
                                   start=k == 0, stop=k == KT - 1)
                mm.then_inc(filled, 1)

            def sum_squares(name):
                tiles = dict(NORMS)[name]
                begin(("ss", name))
                for k in range(tiles):
                    n = SQ_AT[name, k]
                    pe.wait_ge(sq_ready, n + 1)
                    mm = pe.matmul(bank(("ss", name)), ones, sq[:, n % 2, :], start=k == 0, stop=k == tiles - 1)
                    mm.then_inc(sq_used if k < tiles - 1 else filled, 1)

            def attention(tag, units, at):
                base = {"nsa": 0, "mla": len(NSA_UNITS)}[tag]
                for kind, u in attention_order(units):
                    h, qt, br = units[u]
                    probs, turned, scores, values = at
                    if kind == "S":
                        q, k, w = scores(h, qt, br)
                        begin(("S", tag, u))
                        pe.matmul(bank(("S", tag, u))[:, 0:w], q, k, start=True, stop=True).then_inc(filled, 1)
                    elif kind == "PT":
                        begin(("PT", tag, u))
                        pe.wait_ge(p_ready, base + u + 1)
                        for kt, (_, n) in enumerate(values(h, qt, br)):
                            mm = pe.transpose(bank(("PT", tag, u))[0:n, kt * P:kt * P + P],
                                              probs[:, u % 3, kt * P:kt * P + n], eye)
                        mm.then_inc(filled, 1)
                    else:
                        wait_emptied(pe, ("PT", tag, u))
                        pair = base_pair[tag] + h // 2
                        if h % 2 == 0 and qt == 0 and br in (0, None) and pair:
                            pe.wait_ge(o_empty, pair)
                        rows = slice(64 * (h % 2), 64 * (h % 2) + 64)
                        vals = values(h, qt, br)
                        for kt, (v, n) in enumerate(vals):
                            mm = pe.matmul(psum[rows, OBANK, qt * P:qt * P + P], v, turned[0:n, u % 2, kt * P:kt * P + P],
                                           start=br in (0, None) and kt == 0, stop=br in (2, None) and kt == len(vals) - 1)
                        mm.then_inc(o_done, 1)

            base_pair = {"nsa": 0, "mla": H // 2}

            pe.wait_ge(vec_loaded, 16)
            for n in range(16):
                ada(n)
            pe.wait_ge(const_loaded["eye_ones"], 16)
            sum_squares("mix")
            for m in range(16):
                product(("z", m), ("z", m), ah, range(KT), event=("mix",) if m == 0 else None)
                ada(16 + 2 * m)
                ada(17 + 2 * m)
            for i, m in enumerate((7, 9)):
                begin(("vt", i))
                wait_emptied(pe, ("z", m))
                for t in range(TT):
                    mm = pe.transpose(bank(("vt", i))[:, t * P:t * P + P], vT[:, i, t * P:t * P + P], eye)
                mm.then_inc(filled, 1)
            begin(("gt",))
            wait_emptied(pe, ("z", 10))
            for t in range(TT):
                mm = pe.transpose(bank(("gt",))[:, t * 32:t * 32 + 32], gT[:, t * P:t * P + P], eye[0:32, 0:32])
            mm.then_inc(filled, 1)
            for kv in range(2):
                begin(("ck", kv, 0))
                begin(("ck", kv, 1))
                pe.wait_ge(bkv_ready, kv + 1)
                for q in range(LP // 4):
                    wait_loaded(pe, ("ck", kv, q))
                    w = raw_of(("ck", kv, q))
                    for ht in range(2):
                        for i in range(4):
                            lp = 4 * q + i
                            mm = pe.matmul(bank(("ck", kv, ht))[:, 0:G * NC], w[:, i * CHID + ht * P:i * CHID + ht * P + P],
                                           bkv[:, kv, lp, :], start=lp == 0, stop=lp == LP - 1)
                        if q == LP // 4 - 1:
                            mm.then_inc(filled, 1)
                        elif ht == 1:
                            mm.then_inc(raw_used, 1)
            begin(("kc",))
            for ht in range(2):
                wait_emptied(pe, ("ck", 0, ht))
                mm = pe.matmul(bank(("kc",))[:, 0:G * NC], vcol("w_ck2", ht * P, P), hid[:, 0, ht, :], start=ht == 0, stop=ht == 1)
            mm.then_inc(filled, 1)
            begin(("vc",))
            for g in range(G):
                for ht in range(2):
                    wait_emptied(pe, ("ck", 1, ht))
                    mm = pe.matmul(bank(("vc",))[0:NC, g * DH:g * DH + DH], hid[:, 1, ht, g * NC:g * NC + NC],
                                   vcol("w_cv2", ht * DH, DH), start=ht == 0, stop=ht == 1)
            mm.then_inc(filled, 1)
            sum_squares("cq")
            sum_squares("ckv")

            def nsa_scores(h, qt, br):
                rows = slice(64 * (h % 2), 64 * (h % 2) + 64)
                q = qT[rows, h // 2, qt * P:qt * P + P]
                if br == 0:
                    return q, kcT[rows, (h // HG) * NC:(h // HG) * NC + NC], NC
                return q, (ksd, kwd)[br - 1][rows, h // HG, 0:qt * P + P], qt * P + P

            def nsa_values(h, qt, br):
                g = h // HG
                if br == 0:
                    return [(vc[0:NC, g * DH:g * DH + DH], NC)]
                return [(vtok[:, br - 1, kt, g * DH:g * DH + DH], P) for kt in range(qt + 1)]

            for m in (0, 1, 2, 3, 6, 8):
                wait_emptied(pe, ("z", m))
            for n in (("vt", 0), ("vt", 1), ("kc",), ("vc",)):
                wait_emptied(pe, n)
            attention("nsa", NSA_UNITS, (sm, pt, nsa_scores, nsa_values))

            for h in range(MH):
                product(("uq", h), ("uq", h // 2), cqh, range(3), (h % 2) * 3 * P, event=("cq",) if h == 0 else None)
            for i in range(MH // 2):
                product(("uk", i), ("uk",), cqh, range(3, 5), i * 2 * P, event=("ckv",) if i == 0 else None)
            s = SPLIT_AT[("uv",)]
            pe.wait_ge(lo_done, s + 1)
            for t in range(TT):
                begin(("uv", t))
                for k in range(2):
                    mm = three(bank(("uv", t)), s % NHL, slice(k * S, k * S + S), cqh[:, :, :, t * P:t * P + P], 3 + k,
                               k == 0, k == 1, a_moving=False)
                mm.then_inc(filled, 1)

            def mla_scores(h, qt, br):
                return qcat[0:DQK, h, qt * P:qt * P + P], kcat[0:DQK, h, 0:qt * P + P], qt * P + P

            def mla_values(h, qt, br):
                return [(vm[:, kt, h * MV:h * MV + MV], P) for kt in range(qt + 1)]

            pe.wait_ge(rope_done, MH)
            pe.wait_ge(krot_done, 1)
            for i in range(MH // 2):
                wait_emptied(pe, ("uk", i))
            for t in range(TT):
                wait_emptied(pe, ("uv", t))
            attention("mla", MLA_UNITS, (sm2, pt2, mla_scores, mla_values))

            for m in range(16):
                product(("gate", m), ("gate", m), ah, range(KT))
            pe.wait_ge(o_empty, H // 2 + MH // 2)
            for m in range(KT):
                product(("on", m), ("nm", m), oh, range(4))
                product(("om", m), ("nm", m), oh, range(4, 8), col0=4 * P)
            for m in range(KT):
                product(("wo", m), ("wo", m), yh, range(KT), event=("y",) if m == 0 else None)
            sum_squares("mlp")

            def mlp(n, first):
                for half, c in mlp_order():
                    for m in range(KT):
                        if half == 1:
                            product(("fc1", n, c, m), ("fc1", n, c, m), ah, range(KT), event=first if (c, m) == (0, 0) else None)
                        else:
                            product(("fc2", n, c, m), ("fc2", n, c, m), hidden[c % 2], range(KT), event=("hid", n, c) if m == 0 else None)

            mlp(1, ("mlp",))
            sum_squares("final")

            sum_squares("mix2")
            for i in range(3):
                begin(("lh", i))
            wait_loaded(pe, ("lora", 0))
            wait_loaded(pe, ("lora", 1))
            for k in range(KT):
                for i, (blk, c0, n) in enumerate(((0, 0, LORA), (0, LORA, LORA), (1, 0, P))):
                    pe.wait_ge(xm_ready, 3 * k + i + 1)
                    mm = pe.matmul(bank(("lh", i))[0:n, :], raw_of(("lora", blk))[:, k * P + c0:k * P + c0 + n], xm(i, k),
                                   start=k == 0, stop=k == KT - 1)
                    mm.then_inc(xm_used if k < KT - 1 else filled, 1)
            for f in rwkv_order():
                kind, j = f[0], f[1]
                if kind in ("rkv", "glu"):
                    product(f, f, ah, range(KT))
                    continue
                if kind not in NO_BANK:
                    begin(f)
                    b = bank(f)
                if kind in ("lw2", "la2", "lg2"):
                    pe.wait_ge(lw_loaded[j % 2], 16 * (j // 2 + 1))
                    for i in range(3):
                        wait_emptied(pe, ("lh", i))
                    rows, cols, i = {"lw2": (slice(0, LORA), slice(0, P), 0), "la2": (slice(LORA, P), slice(0, P), 0),
                                     "lg2": (slice(0, P), slice(P, 2 * P), 1)}[kind]
                    mm = pe.matmul(b, lwt[rows, j % 2, cols], lh[rows, i, :], start=True, stop=True)
                elif kind == "kkss":
                    pe.wait_ge(kksq_ready, j + 1)
                    mm = pe.matmul(b, heads, sq[:, 0, :], start=True, stop=True)
                elif kind == "bonus":
                    pe.wait_ge(rk_ready, j + 1)
                    mm = pe.matmul(b, heads, tf, start=True, stop=True)
                elif kind == "tok":
                    i = f[2]
                    if i == 0:
                        pe.wait_ge(at_ready, j + 1)
                    elif i < 3:
                        pe.wait_ge(pool_f, POOL_F * j + 9 + i)
                    for t in range(TT):
                        cols = slice(t * P, t * P + P)
                        src = (arow[:, t, 0, :], sw[:, cols], cw[:, cols], rkv[:, 2, cols])[i]
                        mm = pe.transpose(b[:, cols], src, eye)
                elif kind in ("mb", "mk"):
                    hh, half = f[2], f[3]
                    rows = slice(RN * hh, RN * hh + RN)
                    src = bh if kind == "mb" else kh
                    for n in range(2):
                        t = 2 * half + n
                        mm = pe.matmul(b[:, n * 2 * P:n * 2 * P + 2 * P], src[rows, t * P:t * P + P],
                                       arow[rows, t, :, :].rearrange("p a n -> p (a n)"), start=True, stop=True)
                elif kind == "inv":
                    hh, lv = f[2], f[3]
                    if lv == 0:
                        pe.wait_ge(iy0_done, 2 * j + hh + 1)
                    else:
                        wait_emptied(pe, ("iy", j, hh, lv))
                    for t in range(TT):
                        mm = pe.transpose(b[:, t * P:t * P + P], iy[:, t, :], eye)
                elif kind == "akv":
                    hh = f[2]
                    wait_emptied(pe, ("mk", j, hh, 0))
                    wait_emptied(pe, ("mk", j, hh, 1))
                    wait_emptied(pe, ("tok", j, 3))
                    for t in range(TT):
                        mm = pe.matmul(b[:, t * RN:t * RN + RN], mk[:, t, 0:P], vtk[:, t, hh * RN:hh * RN + RN], start=True, stop=True)
                elif kind == "ip":
                    hh, lv = f[2], f[3]
                    wait_emptied(pe, ("inv", j, hh, lv - 1))
                    for t in range(TT):
                        mm = pe.matmul(b[:, t * P:t * P + P], mb[:, t, 0:P], ix[:, t, :], start=True, stop=True)
                elif kind == "iy":
                    hh, lv = f[2], f[3]
                    wait_emptied(pe, ("ip", j, hh, lv))
                    for t in range(TT):
                        mm = pe.matmul(b[:, t * P:t * P + P], ip[:, t, :], iy[:, t, :], start=True, stop=True)
                elif kind == "tav":
                    hh = f[2]
                    wait_emptied(pe, ("iy", j, hh, LEVELS))
                    wait_emptied(pe, ("akv", j, hh))
                    for t in range(TT):
                        mm = pe.matmul(b[:, t * P:t * P + P], iy[:, t, :], ftok[:, t, hh, :, :].rearrange("p a n -> p (a n)"),
                                       start=True, stop=True)
                elif kind == "rr":
                    hh = f[2]
                    wait_emptied(pe, ("tav", j, hh))
                    for t in range(TT):
                        mm = pe.matmul(b[RN * hh:RN * hh + RN, t * P:t * P + P], tav[:, t, 0, hh, :], mb[:, t, P:2 * P],
                                       start=True, stop=True)
                elif kind == "opart":
                    hh = f[2]
                    if j:
                        pe.wait_ge(og_ready, j)
                    else:
                        pe.wait_ge(o_empty, H // 2 + MH // 2)
                    for t in range(TT):
                        dst = psum[RN * hh:RN * hh + RN, OBANK, t * P:t * P + P]
                        pe.matmul(dst, tav[:, t, 1, hh, :], mb[:, t, P:2 * P], start=t == 0, stop=False, skip_group_check=True)
                        mm = pe.matmul(dst, vtk[:, t, hh * RN:hh * RN + RN], mk[:, t, P:2 * P], start=False, stop=False,
                                       skip_group_check=True)
                    mm.then_inc(opart_done, 1)
                elif kind in ("pt", "qq"):
                    rows = slice(CH * f[2], CH * f[2] + CH)
                    for t in range(TT):
                        dst = b[:, t * P:t * P + P]
                        if kind == "pt":
                            mm = pe.matmul(dst, tav[rows, t, 0, :, :].rearrange("p h n -> p (h n)"), btok[rows, t, :], start=True, stop=True)
                        else:
                            pe.matmul(dst, btok[rows, t, :], tav[rows, t, 1, :, :].rearrange("p h n -> p (h n)"), start=True, stop=False)
                            mm = pe.matmul(dst, ktok[rows, t, :], vtk[rows, t, :], start=False, stop=True)
                elif kind == "st":
                    c = f[2]
                    if c == 1:
                        for half in range(2):
                            wait_emptied(pe, ("pt", j, half))
                            wait_emptied(pe, ("qq", j, half))
                    else:
                        pe.wait_ge(st_ready, (NCK - 2) * j + c - 1)
                    mm = pe.matmul(b[:, 0:RN], pts[:, c, :], state(c), start=True, stop=True)
                elif kind == "ost":
                    pe.wait_ge(st_ready, (NCK - 2) * (j + 1))
                    wait_emptied(pe, ("rr", j, 0))
                    wait_emptied(pe, ("rr", j, 1))
                    for c in range(1, NCK):
                        for hh in range(2):
                            rows, cols = slice(RN * hh, RN * hh + RN), slice(c * CH, c * CH + CH)
                            mm = pe.matmul(psum[rows, OBANK, cols], state(c)[rows, :], rp[rows, cols], start=False, stop=True,
                                           skip_group_check=True)
                    mm.then_inc(ost_done, 1)
                elif kind == "gnm":
                    pe.wait_ge(og_ready, j + 1)
                    mm = pe.matmul(b, heads, og, start=True, stop=True)
                elif kind == "gnv":
                    pe.wait_ge(gnsq_ready, j + 1)
                    mm = pe.matmul(b, heads, sq[:, 1, :], start=True, stop=True)
                if kind not in NO_BANK:
                    mm.then_inc(filled, 1)
            begin(("convmean",))
            for k in range(KT):
                pe.wait_ge(conv_done, k + 1)
                mm = pe.matmul(bank(("convmean",)), ones, x[:, k, :], start=k == 0, stop=k == KT - 1)
            mm.then_inc(filled, 1)
            sum_squares("conv")
            for m in range(16):
                product(("gate2", m), ("gate2", m), ah, range(KT))
            pe.wait_ge(ao_ready, KT)
            for m in range(KT):
                product(("pr", m), ("pr", m), aoh, range(KT))
                product(("pc", m), ("pc", m), coh, range(KT), event=("conv",) if m == 0 else None)
            for m in range(KT):
                product(("wo2", m), ("wo2", m), ah, range(KT), event=("y2",) if m == 0 else None)
            sum_squares("ff2")
            mlp(2, ("ff2",))
            sum_squares("final2")

        @block.scalar
        def _(act):
            split = [0]

            def weights_ahead(n):
                while split[0] <= min(n, len(SPLITS) - 1):
                    s = split[0]
                    wait_loaded(act, SPLITS[s])
                    if s >= NHL:
                        act.wait_ge(filled, BLOCK_LAST[SPLITS[s - NHL]] + 1)
                    act.activation(whi[:, s % NHL, :], raw_of(SPLITS[s]), ACT.Copy).then_inc(hi_done, 1)
                    split[0] += 1

            def squares(name, src, wait):
                for k in range(dict(NORMS)[name]):
                    n = SQ_AT[name, k]
                    wait(k)
                    if n >= 2:
                        for nm, tiles in NORMS:
                            if n - 2 == SQ_AT[nm, tiles - 1]:
                                wait_filled(act, ("ss", nm))
                        used = sum(1 for e, (q, kk) in enumerate(SQ_AT) if e <= n - 2 and kk < dict(NORMS)[q] - 1)
                        act.wait_ge(sq_used, used)
                    act.activation(sq[:, n % 2, :], src[:, k, :], ACT.Square).then_inc(sq_ready, 1)

            def root(name):
                wait_emptied(act, ("ss", name))
                act.activation(rstd[:, :], rstd[:, :], ACT.Sqrt).then_inc(root_done, 1)

            def high(event, dst, bias=0.0):
                n = EVENT[event]
                act.wait_ge(pre_split, n + 1)
                act.activation(dst, tmp[:, n % NTMP, :], ACT.Identity, bias=bias).then_inc(hi_ready, 1)

            def empty(name, dst, src=None, **kw):
                wait_filled(act, name)
                emptied_by(act.activation(dst, bank(name) if src is None else src, kw.pop("func", ACT.Copy), **kw), name)

            act.wait_ge(x_loaded, 16)
            squares("mix", x, lambda k: None)
            root("mix")
            weights_ahead(NHL - 1)
            act.wait_ge(modg_ready, 1)
            for k in range(KT):
                high(("mix", k), ah[:, 0, k, :], bias=mod[:, k:k + 1])
            for m in range(16):
                weights_ahead(min(SPLIT_AT["z", m] + 1, SPLIT_AT["z", 15]))
                z = bank(("z", m))
                if m < 4:
                    empty(("z", m), qT[:, m, :], scale=-DH ** -0.5)
                elif m in (4, 5):
                    wait_filled(act, ("z", m))
                    for g in range(G):
                        rows = slice(64 * g, 64 * g + 64)
                        act.activation(kcd[0:64, m - 4, g, :], z[rows, :], ACT.Copy).then_inc(act_step, 1)
                        last = act.activation(kcd[64:128, m - 4, g, 0:S - 1], z[rows, 1:S], ACT.Copy)
                        if g < G - 1:
                            last.then_inc(act_step, 1)
                    emptied_by(last, ("z", m))
                elif m in (6, 8):
                    wait_filled(act, ("z", m))
                    dst = ksd if m == 6 else kwd
                    for g in range(G):
                        for half in range(2):
                            last = act.activation(dst[64 * half:64 * half + 64, g, :], z[64 * g:64 * g + 64, :], ACT.Copy)
                            if (g, half) != (G - 1, 1):
                                last.then_inc(act_step, 1)
                    emptied_by(last, ("z", m))
                elif m in (7, 9):
                    empty(("z", m), vT[:, (m - 7) // 2, :])
                elif m == 10:
                    wait_filled(act, ("z", m))
                    act.activation(gT[:, :], z[0:32, :], ACT.Sigmoid).then_inc(act_step, 1)
                    emptied_by(act.activation(zkr[64:128, :], z[64:128, :], ACT.Copy), ("z", m))
                else:
                    empty(("z", m), zd[:, m - 11, :])
            for i in range(2):
                empty(("vt", i), vtok[:, i, :, :].rearrange("p t n -> p (t n)"))
            empty(("gt",), gates[:, :, :].rearrange("p t n -> p (t n)"), bank(("gt",))[:, 0:TT * 32])
            for kv in range(2):
                for ht in range(2):
                    empty(("ck", kv, ht), hid[:, kv, ht, :], bank(("ck", kv, ht))[:, 0:G * NC], func=ACT.Silu)
            empty(("kc",), kcT[:, :], bank(("kc",))[:, 0:G * NC])
            empty(("vc",), vc[0:NC, :], bank(("vc",))[0:NC, 0:G * DH])
            for name, k0, n in (("cq", 0, 3), ("ckv", 3, 2)):
                squares(name, zd[:, k0:k0 + n, :], lambda k: wait_emptied(act, ("z", 11 + k0 + k)))
                root(name)
                for k in range(n):
                    high((name, k), cqh[:, 0, k0 + k, :])
            weights_ahead(SPLIT_AT["uq", 0] + 1)

            def attention(tag, units, probs, turned, st):
                base = {"nsa": 0, "mla": len(NSA_UNITS)}[tag]
                per_pair = 2 * TT * (3 if tag == "nsa" else 1)
                for kind, u in attention_order(units):
                    if kind == "S":
                        h, qt, br = units[u]
                        w = NC if br == 0 else qt * P + P
                        wait_emptied(act, ("S", tag, u))
                        act.activation(probs[:, u % 3, 0:w], probs[:, u % 3, 0:w], ACT.Exp, bias=st[:, u % 3, 0:1],
                                       scale=-1.0, accum_out=st[:, u % 3, 1:2]).then_inc(exp_done, 1)
                    elif kind == "PT":
                        h, qt, br = units[u]
                        if u >= 2:
                            act.wait_ge(o_done, base + u - 1)
                        if br == 0:
                            empty(("PT", tag, u), turned[0:NC, u % 2, 0:P], bank(("PT", tag, u))[0:NC, 0:P])
                        else:
                            empty(("PT", tag, u), turned[:, u % 2, 0:qt * P + P], bank(("PT", tag, u))[:, 0:qt * P + P])
                    elif (u + 1) % per_pair == 0:
                        act.wait_ge(o_done, base + u + 1)
                        pair = u // per_pair + (H // 2 if tag == "mla" else 0)
                        act.activation(oh[:, 0, pair, :], psum[:, OBANK, :], ACT.Copy).then_inc(o_hi, 1)

            attention("nsa", NSA_UNITS, sm, pt, stat)
            for h in range(MH):
                weights_ahead(SPLIT_AT["uq", h // 2] + 1)
                wait_filled(act, ("uq", h))
                act.activation(qcat[0:NOPE, h, :], bank(("uq", h))[0:NOPE, :], ACT.Copy, scale=-DQK ** -0.5).then_inc(nope_done, 1)
            for i in range(MH // 2):
                weights_ahead(SPLIT_AT["uk",] + 1)
                wait_filled(act, ("uk", i))
                for half in range(2):
                    last = act.activation(kcat[0:NOPE, 2 * i + half, :], bank(("uk", i))[64 * half:64 * half + 64, :], ACT.Copy)
                    if half == 0:
                        last.then_inc(act_step, 1)
                emptied_by(last, ("uk", i))
            for t in range(TT):
                empty(("uv", t), vm[:, t, :])
            weights_ahead(SPLIT_AT["gate", 0] + 1)
            attention("mla", MLA_UNITS, sm2, pt2, stat2)
            for m in range(16):
                weights_ahead(SPLIT_AT["gate", m] + 1)
                empty(("gate", m), sg[:, m, :], func=ACT.Sigmoid)
            for m in range(KT):
                weights_ahead(SPLIT_AT["nm", m] + 1)
                high(("y", m), yh[:, 0, m, :])
            for m in range(KT):
                weights_ahead(SPLIT_AT["wo", m] + 1)
                if m < KT - 1:
                    wait_filled(act, ("wo", m))
            squares("mlp", x, lambda k: wait_emptied(act, ("wo", k)))
            root("mlp")
            for k in range(KT):
                high(("mlp", k), ah[:, 0, k, :], bias=mod[:, 24 + k:25 + k])

            def mlp(n):
                for half, c in mlp_order():
                    for m in range(KT):
                        what = (f"fc{half}", n, c, m)
                        weights_ahead(SPLIT_AT[what] + 1)
                        if half == 1:
                            e = EVENT["hid", n, c, m]
                            act.wait_ge(pre_split, e - 1)
                            empty(what, sq[:, e % 2, :], func=ACT.Relu)
                            if c >= 2 and m == 0:
                                wait_filled(act, ("fc2", n, c - 2, KT - 1))
                            high(("hid", n, c, m), hidden[c % 2][:, 0, m, :])

            mlp(1)
            squares("final", x, lambda k: wait_emptied(act, ("fc2", 1, NCH - 1, k)))
            root("final")

            wait_filled(act, ("fc2", 1, NCH - 1, KT - 1))
            act.dma_start(rw[:, :], io["rw"]).then_inc(const_loaded["rw"], 16)
            act.wait_ge(xn_ready, KT)
            act.dma_start(x_kept, x[:, :, :].rearrange("p k s -> p (k s)")).then_inc(x_put, 16)
            for j in range(2):
                act.dma_start(lwt[:, j, :], io["lw"][j]).then_inc(lw_loaded[j], 16)
            squares("mix2", x, lambda k: None)
            root("mix2")
            weights_ahead(SPLIT_AT["rkv", 0, 1])
            for k in range(KT):
                high(("mix2", k), ah[:, 0, k, :])
            empty(("lh", 0), lh[0:LORA, 0, :], bank(("lh", 0))[0:LORA, :], func=ACT.Tanh)
            empty(("lh", 1), lh[LORA:P, 0, :], bank(("lh", 1))[0:LORA, :])
            empty(("lh", 2), lh[:, 1, :], func=ACT.Sigmoid)
            for f in rwkv_order():
                kind, j = f[0], f[1]
                if kind in ("rkv", "glu"):
                    weights_ahead(SPLIT_AT[f] + 1)
                if kind == "rkv":
                    if j:
                        act.wait_ge(mix_done, 3 * j)
                    else:
                        act.wait_ge(xm_ready, 3 * KT)
                    empty(f, rkvp[:, f[2], 1:S + 1])
                elif kind == "lw2":
                    if j:
                        wait_filled(act, ("tok", j - 1, 1))
                    empty(f, sw[:, :], func=ACT.Sigmoid, bias=vcol("decay_w0_2", j))
                elif kind == "la2":
                    if j:
                        act.wait_ge(pool_f, POOL_F * (j - 1) + 8)
                    empty(f, rate[:, :], func=ACT.Sigmoid, bias=vcol("aaa_a0_2", j))
                elif kind == "lg2":
                    if j >= 2:
                        act.wait_ge(ao_done, j - 1)
                    empty(f, gate[:, j % 2, :])
                    if j + 2 < KT:
                        act.dma_start(lwt[:, j % 2, :], io["lw"][j + 2]).then_inc(lw_loaded[j % 2], 16)
                elif kind == "glu" and f[2] == 1:
                    if j:
                        wait_emptied(act, ("glu", j - 1, 0))
                    else:
                        act.wait_ge(hl_ready, EVENT["mix2", KT - 1] + 1)
                    empty(f, usig, func=ACT.Sigmoid)
                elif kind == "kkss":
                    act.wait_ge(kk0_ready, j + 1)
                    if j == 0:
                        wait_filled(act, ("ss", "mix2"))
                    else:
                        wait_filled(act, ("kkss", j - 1))
                    act.activation(sq[:, 0, :], kk[:, :], ACT.Square).then_inc(kksq_ready, 1)
                    act.wait_ge(cw_ready, j + 1)
                    if j:
                        act.wait_ge(pool_f, POOL_F * j)
                        act.wait_ge(at_ready, j)
                    act.activation(ew[:, :], cw[:, :], ACT.Exp, scale=-DECAY).then_inc(exp_ready, 1)
                    act.activation(ewi[:, :], cw[:, :], ACT.Exp, scale=DECAY).then_inc(exp_ready, 1)
                    act.wait_ge(pool_f, POOL_F * j + 4)
                    act.activation(ewp[:, :], sw[:, :], ACT.Exp, scale=-DECAY).then_inc(exp_ready, 1)
                    if j == 0:
                        act.wait_ge(hl_ready, EVENT["mix2", KT - 1] + 1)
                    elif j >= 2:
                        act.wait_ge(ao_done, j - 1)
                    empty(f, nrm, func=ACT.Sqrt)
                elif kind == "tok":
                    if f[2] == 0:
                        empty(f, ftok[:, :, :, 0, :], bank(f).rearrange("p (t h n) -> p t h n", t=TT, h=2))
                    else:
                        empty(f, (btok, ktok, vtk)[f[2] - 1][:, :, :], bank(f).rearrange("p (t n) -> p t n", t=TT))
                elif kind == "inv":
                    empty(f, ix[:, :, :], bank(f).rearrange("p (t n) -> p t n", t=TT))
                elif kind == "akv":
                    empty(f, ftok[:, :, f[2], 1, :], bank(f)[:, 0:TT * RN].rearrange("p (t n) -> p t n", t=TT))
                elif kind == "tav":
                    empty(f, tav[:, :, :, f[2], :], bank(f).rearrange("p (t a n) -> p t a n", t=TT, a=2))
                elif kind == "qq":
                    wait_filled(act, f)
                    if j:
                        act.wait_ge(st_ready, (NCK - 2) * j)
                    own = bank(f).rearrange("p (c n) -> p c n", c=4)
                    cs = slice(f[2], NCK, 2)
                    act.activation(qs[0:RN, cs, :], own[0:RN, :, 0:RN], ACT.Copy).then_inc(act_step, 1)
                    emptied_by(act.activation(qs[RN:P, cs, :], own[RN:P, :, RN:P], ACT.Copy), f)
                elif kind == "ost":
                    act.wait_ge(ost_done, j + 1)
                    if j:
                        act.wait_ge(ao_done, j)
                    act.activation(og, psum[:, OBANK, :], ACT.Copy).then_inc(og_ready, 1)
                elif kind == "gnm":
                    wait_emptied(act, f)
                    act.activation(sq[:, 1, :], og, ACT.Square).then_inc(gnsq_ready, 1)
                elif kind == "gnv":
                    wait_emptied(act, f)
                    act.activation(rstd[:, :], rstd[:, :], ACT.Sqrt).then_inc(gnroot_done, 1)
            weights_ahead(SPLIT_AT["gate2", 0] + 1)
            act.wait_ge(ao_done, KT)
            wait_filled(act, ("gnv", KT - 1))
            for k in range(KT):
                act.activation(aoh[:, 0, k, :], ao[:, k, :], ACT.Copy).then_inc(ao_hi, 1)
            squares("conv", x, lambda k: act.wait_ge(cen_ready, k + 1))
            root("conv")
            act.wait_ge(ao_ready, KT)
            for k in range(KT):
                n = EVENT["conv", k]
                act.wait_ge(convn_ready, k + 1)
                act.wait_ge(hl_ready, n - NTMP + 1)
                act.activation(tmp[:, n % NTMP, :], x[:, k, :], ACT.Silu, bias=vcol("conv_ln_b_2", k)).then_inc(pre_split, 1)
                high(("conv", k), coh[:, 0, k, :])
            act.wait_ge(pre_split, EVENT["conv", KT - 1] + 1)
            act.wait_ge(x_put, 16)
            act.dma_start(x[:, :, :].rearrange("p k s -> p (k s)"), x_kept).then_inc(x_back, 16)
            for m in range(16):
                weights_ahead(SPLIT_AT["gate2", m] + 1)
                empty(("gate2", m), sg2[:, m, :], func=ACT.Sigmoid, bias=vcol("b_gate_2", m))
            for m in range(KT):
                weights_ahead(SPLIT_AT["pr", m] + 2)
                high(("y2", m), ah[:, 0, m, :])
            for m in range(KT):
                weights_ahead(SPLIT_AT["wo2", m] + 1)
                if m < KT - 1:
                    wait_filled(act, ("wo2", m))
            squares("ff2", x, lambda k: wait_emptied(act, ("wo2", k)))
            root("ff2")
            for k in range(KT):
                high(("ff2", k), ah[:, 0, k, :])
            mlp(2)
            squares("final2", x, lambda k: wait_emptied(act, ("fc2", 2, NCH - 1, k)))
            root("final2")

        @block.vector
        def _(dve):
            steps = [0]

            def step(ins):
                steps[0] += 1
                ins.then_inc(dve_step, 1)
                dve.wait_ge(dve_step, steps[0])

            def mean_square(name, n, eps=EPS):
                wait_filled(dve, ("ss", name))
                emptied_by(dve.tensor_scalar(rstd[:, :], bank(("ss", name)), 1.0 / n, eps, ALU.mult, ALU.add), ("ss", name))

            def inverse_root(name):
                dve.wait_ge(root_done, [n for n, _ in NORMS].index(name) + 1)
                step(dve.reciprocal(rstd[:, :], rstd[:, :]))

            def low(event, dst_hi, dst_lo, bias=0.0):
                n = EVENT[event]
                dve.wait_ge(hi_ready, n + 1)
                dve.scalar_tensor_tensor(dst_lo, tmp[:, n % NTMP, :], bias, dst_hi.bitcast(F32), ALU.add,
                                         ALU.subtract).then_inc(hl_ready, 1)

            def slot(event):
                n = EVENT[event]
                if n >= NTMP:
                    dve.wait_ge(hl_ready, n - NTMP + 1)
                return tmp[:, n % NTMP, :]

            def normed(name, n, src, gain, dst, k0, tiles, bias=None):
                mean_square(name, n)
                inverse_root(name)
                for k in range(tiles + 1):
                    if k < tiles:
                        dve.scalar_tensor_tensor(slot((name, k)), src[:, k, :], gain(k), rstd[:, :], ALU.mult,
                                                 ALU.mult).then_inc(pre_split, 1)
                    if k:
                        low((name, k - 1), dst[:, 0, k0 + k - 1, :], dst[:, 1, k0 + k - 1, :], bias(k - 1) if bias else 0.0)

            def ada(n):
                wait_filled(dve, ("ada", n))
                emptied_by(dve.tensor_tensor(mod[:, n:n + 1], bank(("ada", n))[:, 0:1], vcol("b_ada", n), ALU.add), ("ada", n))

            dve.wait_ge(vec_loaded, 16)
            for n in range(16):
                ada(n)
            for n in range(KT, 2 * KT):
                wait_emptied(dve, ("ada", n))
            dve.scalar_tensor_tensor(modg[:, 0:KT], mod[:, KT:2 * KT], 1.0, vcol("g_mix", 0, KT), ALU.add,
                                     ALU.mult).then_inc(modg_ready, 1)
            dve.wait_ge(modg_ready, 1)
            normed("mix", D, x, lambda k: modg[:, k:k + 1], ah, 0, KT, lambda k: mod[:, k:k + 1])
            for m in range(16):
                ada(16 + 2 * m)
                ada(17 + 2 * m)
            wait_emptied(dve, ("ada", 39))
            dve.scalar_tensor_tensor(modg[:, KT:2 * KT], mod[:, 32:40], 1.0, vcol("g_mlp", 0, KT), ALU.add,
                                     ALU.mult).then_inc(modg_ready, 1)
            for kv, pe_name in enumerate(("pe_ck", "pe_cv")):
                wait_emptied(dve, ("z", 4 + kv))
                for g in range(G):
                    for hi in range(2):
                        src = kcd[:, kv, g, hi * CS:hi * CS + NC * CS].rearrange("p (c r) -> p r c", r=CS)[:, ::2, :]
                        pe8 = vcol(pe_name, 8 * hi, 8).unsqueeze(2).to_broadcast([P, 8, NC])
                        last = dve.tensor_tensor(bkv[:, kv, 8 * hi:8 * hi + 8, g * NC:g * NC + NC], src, pe8, ALU.add)
                        if (g, hi) != (G - 1, 1):
                            last.then_inc(dve_step, 1)
                            steps[0] += 1
                last.then_inc(bkv_ready, 1)
            normed("cq", QR, zd, lambda k: vcol("g_cq", k), cqh, 0, 3)
            normed("ckv", KVR, zd[:, 3:5, :], lambda k: vcol("g_ckv", k), cqh, 3, 2)

            def attention(tag, units, probs, st, bias, gate):
                base = {"nsa": 0, "mla": len(NSA_UNITS)}[tag]
                per_pair = 2 * TT * (3 if tag == "nsa" else 1)

                def normalize(u):
                    h, qt, br = units[u]
                    w = NC if br == 0 else qt * P + P
                    dve.wait_ge(exp_done, base + u + 1)
                    total, inv = st[:, u % 3, 1:2], st[:, u % 3, 2:3]
                    if br == 0:
                        step(dve.tensor_scalar(total, total, 1e-30, None, ALU.max))
                    step(dve.reciprocal(inv, total))
                    pr = probs[:, u % 3, 0:w]
                    if gate is None:
                        ins = dve.tensor_scalar(pr, pr, inv, None, ALU.mult)
                    else:
                        ins = dve.tensor_scalar(pr, pr, inv, gate(h, qt, br), ALU.mult, ALU.mult)
                    ins.then_inc(p_ready, 1)

                for kind, u in attention_order(units):
                    h, qt, br = units[u]
                    if kind == "S":
                        w = NC if br == 0 else qt * P + P
                        wait_filled(dve, ("S", tag, u))
                        if u >= 3:
                            wait_filled(dve, ("PT", tag, u - 3))
                        emptied_by(dve.tensor_tensor_reduce(probs[:, u % 3, 0:w], bank(("S", tag, u))[:, 0:w], bias(h, qt, br),
                                                            1.0, 1e25, ALU.add, ALU.min, st[:, u % 3, 0:1]), ("S", tag, u))
                        if u >= 1:
                            normalize(u - 1)
                        if u == len(units) - 1:
                            normalize(u)
                    elif kind == "O" and (u + 1) % per_pair == 0:
                        pair = u // per_pair + (H // 2 if tag == "mla" else 0)
                        dve.wait_ge(o_hi, pair + 1)
                        dve.tensor_tensor(oh[:, 1, pair, :], psum[:, OBANK, :], oh[:, 0, pair, :].bitcast(F32),
                                          ALU.subtract).then_inc(o_empty, 1)

            def nsa_bias(h, qt, br):
                return cmpb[:, qt, h, :] if br == 0 else alibi[:, h, S - P - qt * P:S]

            for n in ("alibi", "cmpb", "causal", "rope"):
                dve.wait_ge(const_loaded[n], 16)
            wait_emptied(dve, ("gt",))
            attention("nsa", NSA_UNITS, sm, stat, nsa_bias, lambda h, qt, br: gates[:, qt, br * H + h:br * H + h + 1])
            wait_emptied(dve, ("z", 10))
            step(dve.tensor_tensor(kcat[64:96, 0, :], zkr[64:96, :], rope[64:96, :], ALU.mult))
            step(dve.tensor_tensor(rtmp[64:96, :], zkr[96:128, :], rope[96:128, :], ALU.mult))
            step(dve.tensor_tensor(kcat[64:96, 0, :], kcat[64:96, 0, :], rtmp[64:96, :], ALU.add))
            dve.tensor_copy(kcat[64:96, 1:MH, :], kcat[64:96, 0:1, :].to_broadcast([32, MH - 1, S])).then_inc(krot_done, 1)
            for h in range(MH):
                wait_filled(dve, ("uq", h))
                q = bank(("uq", h))
                if h:
                    dve.wait_ge(rope_done, h)
                step(dve.scalar_tensor_tensor(qcat[64:96, h, :], q[64:96, :], -DQK ** -0.5, rope[64:96, :], ALU.mult, ALU.mult))
                dve.wait_ge(nope_done, h + 1)
                emptied_by(dve.scalar_tensor_tensor(rtmp[64:96, :], q[96:128, :], -DQK ** -0.5, rope[96:128, :], ALU.mult,
                                                    ALU.mult), ("uq", h))
                wait_emptied(dve, ("uq", h))
                dve.tensor_tensor(qcat[64:96, h, :], qcat[64:96, h, :], rtmp[64:96, :], ALU.add).then_inc(rope_done, 1)
            attention("mla", MLA_UNITS, sm2, stat2, lambda h, qt, br: causal[:, S - P - qt * P:S], None)
            for m in range(KT + 1):
                if m < KT:
                    wait_emptied(dve, ("gate", 8 + m))
                    wait_filled(dve, ("on", m))
                    emptied_by(dve.tensor_tensor(sg[:, m, :], bank(("on", m)), sg[:, m, :], ALU.mult), ("on", m))
                    wait_filled(dve, ("om", m))
                    emptied_by(dve.tensor_tensor(sg[:, 8 + m, :], bank(("om", m)), sg[:, 8 + m, :], ALU.mult), ("om", m))
                    wait_emptied(dve, ("on", m))
                    wait_emptied(dve, ("om", m))
                    dve.tensor_tensor(slot(("y", m)), sg[:, m, :], sg[:, 8 + m, :], ALU.add).then_inc(pre_split, 1)
                if m:
                    low(("y", m - 1), yh[:, 0, m - 1, :], yh[:, 1, m - 1, :])
            for m in range(KT):
                wait_filled(dve, ("wo", m))
                emptied_by(dve.scalar_tensor_tensor(x[:, m, :], bank(("wo", m)), mod[:, 16 + m:17 + m], x[:, m, :], ALU.mult,
                                                    ALU.add), ("wo", m))
            dve.wait_ge(modg_ready, 2)
            normed("mlp", D, x, lambda k: modg[:, KT + k:KT + k + 1], ah, 0, KT, lambda k: mod[:, 24 + k:25 + k])

            def mlp(n, gate):
                for half, c in mlp_order():
                    for m in range(KT):
                        if half == 1:
                            what = ("fc1", n, c, m)
                            wait_emptied(dve, what)
                            e = EVENT["hid", n, c, m]
                            dve.tensor_tensor(slot(("hid", n, c, m)), sq[:, e % 2, :], sq[:, e % 2, :], ALU.mult).then_inc(pre_split, 1)
                            low(("hid", n, c, m), hidden[c % 2][:, 0, m, :], hidden[c % 2][:, 1, m, :])
                        else:
                            what = ("fc2", n, c, m)
                            wait_filled(dve, what)
                            if c:
                                wait_emptied(dve, ("fc2", n, c - 1, m))
                            if gate is None:
                                emptied_by(dve.tensor_tensor(x[:, m, :], bank(what), x[:, m, :], ALU.add), what)
                            else:
                                emptied_by(dve.scalar_tensor_tensor(x[:, m, :], bank(what), gate(m), x[:, m, :], ALU.mult,
                                                                    ALU.add), what)

            mlp(1, lambda m: mod[:, 40 + m:41 + m])
            def normed_in_place(name, gain):
                mean_square(name, D)
                inverse_root(name)
                for k in range(KT):
                    dve.scalar_tensor_tensor(x[:, k, :], x[:, k, :], vcol(gain, k), rstd[:, :], ALU.mult, ALU.mult).then_inc(xn_ready, 1)

            normed_in_place("final", "g_final")

            normed("mix2", D, x, lambda k: vcol("norm_mix_g_2", k), ah, 0, KT)
            for k in range(KT):
                dve.wait_ge(hp_ready, 2 * k + 2)
                if k >= 2:
                    dve.wait_ge(xm_used, 3 * (k - 1))
                for i in range(3):
                    dve.scalar_tensor_tensor(xm(i, k), rkv[:, k % 2, :], vcol("mu_lora_2", 8 * i + k), rkvp[:, k % 2, 1:S + 1],
                                             ALU.mult, ALU.add).then_inc(xm_ready, 1)
            dve.wait_ge(const_loaded["rw"], 16)
            dve.wait_ge(x_put, 16)
            taps = [0, CONV]

            def convolve(n):
                j, done = taps
                for w in range(done, min(done + n, CONV)):
                    src, tap, acc = upad[:, w:w + S], vcol("conv_w_2", 8 * w + j), x[:, j, :]
                    if w == 0:
                        ins = dve.tensor_scalar(acc, src, tap, vcol("conv_b_2", j), ALU.mult, ALU.add)
                    else:
                        ins = dve.scalar_tensor_tensor(acc, src, tap, acc, ALU.mult, ALU.add)
                    if w < CONV - 1:
                        step(ins)
                    else:
                        ins.then_inc(conv_done, 1)
                    taps[1] += 1

            for f in rwkv_order():
                kind, j = f[0], f[1]
                if kind == "rkv":
                    i = f[2]
                    n = (1, 0, 2).index(i)
                    dve.wait_ge(pool_f, POOL_F * j + n + 1)
                    dve.scalar_tensor_tensor(rkv[:, i, :], rkv[:, i, :], vcol("mu_rkv_2", 8 * i + j), rkvp[:, i, 1:S + 1],
                                             ALU.mult, ALU.add).then_inc(mix_done, 1)
                elif kind == "lw2":
                    wait_emptied(dve, f)
                    if j:
                        wait_filled(dve, ("tok", j - 1, 2))
                    for c in range(NCK):
                        cols = slice(c * CH, c * CH + CH)
                        last = dve.tensor_tensor_scan(cw[:, cols], ones[:, 0:CH], sw[:, cols], 0.0, ALU.mult, ALU.add)
                        if c < NCK - 1:
                            steps[0] += 1
                            last.then_inc(dve_step, 1)
                    last.then_inc(cw_ready, 1)
                elif kind == "la2":
                    wait_emptied(dve, f)
                    dve.wait_ge(mix_done, 3 * j + 3)
                    if j:
                        dve.wait_ge(pool_f, POOL_F * (j - 1) + 7)
                        wait_filled(dve, ("bonus", j - 1))
                    dve.tensor_scalar(kk[:, :], rkv[:, 1, :], vcol("k_k_2", j), None, ALU.mult).then_inc(kk0_ready, 1)
                    step(dve.tensor_scalar(tf, rate[:, :], -1.0, vcol("k_a_2", j), ALU.add, ALU.mult))
                    dve.wait_ge(kk0_ready, j + 1)
                    dve.scalar_tensor_tensor(rkv[:, 1, :], tf, 1.0, rkv[:, 1, :], ALU.add, ALU.mult).then_inc(kmod_ready, 1)
                    dve.wait_ge(kmod_ready, j + 1)
                    dve.scalar_tensor_tensor(tf, rkv[:, 0, :], vcol("r_k_2", j), rkv[:, 1, :], ALU.mult, ALU.mult).then_inc(rk_ready, 1)
                elif kind == "kkss":
                    wait_emptied(dve, f)
                    step(dve.tensor_scalar(nrm, nrm, 1e-12, None, ALU.max))
                    dve.reciprocal(nrm, nrm).then_inc(nrm_ready, 1)
                    dve.wait_ge(exp_ready, 3 * j + 3)
                    step(dve.tensor_copy(wc[:, j % 2, :], ew[:, :].rearrange("p (c n) -> p c n", c=NCK)[:, :, CH - 1]))
                    dve.wait_ge(pool_f, POOL_F * j + 5)
                    if j:
                        wait_filled(dve, ("mk", j - 1, 1, 1))
                    dve.scalar_tensor_tensor(arow[:, :, 0, :], kk[:, :].rearrange("p (t n) -> p t n", t=TT), -1.0,
                                             ewp[:, :].rearrange("p (t n) -> p t n", t=TT), ALU.mult, ALU.mult).then_inc(at_ready, 1)
                elif kind == "bonus":
                    wait_filled(dve, f)
                    emptied_by(dve.tensor_tensor(bv[:, j % 2, :], bank(f), rkv[:, 2, :], ALU.mult), f)
                elif kind == "glu" and f[2] == 0:
                    convolve(CONV)
                    taps[:] = [j, 0]
                    wait_emptied(dve, ("glu", j, 1))
                    wait_filled(dve, f)
                    if j == 0:
                        dve.wait_ge(zeros_done, 2)
                    emptied_by(dve.tensor_tensor(upad[:, CONV - 1:], bank(f), usig, ALU.mult), f)
                    wait_emptied(dve, f)
                elif kind in ("mb", "mk"):
                    wait_filled(dve, f)
                    if (j, f[2]) != (0, 0):
                        dve.wait_ge(opart_done, 2 * j + f[2])
                    dst = (mb if kind == "mb" else mk)[:, 2 * f[3]:2 * f[3] + 2, :]
                    emptied_by(dve.tensor_tensor(dst, bank(f).rearrange("p (t n) -> p t n", t=2),
                                                 strict_incl.unsqueeze(1).to_broadcast([P, 2, 2 * P]), ALU.mult), f)
                elif kind == "ip":
                    wait_filled(dve, f)
                    emptied_by(dve.tensor_tensor(ip[:, :, :], bank(f).rearrange("p (t n) -> p t n", t=TT),
                                                 level[f[3]].unsqueeze(1).to_broadcast([P, TT, P]), ALU.mult), f)
                    convolve(2)
                elif kind == "iy":
                    wait_filled(dve, f)
                    if f[3] == 1:
                        dve.wait_ge(iy0_done, 2 * j + f[2] + 1)
                    else:
                        wait_emptied(dve, ("iy", j, f[2], f[3] - 1))
                    emptied_by(dve.tensor_tensor(iy[:, :, :], bank(f).rearrange("p (t n) -> p t n", t=TT), iy[:, :, :], ALU.add), f)
                    convolve(2)
                elif kind == "rr":
                    hh = f[2]
                    rows = slice(RN * hh, RN * hh + RN)
                    wait_filled(dve, f)
                    dve.wait_ge(pool_f, POOL_F * j + 6)
                    if j:
                        dve.wait_ge(ost_done, j)
                    emptied_by(dve.tensor_tensor(rp[rows, :].rearrange("p (t n) -> p t n", t=TT),
                                                 bank(f)[rows, :].rearrange("p (t n) -> p t n", t=TT), arow[rows, :, 1, :], ALU.add), f)
                elif kind == "pt":
                    wait_filled(dve, f)
                    emptied_by(dve.tensor_tensor(pts[:, f[2]::2, :], bank(f).rearrange("p (c n) -> p c n", c=4),
                                                 heads.unsqueeze(1).to_broadcast([P, 4, P]), ALU.mult), f)
                elif kind == "st":
                    c = f[2]
                    wait_filled(dve, f)
                    if c == 1:
                        wait_emptied(dve, ("qq", j, 0))
                        wait_emptied(dve, ("qq", j, 1))
                        if j:
                            dve.wait_ge(ost_done, j)
                    emptied_by(dve.scalar_tensor_tensor(st[:, c + 1, :], state(c), wc[:, j % 2, c:c + 1], bank(f)[:, 0:RN],
                                                        ALU.mult, ALU.add), f)
                    wait_emptied(dve, f)
                    dve.tensor_tensor(st[:, c + 1, :], st[:, c + 1, :], qs[:, c, :], ALU.add).then_inc(st_ready, 1)
                    dve.wait_ge(st_ready, (NCK - 2) * j + c)
                elif kind == "gnm":
                    wait_filled(dve, f)
                    emptied_by(dve.scalar_tensor_tensor(og, bank(f), -1.0 / RN, og, ALU.mult, ALU.add), f)
                elif kind == "gnv":
                    wait_filled(dve, f)
                    if j + 1 < KT:
                        dve.wait_ge(pool_f, POOL_F * (j + 1) + 5)
                    emptied_by(dve.tensor_scalar(rstd[:, :], bank(f), 1.0 / RN, GN_EPS, ALU.mult, ALU.add), f)
                    dve.wait_ge(gnroot_done, j + 1)
                    step(dve.reciprocal(rstd[:, :], rstd[:, :]))
                    step(dve.scalar_tensor_tensor(og, og, vcol("ln_x_g_2", j), rstd[:, :], ALU.mult, ALU.mult))
                    step(dve.scalar_tensor_tensor(og, og, vcol("ln_x_b_2", j), bv[:, j % 2, :], ALU.add, ALU.add))
                    dve.tensor_tensor(ao[:, j, :], og, gate[:, j % 2, :], ALU.mult).then_inc(ao_done, 1)
            convolve(CONV)
            for k in range(KT):
                dve.wait_ge(ao_hi, k + 1)
                dve.tensor_tensor(aoh[:, 1, k, :], ao[:, k, :], aoh[:, 0, k, :].bitcast(F32), ALU.subtract).then_inc(ao_ready, 1)
            wait_filled(dve, ("convmean",))
            for k in range(KT):
                if k == KT - 1:
                    dve.wait_ge(conv_done, KT)
                ins = dve.scalar_tensor_tensor(x[:, k, :], bank(("convmean",)), -1.0 / D, x[:, k, :], ALU.mult, ALU.add)
                ins.then_inc(cen_ready, 1)
            dve.wait_ge(cen_ready, KT)
            emptied_by(dve.tensor_copy(wc[:, 0, 0:1], bank(("convmean",))[:, 0:1]), ("convmean",))
            mean_square("conv", D, LN_EPS)
            inverse_root("conv")
            for k in range(KT + 1):
                if k < KT:
                    dve.scalar_tensor_tensor(x[:, k, :], x[:, k, :], vcol("conv_ln_g_2", k), rstd[:, :], ALU.mult,
                                             ALU.mult).then_inc(convn_ready, 1)
                if k:
                    low(("conv", k - 1), coh[:, 0, k - 1, :], coh[:, 1, k - 1, :])
            for m in range(KT + 1):
                if m < KT:
                    wait_emptied(dve, ("gate2", 8 + m))
                    wait_filled(dve, ("pr", m))
                    emptied_by(dve.tensor_tensor(sg2[:, m, :], bank(("pr", m)), sg2[:, m, :], ALU.mult), ("pr", m))
                    wait_filled(dve, ("pc", m))
                    emptied_by(dve.tensor_tensor(sg2[:, 8 + m, :], bank(("pc", m)), sg2[:, 8 + m, :], ALU.mult), ("pc", m))
                    wait_emptied(dve, ("pr", m))
                    wait_emptied(dve, ("pc", m))
                    dve.tensor_tensor(slot(("y2", m)), sg2[:, m, :], sg2[:, 8 + m, :], ALU.add).then_inc(pre_split, 1)
                if m:
                    low(("y2", m - 1), ah[:, 0, m - 1, :], ah[:, 1, m - 1, :])
            dve.wait_ge(x_back, 16)
            for m in range(KT):
                wait_filled(dve, ("wo2", m))
                emptied_by(dve.tensor_tensor(x[:, m, :], bank(("wo2", m)), x[:, m, :], ALU.add), ("wo2", m))
            normed("ff2", D, x, lambda k: vcol("norm_ff_g_2", k), ah, 0, KT)
            mlp(2, None)
            normed_in_place("final2", "norm_final_g_2")


def tiles_of(w):
    k, n = w.shape
    return w.reshape(k // P, P, n).transpose(1, 0, 2).reshape(P, -1)


def columns_of(v):
    return v.reshape(-1, P).T


def padded(a, n=D):
    return a if a.shape[1] == n else np.concatenate([a, np.zeros((P, n - a.shape[1]), a.dtype)], 1)


def block_of(what, w):
    kind = what[0]
    w_in = w["w_in"]
    if kind == "ada":
        return tiles_of(w["w_ada"][:, what[1] * P:what[1] * P + P])
    if kind == "z":
        m = what[1]
        if m < 10:
            return tiles_of(w_in[:, m * P:m * P + P])
        if m == 10:
            zero = np.zeros((D, 40), w_in.dtype)
            return tiles_of(np.concatenate([w_in[:, 1280:1304], zero, w_in[:, 1944:1976], w_in[:, 1960:1976],
                                            w_in[:, 1944:1960]], 1))
        return tiles_of(w_in[:, 1304 + (m - 11) * P:1304 + (m - 10) * P])
    if kind == "ck":
        src = w["w_ck1"] if what[1] == 0 else w["w_cv1"]
        return tiles_of(src[what[2] * S:what[2] * S + S])
    if kind == "uq":
        parts = []
        for h in (2 * what[1], 2 * what[1] + 1):
            q = w["w_uq"][:, h * DQK:h * DQK + DQK]
            parts.append(tiles_of(np.concatenate([q, q[:, NOPE + 16:], q[:, NOPE:NOPE + 16]], 1)))
        return padded(np.concatenate(parts, 1))
    if kind == "uk":
        return np.concatenate([tiles_of(w["w_uk"][:, i * P:i * P + P]) for i in range(MH // 2)], 1)
    if kind == "uv":
        return tiles_of(w["w_uv"])
    if kind == "gate":
        return tiles_of(w_in[:, 1976 + what[1] * P:1976 + what[1] * P + P])
    if kind == "nm":
        cols = slice(what[1] * P, what[1] * P + P)
        return np.concatenate([tiles_of(w["w_o_nsa"][:, cols]), tiles_of(w["w_o_mla"][:, cols])], 1)
    if kind == "wo":
        return tiles_of(w["w_out"][:, what[1] * P:what[1] * P + P])
    w2 = w["w_in_2"]
    if kind == "lora":
        return tiles_of(np.concatenate([w["decay_w1_2"], w["aaa_a1_2"]], 1) if what[1] == 0 else w["gate_g1_2"])
    if kind in ("rkv", "glu"):
        c0 = (0 if kind == "rkv" else 3 * D) + what[2] * D + what[1] * P
        return tiles_of(w2[:, c0:c0 + P])
    if kind == "gate2":
        return tiles_of(w2[:, 5 * D + what[1] * P:5 * D + what[1] * P + P])
    if kind in ("pr", "pc", "wo2"):
        src = w[{"pr": "w_rwkv_proj_2", "pc": "w_conv_proj_2", "wo2": "w_out_2"}[kind]]
        return tiles_of(src[:, what[1] * P:what[1] * P + P])
    _, n, c, m = what
    up, down = (w["w_fc1"], w["w_fc2"]) if n == 1 else (w["w_ff1_2"], w["w_ff2_2"])
    if kind == "fc1":
        return tiles_of(up[:, (c * KT + m) * P:(c * KT + m + 1) * P])
    return tiles_of(down[c * D:c * D + D, m * P:m * P + P])


def kernel(**inputs):
    import concourse.bacc as bacc
    from concourse.bass_utils import run_bass_kernel_spmd

    w = {n: np.asarray(a) for n, a in inputs.items()}
    w = {n: a[0] if a.ndim > 1 and a.shape[0] == 1 else a for n, a in w.items()}
    vecs = []
    for name in VEC:
        if name in ("pe_ck", "pe_cv"):
            vecs.append(w[name].reshape(LP, P).T)
        elif name == "w_ck2":
            vecs.append(tiles_of(np.concatenate([w[name], w[name]], 1)))
        elif name == "w_cv2":
            vecs.append(tiles_of(w[name]))
        elif name in ("mu_lora_2", "conv_w_2", "r_k_2"):
            vecs.append(columns_of(w[name].reshape(-1)))
        else:
            vecs.append(columns_of(w[name]))
    arrays = {
        "x": np.ascontiguousarray(tiles_of(w["x"].T)),
        "vec": np.ascontiguousarray(np.concatenate(vecs, 1)),
        "w": np.stack([block_of(what, w) for _, what in BLOCKS]),
    }
    both = np.concatenate([w["decay_w2_2"], w["aaa_a2_2"]], 0)
    arrays["lw"] = np.stack([np.concatenate([both[:, j * P:j * P + P], w["gate_g2_2"][:, j * P:j * P + P]], 1) for j in range(KT)])
    arrays.update({n: np.ascontiguousarray(a) for n, a in block1_constants().items()})
    arrays["rw"] = rwkv_constants()
    nc = bacc.Bacc("TRN2", target_bir_lowering=False, num_devices=1)
    io = {n: nc.dram_tensor(f"in_{n}", a.shape, F32, kind="ExternalInput").ap() for n, a in arrays.items()}
    io["out"] = nc.dram_tensor("out", (P, KT * S), F32, kind="ExternalOutput").ap()
    build_program(nc, io)
    r = run_bass_kernel_spmd(nc, [{f"in_{n}": a for n, a in arrays.items()}], core_ids=[0])
    got = np.asarray(r.results[0]["out"])
    return np.ascontiguousarray(got.reshape(P, KT, S).transpose(2, 1, 0).reshape(1, S, D))
```

```python
from contextlib import ExitStack

import numpy as np
import concourse.bass as bass
from concourse import mybir

F32 = mybir.dt.float32
F32R = mybir.dt.float32r
ACT = mybir.ActivationFunctionType
ALU = mybir.AluOpType

P = 128
S = 512
D = 1024
KT = D // P
TT = S // P
DFF = 4 * D
NCH = DFF // D
H, G, DH = 8, 2, 64
HG = H // G
CL, CS, CHID = 32, 16, 256
NC = S // CS - CL // CS + 1
LP = CL * DH // P
MH, NOPE, ROPE, MV = 8, 64, 32, 64
DQK = NOPE + ROPE
QR, KVR = 384, 256
EPS = 1e-6
BIG = 1e30
RH, RN = 16, 64
CH = 64
NCK = S // CH
LEVELS = 5
CONV = 31
LORA = 64
LN_EPS, GN_EPS = 1e-5, 64e-5
DECAY = float(np.exp(np.float32(-0.5)))

NBANK = 7
OBANK = 7
NRAW, NHL = 4, 2


def vec_columns():
    names = [("c", 8), ("b_ada", 48), ("g_mix", 8), ("g_cq", 3), ("g_ckv", 2), ("g_mlp", 8), ("g_final", 8),
             ("pe_ck", LP), ("pe_cv", LP), ("w_ck2", 256), ("w_cv2", 128), ("norm_mix_g_2", 8), ("b_gate_2", 16), ("mu_rkv_2", 24),
             ("mu_lora_2", 24), ("decay_w0_2", 8), ("aaa_a0_2", 8), ("k_k_2", 8), ("k_a_2", 8), ("r_k_2", 8), ("ln_x_g_2", 8),
             ("ln_x_b_2", 8), ("conv_w_2", CONV * 8), ("conv_b_2", 8), ("conv_ln_g_2", 8), ("conv_ln_b_2", 8),
             ("norm_ff_g_2", 8), ("norm_final_g_2", 8)]
    at, n = {}, 0
    for name, w in names:
        at[name] = n
        n += w
    return at, n


VEC, NVEC = vec_columns()


def weight_blocks():
    out = [("raw", ("ada", n)) for n in range(16)]
    for m in range(16):
        out.append(("split", ("z", m)))
        out += [("raw", ("ada", 16 + 2 * m)), ("raw", ("ada", 17 + 2 * m))]
    out += [("raw", ("ck", kv, q)) for kv in range(2) for q in range(LP // 4)]
    out += [("split", ("uq", i)) for i in range(MH // 2)] + [("split", ("uk",)), ("split", ("uv",))]
    out += [("split", ("gate", m)) for m in range(16)]
    out += [("split", ("nm", m)) for m in range(KT)]
    out += [("split", ("wo", m)) for m in range(KT)]
    out += mlp_blocks(1)
    out += [("raw", ("lora", 0)), ("raw", ("lora", 1))]
    out += [("split", f[1]) for f in rwkv_order() if f[0] == "part" and f[2] == 0]
    out += [("split", (n, m)) for m in range(KT) for n in ("pr", "pc")]
    out += [("split", ("wo2", m)) for m in range(KT)]
    return out + mlp_blocks(2)


def mlp_order():
    order = [(1, 0)]
    for c in range(1, NCH):
        order += [(1, c), (2, c - 1)]
    return order + [(2, NCH - 1)]


def mlp_blocks(n):
    return [("split", (f"fc{half}", n, c, m)) for half, c in mlp_order() for m in range(KT)]


def parts(what, n):
    return [("part", what, KT * i // n, KT * (i + 1) // n) for i in range(n)]


def tile_ahead(j):
    k, r, v, g = (parts(what, 4) for what in (("rkv", j, 1), ("rkv", j, 0), ("rkv", j, 2), ("glu", j, 1)))
    return (k + [("lw2", j)] + r[:2] + [("mix", j, 1), ("scan", j)] + r[2:] + [("la2", j)] + v[:2] + [("mix", j, 0), ("kk", j)]
            + v[2:] + [("lg2", j)] + g[:1] + [("kkss", j), ("mix", j, 2)] + g[1:2] + [("nrm", j)] + g[2:3] + [("bonus", j)]
            + g[3:] + [("at", j)])


def rwkv_order():
    out = tile_ahead(0) + parts(("glu", 0, 0), 1) + [("re", 0)]
    for j in range(KT):
        ahead = tile_ahead(j + 1) if j + 1 < KT else []
        last = parts(("glu", j + 1, 0), KT) if j + 1 < KT else []

        def slot(taps):
            got = [ahead.pop(0)] if ahead else []
            while ahead and ahead[0][0] != "part":
                got.append(ahead.pop(0))
            return got + [("conv", j, taps)]

        out += [("tok", j, 0), ("mb", j, 0, 0), ("mb", j, 0, 1), ("tok", j, 1), ("mb", j, 1, 0), ("mb", j, 1, 1), ("iy0", j, 0), ("iy0", j, 1)]
        if j:
            out.append(("gnm", j - 1))
        out += [("tok", j, 2), ("tok", j, 3), ("mk", j, 0, 0), ("mk", j, 0, 1), ("mk", j, 1, 0), ("mk", j, 1, 1), ("inv", j, 0, 0)]
        if j:
            out.append(("gnv", j - 1))
        out += [("akv", j, 0), ("akv", j, 1), ("inv", j, 1, 0), ("opv", j, 0), ("opv", j, 1)]
        for lv in range(1, LEVELS + 1):
            out += [("ip", j, 0, lv), ("ip", j, 1, lv)]
            if lv == 1 and j:
                out.append(("gnend", j - 1))
            out += slot(2)
            out += [("iy", j, 0, lv), ("iy", j, 1, lv)] + slot(2)
            if lv < LEVELS:
                out += [("inv", j, 0, lv), ("inv", j, 1, lv)] + slot(2)
        out += [("tav", j, 0), ("tav", j, 1)] + slot(1) + [("rr", j, 0), ("rr", j, 1)] + slot(1)
        out += [("opa", j, 0), ("opa", j, 1)] + last[:1] + [("pt", j, 0), ("pt", j, 1)] + last[1:2] + [("qq", j, 0), ("qq", j, 1)]
        out += ahead + ([("re", j + 1)] if j + 1 < KT else [])
        for c in range(1, NCK - 1):
            out += [("st", j, c)] + last[1 + c:2 + c]
        out.append(("ost", j))
    gates = [f for m in range(16) for f in parts(("gate2", m), 1)]
    return out + gates[:1] + [("gnm", KT - 1)] + gates[1:2] + [("gnv", KT - 1)] + gates[2:3] + [("gnend", KT - 1)] + gates[3:]


POOL_F = 7
RKV_SLOT = {1: 0, 0: 1, 2: 0}
IN_BANKS = ("lw2", "la2", "lg2", "kkss", "bonus", "tok", "mb", "mk", "inv", "akv", "ip", "iy", "tav", "rr", "pt", "qq", "st", "gnm", "gnv")

BLOCKS = weight_blocks()
BLOCK_AT = {what: b for b, (_, what) in enumerate(BLOCKS)}
SPLIT_AT = {}
for _b, (_kind, _what) in enumerate(BLOCKS):
    if _kind == "split":
        SPLIT_AT[_what] = len(SPLIT_AT)
SPLITS = list(SPLIT_AT)


NSA_UNITS = [(h, qt, br) for h in range(H) for qt in range(TT) for br in range(3)]
MLA_UNITS = [(h, qt, None) for h in range(MH) for qt in range(TT)]
LAG_T, LAG_O = 2, 3


def attention_order(units):
    for i in range(len(units) + LAG_O):
        if i < len(units):
            yield "S", i
        if 0 <= i - LAG_T < len(units):
            yield "PT", i - LAG_T
        if i >= LAG_O:
            yield "O", i - LAG_O


def bank_order():
    out = [("ada", n) for n in range(16)] + [("ss", "mix")]
    for m in range(16):
        out += [("z", m), ("ada", 16 + 2 * m), ("ada", 17 + 2 * m)]
    out += [("vt", 0), ("vt", 1), ("gt",)]
    out += [("ck", kv, ht) for kv in range(2) for ht in range(2)] + [("kc",), ("vc",)]
    out += [("ss", "cq"), ("ss", "ckv")]
    out += [(k, "nsa", u) for k, u in attention_order(NSA_UNITS) if k != "O"]
    out += [("uq", h) for h in range(MH)] + [("uk", i) for i in range(MH // 2)] + [("uv", t) for t in range(TT)]
    out += [(k, "mla", u) for k, u in attention_order(MLA_UNITS) if k != "O"]
    out += [("gate", m) for m in range(16)]
    for m in range(KT):
        out += [("on", m), ("om", m)]
    out += [("wo", m) for m in range(KT)]
    out += [("ss", "mlp")] + [(f"fc{half}", 1, c, m) for half, c in mlp_order() for m in range(KT)]
    out += [("ss", "final"), ("ss", "mix2"), ("lh", 0), ("lh", 1), ("lh", 2)]
    for f in rwkv_order():
        if f[0] == "part" and f[3] == KT:
            out.append(f[1])
        elif f[0] in IN_BANKS:
            out.append(f)
    out += [("convmean",), ("ss", "conv")]
    for m in range(KT):
        out += [("pr", m), ("pc", m)]
    out += [("wo2", m) for m in range(KT)]
    out += [("ss", "ff2")] + [(f"fc{half}", 2, c, m) for half, c in mlp_order() for m in range(KT)]
    return out + [("ss", "final2")]


BANK_ORDER = bank_order()
FILL = {name: n for n, name in enumerate(BANK_ORDER)}


def bank_places():
    bank, turn, used, at = {}, {}, [0] * NBANK, [0, 0, 0]
    inside = set(f[1] if f[0] == "part" else f for f in rwkv_order())
    for name in BANK_ORDER:
        if name not in inside:
            kind, base, n = 0, 0, NBANK
        elif name[0] in ("rkv", "glu", "gate2"):
            kind, base, n = 1, NBANK - 2, 2
        else:
            kind, base, n = 2, 0, NBANK - 2
        b = base + at[kind] % n
        at[kind] += 1
        bank[name], turn[name] = b, used[b]
        used[b] += 1
    return bank, turn


BANK, TURN = bank_places()
BLOCK_LAST = {}
for _what in SPLITS:
    BLOCK_LAST[_what] = FILL[{"uq": lambda w: ("uq", 2 * w[1] + 1), "uk": lambda w: ("uk", MH // 2 - 1),
                              "uv": lambda w: ("uv", TT - 1), "nm": lambda w: ("om", w[1])}.get(_what[0], lambda w: w)(_what)]

NORMS = [("mix", KT), ("cq", 3), ("ckv", 2), ("mlp", KT), ("final", KT), ("mix2", KT), ("conv", KT), ("ff2", KT),
         ("final2", KT)]
SQ_AT = {}
for _name, _n in NORMS:
    for _k in range(_n):
        SQ_AT[_name, _k] = len(SQ_AT)

def split_order():
    out = [("mix", k) for k in range(KT)] + [("cq", k) for k in range(3)] + [("ckv", k) for k in range(2)]
    out += [("y", m) for m in range(KT)] + [("mlp", k) for k in range(KT)]
    out += [("hid", 1, c, m) for c in range(NCH) for m in range(KT)]
    out += [("mix2", k) for k in range(KT)] + [("conv", k) for k in range(KT)]
    out += [("y2", m) for m in range(KT)] + [("ff2", k) for k in range(KT)]
    return out + [("hid", 2, c, m) for c in range(NCH) for m in range(KT)]


SPLIT_EVENTS = split_order()
EVENT = {name: n for n, name in enumerate(SPLIT_EVENTS)}
NTMP = 3


def block1_constants():
    f = np.float32
    i = np.arange(P)[:, None]
    off = np.arange(S)[None, :] - (S - P)
    dist = (i - off).astype(f)
    slopes = (2.0 ** (-8.0 * np.arange(1, H + 1) / H)).astype(f)
    seen = off <= i
    alibi = np.where(seen[:, None], slopes[None, :, None] * dist[:, None], f(BIG)).astype(f)
    t = np.arange(S).reshape(TT, P).T[:, :, None, None]
    dc = (t - (np.arange(NC) * CS + CL - 1)).astype(f)
    cmpb = np.where(dc >= 0, slopes[None, None, :, None] * dc, f(BIG)).astype(f)
    causal = np.where(seen, f(0), f(BIG)).astype(f)
    half = ROPE // 2
    inv = (f(10000.0) ** (-np.arange(half, dtype=f) / f(half))).astype(f)
    ang = (np.arange(S, dtype=f)[:, None] * inv[None, :]).astype(f)
    cos, sin = np.cos(ang).T.astype(f), np.sin(ang).T.astype(f)
    rope = np.zeros((P, S), f)
    rope[64:96] = np.concatenate([cos, cos])
    rope[96:128] = np.concatenate([-sin, sin])
    return {"eye_ones": np.concatenate([np.eye(P, dtype=f), np.ones((P, P), f)], 1), "alibi": alibi.reshape(P, H * S),
            "cmpb": cmpb.reshape(P, TT * H * NC), "causal": causal, "rope": rope}


def rwkv_constants():
    i, t = np.arange(P)[:, None], np.arange(P)[None, :]
    same = i // CH == t // CH
    out = [same & (i < t), same & (i <= t)]
    for lv in range(LEVELS + 1):
        b = 1 << lv
        joins = (i // (2 * b) == t // (2 * b)) & (i // b % 2 == 0) & (t // b % 2 == 1)
        out.append(joins if lv == 0 else joins.T)
    out.append(i // RN == t // RN)
    return np.concatenate(out, 1).astype(np.float32)


CONSTS = {"rw": (2 + LEVELS + 1 + 1) * P, "eye_ones": 2 * P, "alibi": H * S, "cmpb": TT * H * NC, "causal": S, "rope": S}


def build_program(nc, io):
    x_in, vec_in, w_in, out = io["x"], io["vec"], io["w"], io["out"]
    ctx = ExitStack()
    with ctx:
        def sb(name, shape, dt=F32, at=ctx):
            return at.enter_context(nc.sbuf_tensor(name, shape, dt))

        def sem(name):
            return ctx.enter_context(nc.semaphore(name))

        x = sb("x", [P, KT, S])
        vec = sb("vec", [P, NVEC])
        eye_ones = sb("eye_ones", [P, 2 * P])
        eye, ones = eye_ones[:, 0:P], eye_ones[:, P:2 * P]
        raw = sb("raw", [P, NRAW, D])
        whi = sb("whi", [P, NHL, D], F32R)
        wlo = sb("wlo", [P, NHL, D], F32R)
        ah = sb("ah", [P, 2, KT, S], F32R)
        tmp = sb("tmp", [P, NTMP, S])
        sq = sb("sq", [P, 2, S])
        rstd = sb("rstd", [P, S])
        mod = sb("mod", [P, 48])
        modg = sb("modg", [P, 2 * KT])
        psum = ctx.enter_context(nc.psum_tensor("psum", [P, 8, S], F32))

        mixer = ExitStack()
        oh = sb("oh", [P, 2, KT, S], F32R, mixer)
        with ExitStack() as at:
            cqh = sb("cqh", [P, 2, 5, S], F32R, at)
            zkr = sb("zkr", [P, S], F32, at)
            rope = sb("rope", [P, S], F32, at)
            causal = sb("causal", [P, S], F32, at)
            with ExitStack() as nsa:
                qT = sb("qT", [P, H // 2, S], F32, nsa)
                ksd = sb("ksd", [P, G, S], F32, nsa)
                kwd = sb("kwd", [P, G, S], F32, nsa)
                vtok = sb("vtok", [P, 2, TT, P], F32, nsa)
                kcT = sb("kcT", [P, G * NC], F32, nsa)
                vc = sb("vc", [P, G * DH], F32, nsa)
                gates = sb("gates", [P, TT, 32], F32, nsa)
                alibi = sb("alibi", [P, H, S], F32, nsa)
                cmpb = sb("cmpb", [P, TT, H, NC], F32, nsa)
                sm = sb("sm", [P, 3, S], F32, nsa)
                pt = sb("pt", [P, 2, S], F32, nsa)
                gT = zkr[0:32, :]
                stat = sb("stat", [P, 3, 4], F32, nsa)
            with ExitStack() as mla:
                qcat = sb("qcat", [P, MH, S], F32, mla)
                kcat = sb("kcat", [P, MH, S], F32, mla)
                vm = sb("vm", [P, TT, MH * MV], F32, mla)
                rtmp = sb("rtmp", [P, S], F32, mla)
                sm2 = sb("sm2", [P, 3, S], F32, mla)
                pt2 = sb("pt2", [P, 2, S], F32, mla)
                stat2 = sb("stat2", [P, 3, 4], F32, mla)
        with ExitStack() as at:
            yh = sb("yh", [P, 2, KT, S], F32R, at)
            sg = sb("sg", [P, 16, S], F32, at)
        mixer.close()
        with ExitStack() as at:
            kcd = sb("kcd", [P, 2, G, S], F32, at)
            bkv = sb("bkv", [P, 2, LP, G * NC], F32, at)
            hid = sb("hid", [P, 2, 2, G * NC], F32, at)
            vT = sb("vT", [P, 2, S], F32, at)
            zd = sb("zd", [P, 5, S], F32, at)
        with ExitStack() as at:
            taken = [0]

            def work(name, cols):
                taken[0] += cols
                return sb(name, [P, cols], F32, at)

            def both(name, cols):
                return [work(f"{name}{hh}", cols)[:, :].rearrange("p (t n) -> p t n", t=TT) for hh in range(2)]

            rw = work("rw", CONSTS["rw"])
            rkvp = work("rkvp", 2 * (S + 1))[:, :].rearrange("p (i s) -> p i s", i=2)
            rkv = work("rkv", 3 * S)[:, :].rearrange("p (i s) -> p i s", i=3)
            omu = work("omu", 24)
            lh = work("lh", 2 * S)[:, :].rearrange("p (i s) -> p i s", i=2)
            lwt = work("lwt", 4 * P)[:, :].rearrange("p (i n) -> p i n", i=2)
            upad = work("upad", S + CONV - 1)
            arow = work("arow", 2 * S)[:, :].rearrange("p (t a n) -> p t a n", t=TT, a=2)
            bh, kh = work("bh", S), work("kh", S)
            ewall = work("ewall", NCK * (CH + 1))[:, :].rearrange("p (c n) -> p c n", c=NCK)
            ew, ewp = ewall[:, :, 1:], ewall[:, :, 0:CH]
            ewi = work("ewi", S)
            sw, cw, rate, kk, nrm = (work(n, S) for n in ("sw", "cw", "rate", "kk", "nrm"))
            bv = work("bv", 2 * S)[:, :].rearrange("p (i s) -> p i s", i=2)
            gate = work("gate", 2 * S)[:, :].rearrange("p (i s) -> p i s", i=2)
            wc = work("wc", 2 * NCK)[:, :].rearrange("p (i c) -> p i c", i=2)
            ao = work("ao", 2 * S)[:, :].rearrange("p (k s) -> p k s", k=2)
            assert taken[0] <= 4 * KT * S
            mb = both("mb", 4 * 2 * P)
            mk = both("mk", 4 * 2 * P)
            ix, iy, ip = both("ix", S), both("iy", S), both("ip", S)
            ftok = work("ftok", 2 * S)[:, :].rearrange("p (t h a n) -> p t h a n", t=TT, h=2, a=2)
            tav = work("tav", 2 * S)[:, :].rearrange("p (t a h n) -> p t a h n", t=TT, a=2, h=2)
            btok, ktok, vtk = (work(n, S)[:, :].rearrange("p (t n) -> p t n", t=TT) for n in ("btok", "ktok", "vtk"))
            rp = work("rp", S)
            pts = work("pts", NCK * P)[:, :].rearrange("p (c n) -> p c n", c=NCK)
            qs = work("qs", NCK * RN)[:, :].rearrange("p (c n) -> p c n", c=NCK)
            st = work("st", NCK * RN)[:, :].rearrange("p (c n) -> p c n", c=NCK)
            su = work("su", RN)
        usig, og, tf = tmp[:, 0, :], tmp[:, 1, :], tmp[:, 2, :]
        strict_incl = rw[:, 0:2 * P]
        level = [rw[:, (2 + lv) * P:(3 + lv) * P] for lv in range(LEVELS + 1)]
        heads = rw[:, (3 + LEVELS) * P:(4 + LEVELS) * P]
        with ExitStack() as at:
            with ExitStack() as before:
                aof = sb("aof", [P, KT, S], F32, before)
            coh = sb("coh", [P, 2, KT, S], F32R, at)
            aoh = sb("aoh", [P, 2, KT, S], F32R, at)
            sg2 = sb("sg2", [P, 16, S], F32, at)
        ao_kept = nc.dram_tensor("ao_kept", (KT, P, S), F32, kind="Internal").ap()
        x_kept = nc.dram_tensor("x_kept", (P, KT * S), F32, kind="Internal").ap()
        with ExitStack() as at:
            hidden = [sb(f"hidden{i}", [P, 2, KT, S], F32R, at) for i in range(2)]

        x_loaded, vec_loaded = sem("x_loaded"), sem("vec_loaded")
        const_loaded = {n: sem(f"{n}_loaded") for n in CONSTS}
        w_loaded = [sem(f"w_loaded{i}") for i in range(NRAW)]
        raw_used = sem("raw_used")
        hi_done, lo_done = sem("hi_done"), sem("lo_done")
        filled = sem("filled")
        emptied = [sem(f"emptied{i}") for i in range(NBANK)]
        dve_step, act_step = sem("dve_step"), sem("act_step")
        sq_ready, sq_used = sem("sq_ready"), sem("sq_used")
        root_done = sem("root_done")
        pre_split, hi_ready, hl_ready = sem("pre_split"), sem("hi_ready"), sem("hl_ready")
        modg_ready = sem("modg_ready")
        bkv_ready = sem("bkv_ready")
        exp_done, p_ready, o_done = sem("exp_done"), sem("p_ready"), sem("o_done")
        o_hi, o_empty = sem("o_hi"), sem("o_empty")
        nope_done, rope_done, krot_done = sem("nope_done"), sem("rope_done"), sem("krot_done")
        xn_ready = sem("xn_ready")
        zeros_done = sem("zeros_done")
        hp_ready, xm_ready, xm_used = sem("hp_ready"), sem("xm_ready"), sem("xm_used")
        lw_loaded = [sem(f"lw_loaded{i}") for i in range(2)]
        pool_f = sem("pool_f")
        mu_ready = sem("mu_ready")
        cw_ready, exp_ready = sem("cw_ready"), sem("exp_ready")
        kk0_ready, kksq_ready, nrm_ready = sem("kk0_ready"), sem("kksq_ready"), sem("nrm_ready")
        kmod_ready, rk_ready, at_ready = sem("kmod_ready"), sem("rk_ready"), sem("at_ready")
        iy0_done, pool_step = [sem(f"iy0_done{hh}") for hh in range(2)], sem("pool_step")
        opv_done, opa_done, ost_done, og_ready = sem("opv_done"), sem("opa_done"), sem("ost_done"), sem("og_ready")
        u_ready = sem("u_ready")
        ao_put, ao_back = [sem(f"ao_put{i}") for i in range(2)], sem("ao_back")
        gnsq_ready, gnroot_done, ao_done = sem("gnsq_ready"), sem("gnroot_done"), sem("ao_done")
        conv_done, cen_ready, convn_ready = sem("conv_done"), sem("cen_ready"), sem("convn_ready")
        ao_hi, ao_ready = sem("ao_hi"), sem("ao_ready")
        x_put, x_back = sem("x_put"), sem("x_back")
        stored = sem("stored")

        def bank(name):
            return psum[:, BANK[name], :]

        def wait_filled(eng, name):
            eng.wait_ge(filled, FILL[name] + 1)

        def wait_emptied(eng, name):
            eng.wait_ge(emptied[BANK[name]], TURN[name] + 1)

        def emptied_by(ins, name):
            ins.then_inc(emptied[BANK[name]], 1)

        def vcol(name, k=0, n=1):
            return vec[:, VEC[name] + k:VEC[name] + k + n]

        def wait_loaded(eng, what):
            b = BLOCK_AT[what]
            eng.wait_ge(w_loaded[b % NRAW], 16 * (b // NRAW + 1))

        def raw_of(what):
            return raw[:, BLOCK_AT[what] % NRAW, :]

        def xm(i, k):
            t = (mb[0], mk[0])[k % 2].rearrange("p t n -> p (t n)")
            return t[:, i * S:i * S + S] if i < 2 else (ix[0], iy[0])[k % 2].rearrange("p t n -> p (t n)")

        def state(c):
            return qs[:, 0, :] if c == 1 else st[:, c, :]

        block = ctx.enter_context(nc.Block())

        @block.sync
        def _(sp):
            sp.dma_start(vec[:, :], vec_in).then_inc(vec_loaded, 16)
            sp.dma_start(x[:, :, :], x_in.rearrange("p (k s) -> p k s", k=KT)).then_inc(x_loaded, 16)
            sp.dma_start(eye_ones[:, :], io["eye_ones"]).then_inc(const_loaded["eye_ones"], 16)
            raws = 0
            for b, (kind, what) in enumerate(BLOCKS):
                if b >= NRAW:
                    old_kind, old = BLOCKS[b - NRAW]
                    if old_kind == "split":
                        sp.wait_ge(lo_done, SPLIT_AT[old] + 1)
                    elif old[0] == "ck" and old[2] < LP // 4 - 1:
                        raws += 1
                        sp.wait_ge(raw_used, raws)
                    elif old[0] == "lora":
                        wait_filled(sp, ("lh", 2))
                    else:
                        wait_filled(sp, old if old[0] != "ck" else ("ck", old[1], 1))
                sp.dma_start(raw[:, b % NRAW, :], w_in[b]).then_inc(w_loaded[b % NRAW], 16)
                if what == ("ada", 15):
                    for n, t in (("rope", rope), ("causal", causal), ("cmpb", cmpb), ("alibi", alibi)):
                        dst = {"cmpb": "p a b c -> p (a b c)", "alibi": "p a b -> p (a b)"}.get(n)
                        sp.dma_start(t.rearrange(dst) if dst else t[:, :], io[n]).then_inc(const_loaded[n], 16)
            sp.wait_ge(xn_ready, 2 * KT)
            sp.dma_start(out.rearrange("p (k s) -> p k s", k=KT), x[:, :, :]).then_inc(stored, 16)
            sp.wait_ge(stored, 16)

        @block.gpsimd
        def _(pool):
            low = [0]

            def weights_ahead(n):
                while low[0] <= min(n, len(SPLITS) - 1):
                    s = low[0]
                    pool.wait_ge(hi_done, s + 1)
                    pool.tensor_tensor(wlo[:, s % NHL, :], raw_of(SPLITS[s]), whi[:, s % NHL, :].bitcast(F32),
                                       ALU.subtract).then_inc(lo_done, 1)
                    low[0] += 1

            weights_ahead(SPLIT_AT["rkv", 0, 1] - 1)
            wait_filled(pool, ("fc2", 1, NCH - 1, KT - 1))
            pool.memset(rkvp[:, :, 0:1], 0.0).then_inc(zeros_done, 1)
            pool.memset(upad[:, 0:CONV - 1], 0.0).then_inc(zeros_done, 1)
            pool.memset(ewall[:, :, 0:1], 1.0).then_inc(zeros_done, 1)
            weights_ahead(SPLIT_AT["rkv", 0, 1])
            pool.wait_ge(zeros_done, 3)
            for k in range(KT):
                pool.wait_ge(hl_ready, EVENT["mix2", k] + 1)
                if k >= 2:
                    pool.wait_ge(xm_ready, 3 * (k - 1))
                hp = rkvp[:, k % 2, :]
                pool.tensor_tensor(hp[:, 1:S + 1], ah[:, 0, k, :].bitcast(F32), ah[:, 1, k, :].bitcast(F32), ALU.add).then_inc(hp_ready, 1)
                pool.wait_ge(hp_ready, 2 * k + 1)
                pool.tensor_tensor(rkv[:, k % 2, :], hp[:, 0:S], hp[:, 1:S + 1], ALU.subtract).then_inc(hp_ready, 1)
            psteps = 0
            for f in rwkv_order():
                kind, j = f[0], f[1]
                n = POOL_F * j if kind != "part" else 0
                if kind == "part" and f[2] == 0:
                    weights_ahead(SPLIT_AT[f[1]] + 1)
                elif kind == "kk":
                    pool.wait_ge(kmod_ready, j + 1)
                    pool.wait_ge(exp_ready, 2 * j + 2)
                    if j:
                        wait_filled(pool, ("mk", j - 1, 1, 1))
                    pool.tensor_tensor(kh[:, :], rkv[:, 1, :], ewi[:, :], ALU.mult).then_inc(pool_f, 1)
                    pool.wait_ge(pool_f, n + 1)
                    pool.tensor_tensor(cw[:, :].rearrange("p (c n) -> p c n", c=NCK), kh[:, :].rearrange("p (c n) -> p c n", c=NCK),
                                       ew[:, :, CH - 1:CH].to_broadcast([P, NCK, CH]), ALU.mult).then_inc(pool_f, 1)
                elif kind == "nrm":
                    pool.wait_ge(nrm_ready, j + 1)
                    pool.wait_ge(kksq_ready, j + 1)
                    pool.tensor_tensor(kk[:, :], kk[:, :], nrm[:, :], ALU.mult).then_inc(pool_f, 1)
                    pool.wait_ge(pool_f, n + 3)
                    pool.tensor_tensor(rate[:, :], kk[:, :], rate[:, :], ALU.mult).then_inc(pool_f, 1)
                    pool.wait_ge(pool_f, n + 4)
                    if j:
                        wait_filled(pool, ("mb", j - 1, 1, 1))
                    pool.tensor_tensor(bh[:, :], rate[:, :], ewi[:, :], ALU.mult).then_inc(pool_f, 1)
                    pool.wait_ge(pool_f, n + 5)
                    pool.wait_ge(cw_ready, j + 1)
                    pool.tensor_tensor(sw[:, :].rearrange("p (c n) -> p c n", c=NCK), bh[:, :].rearrange("p (c n) -> p c n", c=NCK),
                                       ew[:, :, CH - 1:CH].to_broadcast([P, NCK, CH]), ALU.mult).then_inc(pool_f, 1)
                elif kind == "re":
                    wait_emptied(pool, ("rkv", j, 0))
                    pool.wait_ge(exp_ready, 2 * j + 2)
                    if j:
                        wait_filled(pool, ("mk", j - 1, 1, 1))
                        wait_emptied(pool, ("rr", j - 1, 1))
                        wait_emptied(pool, ("rr", j - 1, 0))
                    pool.tensor_tensor(arow[:, :, 1, :].rearrange("p t (c n) -> p t c n", c=2),
                                       rkv[:, 0, :].rearrange("p (t c n) -> p t c n", t=TT, c=2),
                                       ew.rearrange("p (t c) n -> p t c n", t=TT), ALU.mult).then_inc(pool_f, 1)
                elif kind == "iy0" and f[2] == 1:
                    wait_emptied(pool, ("mb", j, 1, 0))
                    wait_emptied(pool, ("mb", j, 1, 1))
                    if j:
                        wait_filled(pool, ("tav", j - 1, 1))
                    pool.tensor_tensor(iy[1], mb[1][:, :, 0:P], level[0].unsqueeze(1).to_broadcast([P, TT, P]),
                                       ALU.mult).then_inc(pool_step, 1)
                    psteps += 1
                    pool.wait_ge(pool_step, psteps)
                    pool.tensor_tensor(iy[1], iy[1], eye.unsqueeze(1).to_broadcast([P, TT, P]), ALU.add).then_inc(iy0_done[1], 1)
            weights_ahead(len(SPLITS))

        @block.tensor
        def _(pe):
            fills = [0]

            def begin(name):
                assert FILL[name] == fills[0], (name, BANK_ORDER[fills[0]])
                fills[0] += 1
                free(name)

            def free(name):
                if TURN[name]:
                    pe.wait_ge(emptied[BANK[name]], TURN[name])

            def three(dst, w, wcols, a, k, first, last, a_moving=True):
                wh, wl = whi[:, w, wcols], wlo[:, w, wcols]
                h_, l_ = a[:, 0, k], a[:, 1, k]
                if a_moving:
                    pe.matmul(dst, wh, h_, start=first, stop=False)
                    pe.matmul(dst, wh, l_, start=False, stop=False)
                    return pe.matmul(dst, wl, h_, start=False, stop=last)
                pe.matmul(dst, h_, wh, start=first, stop=False)
                pe.matmul(dst, l_, wh, start=False, stop=False)
                return pe.matmul(dst, h_, wl, start=False, stop=last)

            def product(name, what, a, kts, col0=0, event=None):
                s = SPLIT_AT[what]
                pe.wait_ge(lo_done, s + 1)
                begin(name)
                for i, k in enumerate(kts):
                    if event is not None:
                        pe.wait_ge(hl_ready, EVENT[event + (i,)] + 1)
                    mm = three(bank(name), s % NHL, slice(col0 + i * P, col0 + i * P + P), a, k, i == 0, i == len(kts) - 1)
                mm.then_inc(filled, 1)

            def ada(n):
                what = ("ada", n)
                wait_loaded(pe, what)
                begin(what)
                for k in range(KT):
                    mm = pe.matmul(bank(what)[:, 0:1], raw_of(what)[:, k * P:k * P + P], vcol("c", k),
                                   start=k == 0, stop=k == KT - 1)
                mm.then_inc(filled, 1)

            def sum_squares(name):
                tiles = dict(NORMS)[name]
                begin(("ss", name))
                for k in range(tiles):
                    n = SQ_AT[name, k]
                    pe.wait_ge(sq_ready, n + 1)
                    mm = pe.matmul(bank(("ss", name)), ones, sq[:, n % 2, :], start=k == 0, stop=k == tiles - 1)
                    mm.then_inc(sq_used if k < tiles - 1 else filled, 1)

            def attention(tag, units, at):
                base = {"nsa": 0, "mla": len(NSA_UNITS)}[tag]
                for kind, u in attention_order(units):
                    h, qt, br = units[u]
                    probs, turned, scores, values = at
                    if kind == "S":
                        q, k, w = scores(h, qt, br)
                        begin(("S", tag, u))
                        pe.matmul(bank(("S", tag, u))[:, 0:w], q, k, start=True, stop=True).then_inc(filled, 1)
                    elif kind == "PT":
                        begin(("PT", tag, u))
                        pe.wait_ge(p_ready, base + u + 1)
                        for kt, (_, n) in enumerate(values(h, qt, br)):
                            mm = pe.transpose(bank(("PT", tag, u))[0:n, kt * P:kt * P + P],
                                              probs[:, u % 3, kt * P:kt * P + n], eye)
                        mm.then_inc(filled, 1)
                    else:
                        wait_emptied(pe, ("PT", tag, u))
                        pair = base_pair[tag] + h // 2
                        if h % 2 == 0 and qt == 0 and br in (0, None) and pair:
                            pe.wait_ge(o_empty, pair)
                        rows = slice(64 * (h % 2), 64 * (h % 2) + 64)
                        vals = values(h, qt, br)
                        for kt, (v, n) in enumerate(vals):
                            mm = pe.matmul(psum[rows, OBANK, qt * P:qt * P + P], v, turned[0:n, u % 2, kt * P:kt * P + P],
                                           start=br in (0, None) and kt == 0, stop=br in (2, None) and kt == len(vals) - 1)
                        mm.then_inc(o_done, 1)

            base_pair = {"nsa": 0, "mla": H // 2}

            pe.wait_ge(vec_loaded, 16)
            for n in range(16):
                ada(n)
            pe.wait_ge(const_loaded["eye_ones"], 16)
            sum_squares("mix")
            for m in range(16):
                product(("z", m), ("z", m), ah, range(KT), event=("mix",) if m == 0 else None)
                ada(16 + 2 * m)
                ada(17 + 2 * m)
            for i, m in enumerate((7, 9)):
                begin(("vt", i))
                wait_emptied(pe, ("z", m))
                for t in range(TT):
                    mm = pe.transpose(bank(("vt", i))[:, t * P:t * P + P], vT[:, i, t * P:t * P + P], eye)
                mm.then_inc(filled, 1)
            begin(("gt",))
            wait_emptied(pe, ("z", 10))
            for t in range(TT):
                mm = pe.transpose(bank(("gt",))[:, t * 32:t * 32 + 32], gT[:, t * P:t * P + P], eye[0:32, 0:32])
            mm.then_inc(filled, 1)
            for kv in range(2):
                begin(("ck", kv, 0))
                begin(("ck", kv, 1))
                pe.wait_ge(bkv_ready, kv + 1)
                for q in range(LP // 4):
                    wait_loaded(pe, ("ck", kv, q))
                    w = raw_of(("ck", kv, q))
                    for ht in range(2):
                        for i in range(4):
                            lp = 4 * q + i
                            mm = pe.matmul(bank(("ck", kv, ht))[:, 0:G * NC], w[:, i * CHID + ht * P:i * CHID + ht * P + P],
                                           bkv[:, kv, lp, :], start=lp == 0, stop=lp == LP - 1)
                        if q == LP // 4 - 1:
                            mm.then_inc(filled, 1)
                        elif ht == 1:
                            mm.then_inc(raw_used, 1)
            begin(("kc",))
            for ht in range(2):
                wait_emptied(pe, ("ck", 0, ht))
                mm = pe.matmul(bank(("kc",))[:, 0:G * NC], vcol("w_ck2", ht * P, P), hid[:, 0, ht, :], start=ht == 0, stop=ht == 1)
            mm.then_inc(filled, 1)
            begin(("vc",))
            for g in range(G):
                for ht in range(2):
                    wait_emptied(pe, ("ck", 1, ht))
                    mm = pe.matmul(bank(("vc",))[0:NC, g * DH:g * DH + DH], hid[:, 1, ht, g * NC:g * NC + NC],
                                   vcol("w_cv2", ht * DH, DH), start=ht == 0, stop=ht == 1)
            mm.then_inc(filled, 1)
            sum_squares("cq")
            sum_squares("ckv")

            def nsa_scores(h, qt, br):
                rows = slice(64 * (h % 2), 64 * (h % 2) + 64)
                q = qT[rows, h // 2, qt * P:qt * P + P]
                if br == 0:
                    return q, kcT[rows, (h // HG) * NC:(h // HG) * NC + NC], NC
                return q, (ksd, kwd)[br - 1][rows, h // HG, 0:qt * P + P], qt * P + P

            def nsa_values(h, qt, br):
                g = h // HG
                if br == 0:
                    return [(vc[0:NC, g * DH:g * DH + DH], NC)]
                return [(vtok[:, br - 1, kt, g * DH:g * DH + DH], P) for kt in range(qt + 1)]

            for m in (0, 1, 2, 3, 6, 8):
                wait_emptied(pe, ("z", m))
            for n in (("vt", 0), ("vt", 1), ("kc",), ("vc",)):
                wait_emptied(pe, n)
            attention("nsa", NSA_UNITS, (sm, pt, nsa_scores, nsa_values))

            for h in range(MH):
                product(("uq", h), ("uq", h // 2), cqh, range(3), (h % 2) * 3 * P, event=("cq",) if h == 0 else None)
            for i in range(MH // 2):
                product(("uk", i), ("uk",), cqh, range(3, 5), i * 2 * P, event=("ckv",) if i == 0 else None)
            s = SPLIT_AT[("uv",)]
            pe.wait_ge(lo_done, s + 1)
            for t in range(TT):
                begin(("uv", t))
                for k in range(2):
                    mm = three(bank(("uv", t)), s % NHL, slice(k * S, k * S + S), cqh[:, :, :, t * P:t * P + P], 3 + k,
                               k == 0, k == 1, a_moving=False)
                mm.then_inc(filled, 1)

            def mla_scores(h, qt, br):
                return qcat[0:DQK, h, qt * P:qt * P + P], kcat[0:DQK, h, 0:qt * P + P], qt * P + P

            def mla_values(h, qt, br):
                return [(vm[:, kt, h * MV:h * MV + MV], P) for kt in range(qt + 1)]

            pe.wait_ge(rope_done, MH)
            pe.wait_ge(krot_done, 1)
            for i in range(MH // 2):
                wait_emptied(pe, ("uk", i))
            for t in range(TT):
                wait_emptied(pe, ("uv", t))
            attention("mla", MLA_UNITS, (sm2, pt2, mla_scores, mla_values))

            for m in range(16):
                product(("gate", m), ("gate", m), ah, range(KT))
            pe.wait_ge(o_empty, H // 2 + MH // 2)
            for m in range(KT):
                product(("on", m), ("nm", m), oh, range(4))
                product(("om", m), ("nm", m), oh, range(4, 8), col0=4 * P)
            for m in range(KT):
                product(("wo", m), ("wo", m), yh, range(KT), event=("y",) if m == 0 else None)
            sum_squares("mlp")

            def mlp(n, first):
                for half, c in mlp_order():
                    for m in range(KT):
                        if half == 1:
                            product(("fc1", n, c, m), ("fc1", n, c, m), ah, range(KT), event=first if (c, m) == (0, 0) else None)
                        else:
                            product(("fc2", n, c, m), ("fc2", n, c, m), hidden[c % 2], range(KT), event=("hid", n, c) if m == 0 else None)

            mlp(1, ("mlp",))
            sum_squares("final")

            sum_squares("mix2")
            for i in range(3):
                begin(("lh", i))
            wait_loaded(pe, ("lora", 0))
            wait_loaded(pe, ("lora", 1))
            for k in range(KT):
                for i, (blk, c0, n) in enumerate(((0, 0, LORA), (0, LORA, LORA), (1, 0, P))):
                    pe.wait_ge(xm_ready, 3 * k + i + 1)
                    mm = pe.matmul(bank(("lh", i))[0:n, :], raw_of(("lora", blk))[:, k * P + c0:k * P + c0 + n], xm(i, k),
                                   start=k == 0, stop=k == KT - 1)
                    mm.then_inc(xm_used if k < KT - 1 else filled, 1)
            for f in rwkv_order():
                kind, j = f[0], f[1]
                if kind == "part":
                    what, k0, k1 = f[1:]
                    n = SPLIT_AT[what]
                    if k0 == 0:
                        pe.wait_ge(lo_done, n + 1)
                        free(what)
                    for k in range(k0, k1):
                        mm = three(bank(what), n % NHL, slice(k * P, k * P + P), ah, k, k == 0, k == KT - 1)
                    if k1 == KT:
                        assert FILL[what] == fills[0], (what, BANK_ORDER[fills[0]])
                        fills[0] += 1
                        mm.then_inc(filled, 1)
                    continue
                if kind in IN_BANKS:
                    begin(f)
                    b = bank(f)
                elif kind not in ("opv", "opa", "ost"):
                    continue
                if kind in ("lw2", "la2", "lg2"):
                    pe.wait_ge(lw_loaded[j % 2], 16 * (j // 2 + 1))
                    for i in range(3):
                        wait_emptied(pe, ("lh", i))
                    rows, cols, i = {"lw2": (slice(0, LORA), slice(0, P), 0), "la2": (slice(LORA, P), slice(0, P), 0),
                                     "lg2": (slice(0, P), slice(P, 2 * P), 1)}[kind]
                    mm = pe.matmul(b, lwt[rows, j % 2, cols], lh[rows, i, :], start=True, stop=True)
                elif kind == "kkss":
                    pe.wait_ge(kksq_ready, j + 1)
                    mm = pe.matmul(b, heads, sq[:, 0, :], start=True, stop=True)
                elif kind == "bonus":
                    pe.wait_ge(rk_ready, j + 1)
                    mm = pe.matmul(b, heads, tf, start=True, stop=True)
                elif kind == "tok":
                    i = f[2]
                    if i == 0:
                        pe.wait_ge(at_ready, j + 1)
                    elif i < 3:
                        pe.wait_ge(pool_f, POOL_F * j + (6, 2)[i - 1])
                    for t in range(TT):
                        cols = slice(t * P, t * P + P)
                        src = (arow[:, t, 0, :], sw[:, cols], cw[:, cols], rkv[:, 2, cols])[i]
                        mm = pe.transpose(b[:, cols], src, eye)
                elif kind in ("mb", "mk"):
                    hh, half = f[2], f[3]
                    rows = slice(RN * hh, RN * hh + RN)
                    src = bh if kind == "mb" else kh
                    pe.wait_ge(at_ready, j + 1)
                    pe.wait_ge(pool_f, POOL_F * j + 7)
                    for n in range(2):
                        t = 2 * half + n
                        mm = pe.matmul(b[:, n * 2 * P:n * 2 * P + 2 * P], src[rows, t * P:t * P + P],
                                       arow[rows, t, :, :].rearrange("p a n -> p (a n)"), start=True, stop=True)
                elif kind == "inv":
                    hh, lv = f[2], f[3]
                    if lv == 0:
                        pe.wait_ge(iy0_done[hh], j + 1)
                    else:
                        wait_emptied(pe, ("iy", j, hh, lv))
                    for t in range(TT):
                        mm = pe.transpose(b[:, t * P:t * P + P], iy[hh][:, t, :], eye)
                elif kind == "akv":
                    hh = f[2]
                    wait_emptied(pe, ("mk", j, hh, 0))
                    wait_emptied(pe, ("mk", j, hh, 1))
                    wait_emptied(pe, ("tok", j, 3))
                    for t in range(TT):
                        mm = pe.matmul(b[:, t * RN:t * RN + RN], mk[hh][:, t, 0:P], vtk[:, t, hh * RN:hh * RN + RN], start=True, stop=True)
                elif kind == "ip":
                    hh, lv = f[2], f[3]
                    wait_emptied(pe, ("inv", j, hh, lv - 1))
                    for t in range(TT):
                        mm = pe.matmul(b[:, t * P:t * P + P], mb[hh][:, t, 0:P], ix[hh][:, t, :], start=True, stop=True)
                elif kind == "iy":
                    hh, lv = f[2], f[3]
                    wait_emptied(pe, ("ip", j, hh, lv))
                    for t in range(TT):
                        mm = pe.matmul(b[:, t * P:t * P + P], ip[hh][:, t, :], iy[hh][:, t, :], start=True, stop=True)
                elif kind == "tav":
                    hh = f[2]
                    wait_emptied(pe, ("iy", j, hh, LEVELS))
                    wait_emptied(pe, ("akv", j, hh))
                    for t in range(TT):
                        mm = pe.matmul(b[:, t * P:t * P + P], iy[hh][:, t, :], ftok[:, t, hh, :, :].rearrange("p a n -> p (a n)"),
                                       start=True, stop=True)
                elif kind == "rr":
                    hh = f[2]
                    wait_emptied(pe, ("tav", j, hh))
                    for t in range(TT):
                        mm = pe.matmul(b[RN * hh:RN * hh + RN, t * P:t * P + P], tav[:, t, 0, hh, :], mb[hh][:, t, P:2 * P],
                                       start=True, stop=True)
                elif kind == "opv":
                    hh = f[2]
                    wait_emptied(pe, ("mk", j, hh, 0))
                    wait_emptied(pe, ("mk", j, hh, 1))
                    wait_emptied(pe, ("tok", j, 3))
                    if j:
                        pe.wait_ge(og_ready, j)
                    else:
                        pe.wait_ge(o_empty, H // 2 + MH // 2)
                    for t in range(TT):
                        mm = pe.matmul(psum[RN * hh:RN * hh + RN, OBANK, t * P:t * P + P], vtk[:, t, hh * RN:hh * RN + RN],
                                       mk[hh][:, t, P:2 * P], start=t == 0, stop=False, skip_group_check=True)
                    mm.then_inc(opv_done, 1)
                elif kind == "opa":
                    hh = f[2]
                    wait_emptied(pe, ("tav", j, hh))
                    for t in range(TT):
                        mm = pe.matmul(psum[RN * hh:RN * hh + RN, OBANK, t * P:t * P + P], tav[:, t, 1, hh, :],
                                       mb[hh][:, t, P:2 * P], start=False, stop=False, skip_group_check=True)
                    mm.then_inc(opa_done, 1)
                elif kind in ("pt", "qq"):
                    rows = slice(CH * f[2], CH * f[2] + CH)
                    for t in range(TT):
                        dst = b[:, t * P:t * P + P]
                        if kind == "pt":
                            mm = pe.matmul(dst, tav[rows, t, 0, :, :].rearrange("p h n -> p (h n)"), btok[rows, t, :], start=True, stop=True)
                        else:
                            pe.matmul(dst, btok[rows, t, :], tav[rows, t, 1, :, :].rearrange("p h n -> p (h n)"), start=True, stop=False)
                            mm = pe.matmul(dst, ktok[rows, t, :], vtk[rows, t, :], start=False, stop=True)
                elif kind == "st":
                    c = f[2]
                    if c == 1:
                        for half in range(2):
                            wait_emptied(pe, ("pt", j, half))
                            wait_emptied(pe, ("qq", j, half))
                    else:
                        wait_emptied(pe, ("st", j, c - 1))
                    mm = pe.matmul(b[:, 0:RN], pts[:, c, :], state(c), start=True, stop=True)
                elif kind == "ost":
                    wait_emptied(pe, ("st", j, NCK - 2))
                    wait_emptied(pe, ("rr", j, 0))
                    wait_emptied(pe, ("rr", j, 1))
                    for c in range(1, NCK):
                        for hh in range(2):
                            rows, cols = slice(RN * hh, RN * hh + RN), slice(c * CH, c * CH + CH)
                            mm = pe.matmul(psum[rows, OBANK, cols], state(c)[rows, :], rp[rows, cols], start=False, stop=True,
                                           skip_group_check=True)
                    mm.then_inc(ost_done, 1)
                elif kind == "gnm":
                    pe.wait_ge(og_ready, j + 1)
                    mm = pe.matmul(b, heads, og, start=True, stop=True)
                elif kind == "gnv":
                    pe.wait_ge(gnsq_ready, j + 1)
                    mm = pe.matmul(b, heads, sq[:, 1, :], start=True, stop=True)
                if kind in IN_BANKS:
                    mm.then_inc(filled, 1)
            begin(("convmean",))
            for k in range(KT):
                pe.wait_ge(conv_done, k + 1)
                mm = pe.matmul(bank(("convmean",)), ones, x[:, k, :], start=k == 0, stop=k == KT - 1)
            mm.then_inc(filled, 1)
            sum_squares("conv")
            pe.wait_ge(ao_ready, KT)
            for m in range(KT):
                product(("pr", m), ("pr", m), aoh, range(KT))
                product(("pc", m), ("pc", m), coh, range(KT), event=("conv",) if m == 0 else None)
            for m in range(KT):
                product(("wo2", m), ("wo2", m), ah, range(KT), event=("y2",) if m == 0 else None)
            sum_squares("ff2")
            mlp(2, ("ff2",))
            sum_squares("final2")

        @block.scalar
        def _(act):
            split = [0]

            def weights_ahead(n):
                while split[0] <= min(n, len(SPLITS) - 1):
                    s = split[0]
                    wait_loaded(act, SPLITS[s])
                    if s >= NHL:
                        act.wait_ge(filled, BLOCK_LAST[SPLITS[s - NHL]] + 1)
                    act.activation(whi[:, s % NHL, :], raw_of(SPLITS[s]), ACT.Copy).then_inc(hi_done, 1)
                    split[0] += 1

            def squares(name, src, wait):
                for k in range(dict(NORMS)[name]):
                    n = SQ_AT[name, k]
                    wait(k)
                    if n >= 2:
                        for nm, tiles in NORMS:
                            if n - 2 == SQ_AT[nm, tiles - 1]:
                                wait_filled(act, ("ss", nm))
                        used = sum(1 for e, (q, kk) in enumerate(SQ_AT) if e <= n - 2 and kk < dict(NORMS)[q] - 1)
                        act.wait_ge(sq_used, used)
                    act.activation(sq[:, n % 2, :], src[:, k, :], ACT.Square).then_inc(sq_ready, 1)

            def root(name):
                wait_emptied(act, ("ss", name))
                act.activation(rstd[:, :], rstd[:, :], ACT.Sqrt).then_inc(root_done, 1)

            def high(event, dst, bias=0.0):
                n = EVENT[event]
                act.wait_ge(pre_split, n + 1)
                act.activation(dst, tmp[:, n % NTMP, :], ACT.Identity, bias=bias).then_inc(hi_ready, 1)

            def empty(name, dst, src=None, **kw):
                wait_filled(act, name)
                emptied_by(act.activation(dst, bank(name) if src is None else src, kw.pop("func", ACT.Copy), **kw), name)

            act.wait_ge(x_loaded, 16)
            squares("mix", x, lambda k: None)
            root("mix")
            weights_ahead(NHL - 1)
            act.wait_ge(modg_ready, 1)
            for k in range(KT):
                high(("mix", k), ah[:, 0, k, :], bias=mod[:, k:k + 1])
            for m in range(16):
                weights_ahead(min(SPLIT_AT["z", m] + 1, SPLIT_AT["z", 15]))
                z = bank(("z", m))
                if m < 4:
                    empty(("z", m), qT[:, m, :], scale=-DH ** -0.5)
                elif m in (4, 5):
                    wait_filled(act, ("z", m))
                    for g in range(G):
                        rows = slice(64 * g, 64 * g + 64)
                        act.activation(kcd[0:64, m - 4, g, :], z[rows, :], ACT.Copy).then_inc(act_step, 1)
                        last = act.activation(kcd[64:128, m - 4, g, 0:S - 1], z[rows, 1:S], ACT.Copy)
                        if g < G - 1:
                            last.then_inc(act_step, 1)
                    emptied_by(last, ("z", m))
                elif m in (6, 8):
                    wait_filled(act, ("z", m))
                    dst = ksd if m == 6 else kwd
                    for g in range(G):
                        for half in range(2):
                            last = act.activation(dst[64 * half:64 * half + 64, g, :], z[64 * g:64 * g + 64, :], ACT.Copy)
                            if (g, half) != (G - 1, 1):
                                last.then_inc(act_step, 1)
                    emptied_by(last, ("z", m))
                elif m in (7, 9):
                    empty(("z", m), vT[:, (m - 7) // 2, :])
                elif m == 10:
                    wait_filled(act, ("z", m))
                    act.activation(gT[:, :], z[0:32, :], ACT.Sigmoid).then_inc(act_step, 1)
                    emptied_by(act.activation(zkr[64:128, :], z[64:128, :], ACT.Copy), ("z", m))
                else:
                    empty(("z", m), zd[:, m - 11, :])
            for i in range(2):
                empty(("vt", i), vtok[:, i, :, :].rearrange("p t n -> p (t n)"))
            empty(("gt",), gates[:, :, :].rearrange("p t n -> p (t n)"), bank(("gt",))[:, 0:TT * 32])
            for kv in range(2):
                for ht in range(2):
                    empty(("ck", kv, ht), hid[:, kv, ht, :], bank(("ck", kv, ht))[:, 0:G * NC], func=ACT.Silu)
            empty(("kc",), kcT[:, :], bank(("kc",))[:, 0:G * NC])
            empty(("vc",), vc[0:NC, :], bank(("vc",))[0:NC, 0:G * DH])
            for name, k0, n in (("cq", 0, 3), ("ckv", 3, 2)):
                squares(name, zd[:, k0:k0 + n, :], lambda k: wait_emptied(act, ("z", 11 + k0 + k)))
                root(name)
                for k in range(n):
                    high((name, k), cqh[:, 0, k0 + k, :])
            weights_ahead(SPLIT_AT["uq", 0] + 1)

            def attention(tag, units, probs, turned, st):
                base = {"nsa": 0, "mla": len(NSA_UNITS)}[tag]
                per_pair = 2 * TT * (3 if tag == "nsa" else 1)
                for kind, u in attention_order(units):
                    if kind == "S":
                        h, qt, br = units[u]
                        w = NC if br == 0 else qt * P + P
                        wait_emptied(act, ("S", tag, u))
                        act.activation(probs[:, u % 3, 0:w], probs[:, u % 3, 0:w], ACT.Exp, bias=st[:, u % 3, 0:1],
                                       scale=-1.0, accum_out=st[:, u % 3, 1:2]).then_inc(exp_done, 1)
                    elif kind == "PT":
                        h, qt, br = units[u]
                        if u >= 2:
                            act.wait_ge(o_done, base + u - 1)
                        if br == 0:
                            empty(("PT", tag, u), turned[0:NC, u % 2, 0:P], bank(("PT", tag, u))[0:NC, 0:P])
                        else:
                            empty(("PT", tag, u), turned[:, u % 2, 0:qt * P + P], bank(("PT", tag, u))[:, 0:qt * P + P])
                    elif (u + 1) % per_pair == 0:
                        act.wait_ge(o_done, base + u + 1)
                        pair = u // per_pair + (H // 2 if tag == "mla" else 0)
                        act.activation(oh[:, 0, pair, :], psum[:, OBANK, :], ACT.Copy).then_inc(o_hi, 1)

            attention("nsa", NSA_UNITS, sm, pt, stat)
            for h in range(MH):
                weights_ahead(SPLIT_AT["uq", h // 2] + 1)
                wait_filled(act, ("uq", h))
                act.activation(qcat[0:NOPE, h, :], bank(("uq", h))[0:NOPE, :], ACT.Copy, scale=-DQK ** -0.5).then_inc(nope_done, 1)
            for i in range(MH // 2):
                weights_ahead(SPLIT_AT["uk",] + 1)
                wait_filled(act, ("uk", i))
                for half in range(2):
                    last = act.activation(kcat[0:NOPE, 2 * i + half, :], bank(("uk", i))[64 * half:64 * half + 64, :], ACT.Copy)
                    if half == 0:
                        last.then_inc(act_step, 1)
                emptied_by(last, ("uk", i))
            for t in range(TT):
                empty(("uv", t), vm[:, t, :])
            weights_ahead(SPLIT_AT["gate", 0] + 1)
            attention("mla", MLA_UNITS, sm2, pt2, stat2)
            for m in range(16):
                weights_ahead(SPLIT_AT["gate", m] + 1)
                empty(("gate", m), sg[:, m, :], func=ACT.Sigmoid)
            for m in range(KT):
                weights_ahead(SPLIT_AT["nm", m] + 1)
                high(("y", m), yh[:, 0, m, :])
            for m in range(KT):
                weights_ahead(SPLIT_AT["wo", m] + 1)
                if m < KT - 1:
                    wait_filled(act, ("wo", m))
            squares("mlp", x, lambda k: wait_emptied(act, ("wo", k)))
            root("mlp")
            for k in range(KT):
                high(("mlp", k), ah[:, 0, k, :], bias=mod[:, 24 + k:25 + k])

            def mlp(n):
                for half, c in mlp_order():
                    for m in range(KT):
                        what = (f"fc{half}", n, c, m)
                        weights_ahead(SPLIT_AT[what] + 1)
                        if half == 1:
                            e = EVENT["hid", n, c, m]
                            act.wait_ge(pre_split, e - 1)
                            empty(what, sq[:, e % 2, :], func=ACT.Relu)
                            if c >= 2 and m == 0:
                                wait_filled(act, ("fc2", n, c - 2, KT - 1))
                            high(("hid", n, c, m), hidden[c % 2][:, 0, m, :])

            mlp(1)
            squares("final", x, lambda k: wait_emptied(act, ("fc2", 1, NCH - 1, k)))
            root("final")

            wait_filled(act, ("fc2", 1, NCH - 1, KT - 1))
            act.dma_start(rw[:, :], io["rw"]).then_inc(const_loaded["rw"], 16)
            act.wait_ge(xn_ready, KT)
            act.dma_start(x_kept, x[:, :, :].rearrange("p k s -> p (k s)")).then_inc(x_put, 16)
            for j in range(2):
                act.dma_start(lwt[:, j, :], io["lw"][j]).then_inc(lw_loaded[j], 16)
            squares("mix2", x, lambda k: None)
            root("mix2")
            weights_ahead(SPLIT_AT["rkv", 0, 1])
            for k in range(KT):
                high(("mix2", k), ah[:, 0, k, :])
            empty(("lh", 0), lh[0:LORA, 0, :], bank(("lh", 0))[0:LORA, :], func=ACT.Tanh)
            empty(("lh", 1), lh[LORA:P, 0, :], bank(("lh", 1))[0:LORA, :])
            empty(("lh", 2), lh[:, 1, :], func=ACT.Sigmoid)
            for f in rwkv_order():
                kind, j = f[0], f[1]
                if kind == "part":
                    what = f[1]
                    if f[2] == 0:
                        weights_ahead(SPLIT_AT[what] + 1)
                    if f[3] < KT or what[:1] + what[2:] == ("glu", 0):
                        continue
                    if what[0] == "rkv":
                        j, i = what[1:]
                        old = {1: ("rkv", j - 1, 2), 0: ("rkv", j - 1, 0), 2: ("rkv", j, 1)}[i]
                        if old[1] >= 0:
                            wait_emptied(act, old)
                        act.wait_ge(xm_ready, 3 * KT)
                        wait_filled(act, what)
                        act.activation(rkvp[:, RKV_SLOT[i], 1:S + 1], bank(what), ACT.Copy, scale=vcol("mu_rkv_2", 8 * i + j)).then_inc(mu_ready, 1)
                    elif what[0] == "glu":
                        j = what[1]
                        if j:
                            wait_emptied(act, ("glu", j - 1, 0))
                        else:
                            act.wait_ge(hl_ready, EVENT["mix2", KT - 1] + 1)
                        empty(what, usig, func=ACT.Sigmoid)
                    else:
                        empty(what, sg2[:, what[1], :], func=ACT.Sigmoid, bias=vcol("b_gate_2", what[1]))
                elif kind == "lw2":
                    if j:
                        wait_filled(act, ("tok", j - 1, 1))
                    empty(f, sw[:, :], func=ACT.Sigmoid, bias=vcol("decay_w0_2", j))
                elif kind == "la2":
                    if j:
                        act.wait_ge(pool_f, POOL_F * (j - 1) + 5)
                    empty(f, rate[:, :], func=ACT.Sigmoid, bias=vcol("aaa_a0_2", j))
                elif kind == "lg2":
                    if j >= 2:
                        act.wait_ge(ao_done, j - 1)
                    empty(f, gate[:, j % 2, :])
                    if j + 2 < KT:
                        act.dma_start(lwt[:, j % 2, :], io["lw"][j + 2]).then_inc(lw_loaded[j % 2], 16)
                elif kind == "kk":
                    act.wait_ge(kk0_ready, j + 1)
                    if j == 0:
                        wait_filled(act, ("ss", "mix2"))
                    else:
                        wait_filled(act, ("kkss", j - 1))
                    act.activation(sq[:, 0, :], kk[:, :], ACT.Square).then_inc(kksq_ready, 1)
                    act.wait_ge(cw_ready, j + 1)
                    if j:
                        act.wait_ge(pool_f, POOL_F * j)
                        act.wait_ge(at_ready, j)
                    else:
                        act.wait_ge(zeros_done, 3)
                    act.activation(ewi[:, :], cw[:, :], ACT.Exp, scale=DECAY).then_inc(exp_ready, 1)
                    act.activation(ew, cw[:, :].rearrange("p (c n) -> p c n", c=NCK), ACT.Exp, scale=-DECAY).then_inc(exp_ready, 1)
                elif kind == "kkss":
                    if j:
                        act.wait_ge(pool_f, POOL_F * (j - 1) + 3)
                    empty(f, nrm[:, :], func=ACT.Sqrt)
                elif kind == "tok":
                    if f[2] == 0:
                        empty(f, ftok[:, :, :, 0, :], bank(f).rearrange("p (t h n) -> p t h n", t=TT, h=2))
                    else:
                        empty(f, (btok, ktok, vtk)[f[2] - 1][:, :, :], bank(f).rearrange("p (t n) -> p t n", t=TT))
                elif kind == "inv":
                    empty(f, ix[f[2]], bank(f).rearrange("p (t n) -> p t n", t=TT))
                elif kind == "akv":
                    empty(f, ftok[:, :, f[2], 1, :], bank(f)[:, 0:TT * RN].rearrange("p (t n) -> p t n", t=TT))
                elif kind == "tav":
                    empty(f, tav[:, :, :, f[2], :], bank(f).rearrange("p (t a n) -> p t a n", t=TT, a=2))
                elif kind == "qq":
                    wait_filled(act, f)
                    if j:
                        wait_emptied(act, ("st", j - 1, NCK - 2))
                    own = bank(f).rearrange("p (c n) -> p c n", c=4)
                    cs = slice(f[2], NCK, 2)
                    act.activation(qs[0:RN, cs, :], own[0:RN, :, 0:RN], ACT.Copy).then_inc(act_step, 1)
                    emptied_by(act.activation(qs[RN:P, cs, :], own[RN:P, :, RN:P], ACT.Copy), f)
                elif kind == "ost":
                    act.wait_ge(ost_done, j + 1)
                    if j:
                        act.wait_ge(ao_done, j)
                    else:
                        act.wait_ge(hl_ready, EVENT["mix2", KT - 1] + 1)
                    act.activation(og, psum[:, OBANK, :], ACT.Copy).then_inc(og_ready, 1)
                elif kind == "gnm":
                    wait_emptied(act, f)
                    act.activation(sq[:, 1, :], og, ACT.Square).then_inc(gnsq_ready, 1)
                elif kind == "gnv":
                    wait_emptied(act, f)
                    act.activation(rstd[:, :], rstd[:, :], ACT.Sqrt).then_inc(gnroot_done, 1)
                elif kind == "gnend":
                    act.wait_ge(ao_done, j + 1)
                    act.dma_start(ao_kept[j], ao[:, j % 2, :]).then_inc(ao_put[j % 2], 16)
            act.wait_ge(conv_done, KT)
            for i in range(2):
                act.wait_ge(ao_put[i], 16 * KT // 2)
            act.dma_start(aof[:, :, :], ao_kept.rearrange("k p s -> p k s")).then_inc(ao_back, 16)
            act.wait_ge(ao_back, 16)
            for k in range(KT):
                act.activation(aoh[:, 0, k, :], aof[:, k, :], ACT.Copy).then_inc(ao_hi, 1)
            squares("conv", x, lambda k: act.wait_ge(cen_ready, k + 1) if k < KT - 1 else wait_emptied(act, ("convmean",)))
            root("conv")
            act.wait_ge(ao_ready, KT)
            for k in range(KT):
                n = EVENT["conv", k]
                act.wait_ge(convn_ready, k + 1)
                act.wait_ge(hl_ready, n - NTMP + 1)
                act.activation(tmp[:, n % NTMP, :], x[:, k, :], ACT.Silu, bias=vcol("conv_ln_b_2", k)).then_inc(pre_split, 1)
                high(("conv", k), coh[:, 0, k, :])
            act.wait_ge(pre_split, EVENT["conv", KT - 1] + 1)
            act.wait_ge(x_put, 16)
            act.dma_start(x[:, :, :].rearrange("p k s -> p (k s)"), x_kept).then_inc(x_back, 16)
            for m in range(KT):
                weights_ahead(SPLIT_AT["pr", m] + 2)
                high(("y2", m), ah[:, 0, m, :])
            for m in range(KT):
                weights_ahead(SPLIT_AT["wo2", m] + 1)
                if m < KT - 1:
                    wait_filled(act, ("wo2", m))
            squares("ff2", x, lambda k: wait_emptied(act, ("wo2", k)))
            root("ff2")
            for k in range(KT):
                high(("ff2", k), ah[:, 0, k, :])
            mlp(2)
            squares("final2", x, lambda k: wait_emptied(act, ("fc2", 2, NCH - 1, k)))
            root("final2")

        @block.vector
        def _(dve):
            steps = [0]

            def step(ins):
                steps[0] += 1
                ins.then_inc(dve_step, 1)
                dve.wait_ge(dve_step, steps[0])

            def mean_square(name, n, eps=EPS):
                wait_filled(dve, ("ss", name))
                emptied_by(dve.tensor_scalar(rstd[:, :], bank(("ss", name)), 1.0 / n, eps, ALU.mult, ALU.add), ("ss", name))

            def inverse_root(name):
                dve.wait_ge(root_done, [n for n, _ in NORMS].index(name) + 1)
                step(dve.reciprocal(rstd[:, :], rstd[:, :]))

            def low(event, dst_hi, dst_lo, bias=0.0):
                n = EVENT[event]
                dve.wait_ge(hi_ready, n + 1)
                dve.scalar_tensor_tensor(dst_lo, tmp[:, n % NTMP, :], bias, dst_hi.bitcast(F32), ALU.add,
                                         ALU.subtract).then_inc(hl_ready, 1)

            def slot(event):
                n = EVENT[event]
                if n >= NTMP:
                    dve.wait_ge(hl_ready, n - NTMP + 1)
                return tmp[:, n % NTMP, :]

            def normed(name, n, src, gain, dst, k0, tiles, bias=None):
                mean_square(name, n)
                inverse_root(name)
                for k in range(tiles + 1):
                    if k < tiles:
                        dve.scalar_tensor_tensor(slot((name, k)), src[:, k, :], gain(k), rstd[:, :], ALU.mult,
                                                 ALU.mult).then_inc(pre_split, 1)
                    if k:
                        low((name, k - 1), dst[:, 0, k0 + k - 1, :], dst[:, 1, k0 + k - 1, :], bias(k - 1) if bias else 0.0)

            def ada(n):
                wait_filled(dve, ("ada", n))
                emptied_by(dve.tensor_tensor(mod[:, n:n + 1], bank(("ada", n))[:, 0:1], vcol("b_ada", n), ALU.add), ("ada", n))

            dve.wait_ge(vec_loaded, 16)
            for n in range(16):
                ada(n)
            for n in range(KT, 2 * KT):
                wait_emptied(dve, ("ada", n))
            dve.scalar_tensor_tensor(modg[:, 0:KT], mod[:, KT:2 * KT], 1.0, vcol("g_mix", 0, KT), ALU.add,
                                     ALU.mult).then_inc(modg_ready, 1)
            dve.wait_ge(modg_ready, 1)
            normed("mix", D, x, lambda k: modg[:, k:k + 1], ah, 0, KT, lambda k: mod[:, k:k + 1])
            for m in range(16):
                ada(16 + 2 * m)
                ada(17 + 2 * m)
            wait_emptied(dve, ("ada", 39))
            dve.scalar_tensor_tensor(modg[:, KT:2 * KT], mod[:, 32:40], 1.0, vcol("g_mlp", 0, KT), ALU.add,
                                     ALU.mult).then_inc(modg_ready, 1)
            for kv, pe_name in enumerate(("pe_ck", "pe_cv")):
                wait_emptied(dve, ("z", 4 + kv))
                for g in range(G):
                    for hi in range(2):
                        src = kcd[:, kv, g, hi * CS:hi * CS + NC * CS].rearrange("p (c r) -> p r c", r=CS)[:, ::2, :]
                        pe8 = vcol(pe_name, 8 * hi, 8).unsqueeze(2).to_broadcast([P, 8, NC])
                        last = dve.tensor_tensor(bkv[:, kv, 8 * hi:8 * hi + 8, g * NC:g * NC + NC], src, pe8, ALU.add)
                        if (g, hi) != (G - 1, 1):
                            last.then_inc(dve_step, 1)
                            steps[0] += 1
                last.then_inc(bkv_ready, 1)
            normed("cq", QR, zd, lambda k: vcol("g_cq", k), cqh, 0, 3)
            normed("ckv", KVR, zd[:, 3:5, :], lambda k: vcol("g_ckv", k), cqh, 3, 2)

            def attention(tag, units, probs, st, bias, gate):
                base = {"nsa": 0, "mla": len(NSA_UNITS)}[tag]
                per_pair = 2 * TT * (3 if tag == "nsa" else 1)

                def normalize(u):
                    h, qt, br = units[u]
                    w = NC if br == 0 else qt * P + P
                    dve.wait_ge(exp_done, base + u + 1)
                    total, inv = st[:, u % 3, 1:2], st[:, u % 3, 2:3]
                    if br == 0:
                        step(dve.tensor_scalar(total, total, 1e-30, None, ALU.max))
                    step(dve.reciprocal(inv, total))
                    pr = probs[:, u % 3, 0:w]
                    if gate is None:
                        ins = dve.tensor_scalar(pr, pr, inv, None, ALU.mult)
                    else:
                        ins = dve.tensor_scalar(pr, pr, inv, gate(h, qt, br), ALU.mult, ALU.mult)
                    ins.then_inc(p_ready, 1)

                for kind, u in attention_order(units):
                    h, qt, br = units[u]
                    if kind == "S":
                        w = NC if br == 0 else qt * P + P
                        wait_filled(dve, ("S", tag, u))
                        if u >= 3:
                            wait_filled(dve, ("PT", tag, u - 3))
                        emptied_by(dve.tensor_tensor_reduce(probs[:, u % 3, 0:w], bank(("S", tag, u))[:, 0:w], bias(h, qt, br),
                                                            1.0, 1e25, ALU.add, ALU.min, st[:, u % 3, 0:1]), ("S", tag, u))
                        if u >= 1:
                            normalize(u - 1)
                        if u == len(units) - 1:
                            normalize(u)
                    elif kind == "O" and (u + 1) % per_pair == 0:
                        pair = u // per_pair + (H // 2 if tag == "mla" else 0)
                        dve.wait_ge(o_hi, pair + 1)
                        dve.tensor_tensor(oh[:, 1, pair, :], psum[:, OBANK, :], oh[:, 0, pair, :].bitcast(F32),
                                          ALU.subtract).then_inc(o_empty, 1)

            def nsa_bias(h, qt, br):
                return cmpb[:, qt, h, :] if br == 0 else alibi[:, h, S - P - qt * P:S]

            for n in ("alibi", "cmpb", "causal", "rope"):
                dve.wait_ge(const_loaded[n], 16)
            wait_emptied(dve, ("gt",))
            attention("nsa", NSA_UNITS, sm, stat, nsa_bias, lambda h, qt, br: gates[:, qt, br * H + h:br * H + h + 1])
            wait_emptied(dve, ("z", 10))
            step(dve.tensor_tensor(kcat[64:96, 0, :], zkr[64:96, :], rope[64:96, :], ALU.mult))
            step(dve.tensor_tensor(rtmp[64:96, :], zkr[96:128, :], rope[96:128, :], ALU.mult))
            step(dve.tensor_tensor(kcat[64:96, 0, :], kcat[64:96, 0, :], rtmp[64:96, :], ALU.add))
            dve.tensor_copy(kcat[64:96, 1:MH, :], kcat[64:96, 0:1, :].to_broadcast([32, MH - 1, S])).then_inc(krot_done, 1)
            for h in range(MH):
                wait_filled(dve, ("uq", h))
                q = bank(("uq", h))
                if h:
                    dve.wait_ge(rope_done, h)
                step(dve.scalar_tensor_tensor(qcat[64:96, h, :], q[64:96, :], -DQK ** -0.5, rope[64:96, :], ALU.mult, ALU.mult))
                dve.wait_ge(nope_done, h + 1)
                emptied_by(dve.scalar_tensor_tensor(rtmp[64:96, :], q[96:128, :], -DQK ** -0.5, rope[96:128, :], ALU.mult,
                                                    ALU.mult), ("uq", h))
                wait_emptied(dve, ("uq", h))
                dve.tensor_tensor(qcat[64:96, h, :], qcat[64:96, h, :], rtmp[64:96, :], ALU.add).then_inc(rope_done, 1)
            attention("mla", MLA_UNITS, sm2, stat2, lambda h, qt, br: causal[:, S - P - qt * P:S], None)
            for m in range(KT + 1):
                if m < KT:
                    wait_emptied(dve, ("gate", 8 + m))
                    wait_filled(dve, ("on", m))
                    emptied_by(dve.tensor_tensor(sg[:, m, :], bank(("on", m)), sg[:, m, :], ALU.mult), ("on", m))
                    wait_filled(dve, ("om", m))
                    emptied_by(dve.tensor_tensor(sg[:, 8 + m, :], bank(("om", m)), sg[:, 8 + m, :], ALU.mult), ("om", m))
                    wait_emptied(dve, ("on", m))
                    wait_emptied(dve, ("om", m))
                    dve.tensor_tensor(slot(("y", m)), sg[:, m, :], sg[:, 8 + m, :], ALU.add).then_inc(pre_split, 1)
                if m:
                    low(("y", m - 1), yh[:, 0, m - 1, :], yh[:, 1, m - 1, :])
            for m in range(KT):
                wait_filled(dve, ("wo", m))
                emptied_by(dve.scalar_tensor_tensor(x[:, m, :], bank(("wo", m)), mod[:, 16 + m:17 + m], x[:, m, :], ALU.mult,
                                                    ALU.add), ("wo", m))
            dve.wait_ge(modg_ready, 2)
            normed("mlp", D, x, lambda k: modg[:, KT + k:KT + k + 1], ah, 0, KT, lambda k: mod[:, 24 + k:25 + k])

            def mlp(n, gate):
                for half, c in mlp_order():
                    for m in range(KT):
                        if half == 1:
                            what = ("fc1", n, c, m)
                            wait_emptied(dve, what)
                            e = EVENT["hid", n, c, m]
                            dve.tensor_tensor(slot(("hid", n, c, m)), sq[:, e % 2, :], sq[:, e % 2, :], ALU.mult).then_inc(pre_split, 1)
                            low(("hid", n, c, m), hidden[c % 2][:, 0, m, :], hidden[c % 2][:, 1, m, :])
                        else:
                            what = ("fc2", n, c, m)
                            wait_filled(dve, what)
                            if c:
                                wait_emptied(dve, ("fc2", n, c - 1, m))
                            if gate is None:
                                emptied_by(dve.tensor_tensor(x[:, m, :], bank(what), x[:, m, :], ALU.add), what)
                            else:
                                emptied_by(dve.scalar_tensor_tensor(x[:, m, :], bank(what), gate(m), x[:, m, :], ALU.mult,
                                                                    ALU.add), what)

            mlp(1, lambda m: mod[:, 40 + m:41 + m])
            def normed_in_place(name, gain):
                mean_square(name, D)
                inverse_root(name)
                for k in range(KT):
                    dve.scalar_tensor_tensor(x[:, k, :], x[:, k, :], vcol(gain, k), rstd[:, :], ALU.mult, ALU.mult).then_inc(xn_ready, 1)

            normed_in_place("final", "g_final")

            normed("mix2", D, x, lambda k: vcol("norm_mix_g_2", k), ah, 0, KT)
            for k in range(KT):
                dve.wait_ge(hp_ready, 2 * k + 2)
                if k >= 2:
                    dve.wait_ge(xm_used, 3 * (k - 1))
                for i in range(3):
                    dve.scalar_tensor_tensor(xm(i, k), rkv[:, k % 2, :], vcol("mu_lora_2", 8 * i + k), rkvp[:, k % 2, 1:S + 1],
                                             ALU.mult, ALU.add).then_inc(xm_ready, 1)
            dve.wait_ge(const_loaded["rw"], 16)
            dve.wait_ge(x_put, 16)
            taps = [0, CONV]

            def convolve(n):
                j, done = taps
                for w in range(done, min(done + n, CONV)):
                    src, tap, acc = upad[:, w:w + S], vcol("conv_w_2", 8 * w + j), x[:, j, :]
                    if w == 0:
                        ins = dve.tensor_scalar(acc, src, tap, vcol("conv_b_2", j), ALU.mult, ALU.add)
                    else:
                        ins = dve.scalar_tensor_tensor(acc, src, tap, acc, ALU.mult, ALU.add)
                    if w < CONV - 1:
                        step(ins)
                    else:
                        ins.then_inc(conv_done, 1)
                    taps[1] += 1

            step(dve.tensor_scalar(omu[:, :], vcol("mu_rkv_2", 0, 24), -1.0, 1.0, ALU.mult, ALU.add))
            for f in rwkv_order():
                kind, j = f[0], f[1]
                if kind == "mix":
                    i = f[2]
                    n = (1, 0, 2).index(i)
                    what = ("rkv", j, i)
                    dve.wait_ge(mu_ready, 3 * j + n + 1)
                    if j:
                        dve.wait_ge(pool_f, POOL_F * j)
                        wait_emptied(dve, ("bonus", j - 1))
                        wait_filled(dve, ("tok", j - 1, 3))
                    else:
                        dve.wait_ge(xm_ready, 3 * KT)
                    emptied_by(dve.scalar_tensor_tensor(rkv[:, i, :], bank(what), omu[:, 8 * i + j:8 * i + j + 1], rkvp[:, RKV_SLOT[i], 0:S],
                                                        ALU.mult, ALU.add), what)
                elif kind == "scan":
                    wait_emptied(dve, ("lw2", j))
                    if j:
                        wait_filled(dve, ("tok", j - 1, 2))
                    for c in range(NCK):
                        cols = slice(c * CH, c * CH + CH)
                        last = dve.tensor_tensor_scan(cw[:, cols], ones[:, 0:CH], sw[:, cols], 0.0, ALU.mult, ALU.add)
                        if c < NCK - 1:
                            steps[0] += 1
                            last.then_inc(dve_step, 1)
                    last.then_inc(cw_ready, 1)
                elif kind == "kk":
                    wait_emptied(dve, ("la2", j))
                    wait_emptied(dve, ("rkv", j, 1))
                    wait_emptied(dve, ("rkv", j, 0))
                    if j:
                        dve.wait_ge(pool_f, POOL_F * (j - 1) + 4)
                        wait_filled(dve, ("bonus", j - 1))
                    dve.tensor_scalar(kk[:, :], rkv[:, 1, :], vcol("k_k_2", j), None, ALU.mult).then_inc(kk0_ready, 1)
                    step(dve.tensor_scalar(tf, rate[:, :], -1.0, vcol("k_a_2", j), ALU.add, ALU.mult))
                    dve.wait_ge(kk0_ready, j + 1)
                    dve.scalar_tensor_tensor(rkv[:, 1, :], tf, 1.0, rkv[:, 1, :], ALU.add, ALU.mult).then_inc(kmod_ready, 1)
                    dve.wait_ge(kmod_ready, j + 1)
                    dve.scalar_tensor_tensor(tf, rkv[:, 0, :], vcol("r_k_2", j), rkv[:, 1, :], ALU.mult, ALU.mult).then_inc(rk_ready, 1)
                elif kind == "nrm":
                    wait_emptied(dve, ("kkss", j))
                    step(dve.tensor_scalar(nrm[:, :], nrm[:, :], 1e-12, None, ALU.max))
                    dve.reciprocal(nrm[:, :], nrm[:, :]).then_inc(nrm_ready, 1)
                    dve.wait_ge(exp_ready, 2 * j + 2)
                    step(dve.tensor_copy(wc[:, j % 2, :], ew[:, :, CH - 1]))
                elif kind == "at":
                    dve.wait_ge(pool_f, POOL_F * j + 3)
                    if j:
                        wait_filled(dve, ("mk", j - 1, 1, 1))
                    dve.scalar_tensor_tensor(arow[:, :, 0, :].rearrange("p t (c n) -> p t c n", c=2),
                                             kk[:, :].rearrange("p (t c n) -> p t c n", t=TT, c=2), -1.0,
                                             ewp.rearrange("p (t c) n -> p t c n", t=TT), ALU.mult, ALU.mult).then_inc(at_ready, 1)
                elif kind == "bonus":
                    wait_filled(dve, f)
                    wait_emptied(dve, ("rkv", j, 2))
                    emptied_by(dve.tensor_tensor(bv[:, j % 2, :], bank(f), rkv[:, 2, :], ALU.mult), f)
                elif kind == "part" and f[1][:1] + f[1][2:] == ("glu", 0) and f[3] == KT:
                    what = f[1]
                    j = what[1]
                    convolve(CONV)
                    taps[:] = [j, 0]
                    wait_emptied(dve, ("glu", j, 1))
                    wait_filled(dve, what)
                    if j == 0:
                        dve.wait_ge(zeros_done, 3)
                    else:
                        dve.wait_ge(conv_done, j)
                    emptied_by(dve.tensor_tensor(upad[:, CONV - 1:], bank(what), usig, ALU.mult), what)
                    wait_emptied(dve, what)
                elif kind == "conv":
                    convolve(f[2])
                elif kind == "iy0" and f[2] == 0:
                    wait_emptied(dve, ("mb", j, 0, 0))
                    wait_emptied(dve, ("mb", j, 0, 1))
                    if j:
                        wait_filled(dve, ("tav", j - 1, 0))
                    step(dve.tensor_tensor(iy[0], mb[0][:, :, 0:P], level[0].unsqueeze(1).to_broadcast([P, TT, P]), ALU.mult))
                    dve.tensor_tensor(iy[0], iy[0], eye.unsqueeze(1).to_broadcast([P, TT, P]), ALU.add).then_inc(iy0_done[0], 1)
                elif kind in ("mb", "mk"):
                    wait_filled(dve, f)
                    if j:
                        dve.wait_ge(opa_done if kind == "mb" else opv_done, 2 * j - 1 + f[2])
                    dst = (mb if kind == "mb" else mk)[f[2]][:, 2 * f[3]:2 * f[3] + 2, :]
                    emptied_by(dve.tensor_tensor(dst, bank(f).rearrange("p (t n) -> p t n", t=2),
                                                 strict_incl.unsqueeze(1).to_broadcast([P, 2, 2 * P]), ALU.mult), f)
                elif kind == "ip":
                    wait_filled(dve, f)
                    emptied_by(dve.tensor_tensor(ip[f[2]], bank(f).rearrange("p (t n) -> p t n", t=TT),
                                                 level[f[3]].unsqueeze(1).to_broadcast([P, TT, P]), ALU.mult), f)
                elif kind == "iy":
                    wait_filled(dve, f)
                    if f[3] == 1:
                        dve.wait_ge(iy0_done[f[2]], j + 1)
                    else:
                        wait_emptied(dve, ("iy", j, f[2], f[3] - 1))
                    emptied_by(dve.tensor_tensor(iy[f[2]], bank(f).rearrange("p (t n) -> p t n", t=TT), iy[f[2]], ALU.add), f)
                elif kind == "rr":
                    hh = f[2]
                    rows = slice(RN * hh, RN * hh + RN)
                    wait_filled(dve, f)
                    dve.wait_ge(pool_f, POOL_F * j + 7)
                    if j:
                        dve.wait_ge(ost_done, j)
                    emptied_by(dve.tensor_tensor(rp[rows, :].rearrange("p (t n) -> p t n", t=TT),
                                                 bank(f)[rows, :].rearrange("p (t n) -> p t n", t=TT), arow[rows, :, 1, :], ALU.add), f)
                elif kind == "pt":
                    wait_filled(dve, f)
                    emptied_by(dve.tensor_tensor(pts[:, f[2]::2, :], bank(f).rearrange("p (c n) -> p c n", c=4),
                                                 heads.unsqueeze(1).to_broadcast([P, 4, P]), ALU.mult), f)
                elif kind == "st":
                    c = f[2]
                    if c == 1:
                        wait_emptied(dve, ("qq", j, 0))
                        wait_emptied(dve, ("qq", j, 1))
                        if j:
                            dve.wait_ge(ost_done, j)
                    dve.scalar_tensor_tensor(su[:, :], state(c), wc[:, j % 2, c:c + 1], qs[:, c, :], ALU.mult, ALU.add).then_inc(u_ready, 1)
                    dve.wait_ge(u_ready, (NCK - 2) * j + c)
                    wait_filled(dve, f)
                    emptied_by(dve.tensor_tensor(st[:, c + 1, :], bank(f)[:, 0:RN], su[:, :], ALU.add), f)
                    wait_emptied(dve, f)
                elif kind == "gnm":
                    wait_filled(dve, f)
                    emptied_by(dve.scalar_tensor_tensor(og, bank(f), -1.0 / RN, og, ALU.mult, ALU.add), f)
                elif kind == "gnv":
                    wait_filled(dve, f)
                    emptied_by(dve.tensor_scalar(rstd[:, :], bank(f), 1.0 / RN, GN_EPS, ALU.mult, ALU.add), f)
                elif kind == "gnend":
                    dve.wait_ge(gnroot_done, j + 1)
                    step(dve.reciprocal(rstd[:, :], rstd[:, :]))
                    step(dve.scalar_tensor_tensor(og, og, vcol("ln_x_g_2", j), rstd[:, :], ALU.mult, ALU.mult))
                    step(dve.scalar_tensor_tensor(og, og, vcol("ln_x_b_2", j), bv[:, j % 2, :], ALU.add, ALU.add))
                    if j >= 2:
                        dve.wait_ge(ao_put[j % 2], 16 * (j // 2))
                    dve.tensor_tensor(ao[:, j % 2, :], og, gate[:, j % 2, :], ALU.mult).then_inc(ao_done, 1)
            convolve(CONV)
            for k in range(KT):
                dve.wait_ge(ao_hi, k + 1)
                dve.tensor_tensor(aoh[:, 1, k, :], aof[:, k, :], aoh[:, 0, k, :].bitcast(F32), ALU.subtract).then_inc(ao_ready, 1)
            wait_filled(dve, ("convmean",))
            for k in range(KT):
                if k == KT - 1:
                    dve.wait_ge(conv_done, KT)
                ins = dve.scalar_tensor_tensor(x[:, k, :], bank(("convmean",)), -1.0 / D, x[:, k, :], ALU.mult, ALU.add)
                if k < KT - 1:
                    ins.then_inc(cen_ready, 1)
                else:
                    emptied_by(ins, ("convmean",))
            mean_square("conv", D, LN_EPS)
            inverse_root("conv")
            for k in range(KT + 1):
                if k < KT:
                    dve.scalar_tensor_tensor(x[:, k, :], x[:, k, :], vcol("conv_ln_g_2", k), rstd[:, :], ALU.mult,
                                             ALU.mult).then_inc(convn_ready, 1)
                if k:
                    low(("conv", k - 1), coh[:, 0, k - 1, :], coh[:, 1, k - 1, :])
            for m in range(KT + 1):
                if m < KT:
                    wait_emptied(dve, ("gate2", 8 + m))
                    wait_filled(dve, ("pr", m))
                    emptied_by(dve.tensor_tensor(sg2[:, m, :], bank(("pr", m)), sg2[:, m, :], ALU.mult), ("pr", m))
                    wait_filled(dve, ("pc", m))
                    emptied_by(dve.tensor_tensor(sg2[:, 8 + m, :], bank(("pc", m)), sg2[:, 8 + m, :], ALU.mult), ("pc", m))
                    wait_emptied(dve, ("pr", m))
                    wait_emptied(dve, ("pc", m))
                    dve.tensor_tensor(slot(("y2", m)), sg2[:, m, :], sg2[:, 8 + m, :], ALU.add).then_inc(pre_split, 1)
                if m:
                    low(("y2", m - 1), ah[:, 0, m - 1, :], ah[:, 1, m - 1, :])
            dve.wait_ge(x_back, 16)
            for m in range(KT):
                wait_filled(dve, ("wo2", m))
                emptied_by(dve.tensor_tensor(x[:, m, :], bank(("wo2", m)), x[:, m, :], ALU.add), ("wo2", m))
            normed("ff2", D, x, lambda k: vcol("norm_ff_g_2", k), ah, 0, KT)
            mlp(2, None)
            normed_in_place("final2", "norm_final_g_2")


def tiles_of(w):
    k, n = w.shape
    return w.reshape(k // P, P, n).transpose(1, 0, 2).reshape(P, -1)


def columns_of(v):
    return v.reshape(-1, P).T


def padded(a, n=D):
    return a if a.shape[1] == n else np.concatenate([a, np.zeros((P, n - a.shape[1]), a.dtype)], 1)


def block_of(what, w):
    kind = what[0]
    w_in = w["w_in"]
    if kind == "ada":
        return tiles_of(w["w_ada"][:, what[1] * P:what[1] * P + P])
    if kind == "z":
        m = what[1]
        if m < 10:
            return tiles_of(w_in[:, m * P:m * P + P])
        if m == 10:
            zero = np.zeros((D, 40), w_in.dtype)
            return tiles_of(np.concatenate([w_in[:, 1280:1304], zero, w_in[:, 1944:1976], w_in[:, 1960:1976],
                                            w_in[:, 1944:1960]], 1))
        return tiles_of(w_in[:, 1304 + (m - 11) * P:1304 + (m - 10) * P])
    if kind == "ck":
        src = w["w_ck1"] if what[1] == 0 else w["w_cv1"]
        return tiles_of(src[what[2] * S:what[2] * S + S])
    if kind == "uq":
        parts = []
        for h in (2 * what[1], 2 * what[1] + 1):
            q = w["w_uq"][:, h * DQK:h * DQK + DQK]
            parts.append(tiles_of(np.concatenate([q, q[:, NOPE + 16:], q[:, NOPE:NOPE + 16]], 1)))
        return padded(np.concatenate(parts, 1))
    if kind == "uk":
        return np.concatenate([tiles_of(w["w_uk"][:, i * P:i * P + P]) for i in range(MH // 2)], 1)
    if kind == "uv":
        return tiles_of(w["w_uv"])
    if kind == "gate":
        return tiles_of(w_in[:, 1976 + what[1] * P:1976 + what[1] * P + P])
    if kind == "nm":
        cols = slice(what[1] * P, what[1] * P + P)
        return np.concatenate([tiles_of(w["w_o_nsa"][:, cols]), tiles_of(w["w_o_mla"][:, cols])], 1)
    if kind == "wo":
        return tiles_of(w["w_out"][:, what[1] * P:what[1] * P + P])
    w2 = w["w_in_2"]
    if kind == "lora":
        return tiles_of(np.concatenate([w["decay_w1_2"], w["aaa_a1_2"]], 1) if what[1] == 0 else w["gate_g1_2"])
    if kind in ("rkv", "glu"):
        c0 = (0 if kind == "rkv" else 3 * D) + what[2] * D + what[1] * P
        return tiles_of(w2[:, c0:c0 + P])
    if kind == "gate2":
        return tiles_of(w2[:, 5 * D + what[1] * P:5 * D + what[1] * P + P])
    if kind in ("pr", "pc", "wo2"):
        src = w[{"pr": "w_rwkv_proj_2", "pc": "w_conv_proj_2", "wo2": "w_out_2"}[kind]]
        return tiles_of(src[:, what[1] * P:what[1] * P + P])
    _, n, c, m = what
    up, down = (w["w_fc1"], w["w_fc2"]) if n == 1 else (w["w_ff1_2"], w["w_ff2_2"])
    if kind == "fc1":
        return tiles_of(up[:, (c * KT + m) * P:(c * KT + m + 1) * P])
    return tiles_of(down[c * D:c * D + D, m * P:m * P + P])


def kernel(**inputs):
    import concourse.bacc as bacc
    from concourse.bass_utils import run_bass_kernel_spmd

    w = {n: np.asarray(a) for n, a in inputs.items()}
    w = {n: a[0] if a.ndim > 1 and a.shape[0] == 1 else a for n, a in w.items()}
    vecs = []
    for name in VEC:
        if name in ("pe_ck", "pe_cv"):
            vecs.append(w[name].reshape(LP, P).T)
        elif name == "w_ck2":
            vecs.append(tiles_of(np.concatenate([w[name], w[name]], 1)))
        elif name == "w_cv2":
            vecs.append(tiles_of(w[name]))
        elif name in ("mu_lora_2", "conv_w_2", "r_k_2"):
            vecs.append(columns_of(w[name].reshape(-1)))
        else:
            vecs.append(columns_of(w[name]))
    arrays = {
        "x": np.ascontiguousarray(tiles_of(w["x"].T)),
        "vec": np.ascontiguousarray(np.concatenate(vecs, 1)),
        "w": np.stack([block_of(what, w) for _, what in BLOCKS]),
    }
    both = np.concatenate([w["decay_w2_2"], w["aaa_a2_2"]], 0)
    arrays["lw"] = np.stack([np.concatenate([both[:, j * P:j * P + P], w["gate_g2_2"][:, j * P:j * P + P]], 1) for j in range(KT)])
    arrays.update({n: np.ascontiguousarray(a) for n, a in block1_constants().items()})
    arrays["rw"] = rwkv_constants()
    nc = bacc.Bacc("TRN2", target_bir_lowering=False, num_devices=1)
    io = {n: nc.dram_tensor(f"in_{n}", a.shape, F32, kind="ExternalInput").ap() for n, a in arrays.items()}
    io["out"] = nc.dram_tensor("out", (P, KT * S), F32, kind="ExternalOutput").ap()
    build_program(nc, io)
    r = run_bass_kernel_spmd(nc, [{f"in_{n}": a for n, a in arrays.items()}], core_ids=[0])
    got = np.asarray(r.results[0]["out"])
    return np.ascontiguousarray(got.reshape(P, KT, S).transpose(2, 1, 0).reshape(1, S, D))
```

```python
from contextlib import ExitStack

import numpy as np
import concourse.bass as bass
from concourse import mybir

F32 = mybir.dt.float32
F32R = mybir.dt.float32r
ACT = mybir.ActivationFunctionType
ALU = mybir.AluOpType

P = 128
S = 512
D = 1024
KT = D // P
TT = S // P
DFF = 4 * D
NCH = DFF // D
H, G, DH = 8, 2, 64
HG = H // G
CL, CS, CHID = 32, 16, 256
NC = S // CS - CL // CS + 1
LP = CL * DH // P
MH, NOPE, ROPE, MV = 8, 64, 32, 64
DQK = NOPE + ROPE
QR, KVR = 384, 256
EPS = 1e-6
BIG = 1e30
SLOPES = [2.0 ** (-8.0 * h / H) for h in range(1, H + 1)]
RH, RN = 16, 64
CH = 64
NCK = S // CH
LEVELS = 5
CONV = 31
LORA = 64
LN_EPS, GN_EPS = 1e-5, 64e-5
DECAY = float(np.exp(np.float32(-0.5)))

NBANK = 7
OBANK = 7
NRAW, NHL = 4, 2
EARLY = 3


def vec_columns():
    names = [("c", 8), ("b_ada", 48), ("g_mix", 8), ("g_cq", 3), ("g_ckv", 2), ("g_mlp", 8), ("g_final", 8),
             ("pe_ck", LP), ("pe_cv", LP), ("w_ck2", 256), ("w_cv2", 128), ("norm_mix_g_2", 8), ("b_gate_2", 16), ("mu_rkv_2", 24),
             ("mu_lora_2", 24), ("decay_w0_2", 8), ("aaa_a0_2", 8), ("k_k_2", 8), ("k_a_2", 8), ("r_k_2", 8), ("ln_x_g_2", 8),
             ("ln_x_b_2", 8), ("conv_w_2", CONV * 8), ("conv_b_2", 8), ("conv_ln_g_2", 8), ("conv_ln_b_2", 8),
             ("norm_ff_g_2", 8), ("norm_final_g_2", 8)]
    at, n = {}, 0
    for name, w in names:
        at[name] = n
        n += w
    return at, n


VEC, NVEC = vec_columns()


FRONT = [("z", 4), ("z", 5), ("z", 11), ("bkv", 0), ("z", 12), ("bkv", 1), ("ck", 0, 0), ("z", 13), ("ck", 0, 1), ("z", 14), ("ck", 0, 2),
         ("z", 15), ("ck", 0, 3), ("z", 10), ("ss", "cq"), ("ck", 1, 0), ("z", 7), ("ck", 1, 1), ("z", 9), ("norm", "cq"), ("ck", 1, 2),
         ("z", 6), ("ck", 1, 3), ("kc",), ("gt",), ("z", 8), ("ss", "ckv"), ("vt", 0), ("vt", 1), ("ada", 2), ("vc",), ("z", 0),
         ("norm", "ckv"), ("z", 1), ("z", 2), ("z", 3), ("ada", 3)]
CK_PARTS = LP // 4
Z_ORDER = [f for f in FRONT if f[0] == "z"]


def ada_beside(f):
    n = Z_ORDER.index(f)
    return "ada", 2 + n // KT, n % KT


def weight_blocks():
    out = [("raw", ("ada", s, k)) for s in range(2) for k in range(KT)]
    for f in FRONT:
        if f[0] == "z":
            out += [("split", f), ("raw", ada_beside(f))]
        elif f[0] == "ck":
            out.append(("raw", f))
    out += [("split", ("uq", i)) for i in range(MH // 2)] + [("split", ("uk",)), ("split", ("uv",))]
    for m in range(16):
        out += [("split", ("gate", m)), ("raw", ("ada", 4 + m // KT, m % KT))]
    out += [("split", ("nm", m)) for m in range(KT)]
    out += [("split", ("wo", m)) for m in range(KT)]
    out += mlp_blocks(1)
    out += [("split", f[1]) for f in rwkv_order() if f[0] == "part" and f[2] == 0]
    out += [("split", (n, m)) for n in ("pr", "pc") for m in range(KT)]
    out += [("split", ("wo2", m)) for m in range(KT)]
    return out + mlp_blocks(2)


def mlp_order():
    order = [(1, 0)]
    for c in range(1, NCH):
        order += [(1, c), (2, c - 1)]
    return order + [(2, NCH - 1)]


def mlp_blocks(n):
    return [("split", (f"fc{half}", n, c, m)) for half, c in mlp_order() for m in range(KT)]


def parts(what, n):
    return [("part", what, KT * i // n, KT * (i + 1) // n) for i in range(n)]


def tile_ahead(j):
    k, r, v, g = (parts(what, 4) for what in (("rkv", j, 1), ("rkv", j, 0), ("rkv", j, 2), ("glu", j, 1)))
    return (k + [("lw2", j)] + r[:2] + [("mix", j, 1), ("scan", j)] + r[2:] + [("la2", j)] + v[:2] + [("mix", j, 0), ("kk", j)]
            + v[2:3] + [("lg2", j)] + v[3:] + [("kkss", j)] + g[:1] + [("mix", j, 2)] + g[1:2] + [("kkb", j)] + g[2:3] + [("bonus", j)]
            + g[3:] + [("at", j)])


def first_tile():
    v, g1, g0 = (parts(what, 1) for what in (("rkv", 0, 2), ("glu", 0, 1), ("glu", 0, 0)))
    k, r = parts(("rkv", 0, 1), KT), parts(("rkv", 0, 0), KT)
    normed = [("norm2", i) for i in range(KT)]
    last0, own0, last1, own1 = (parts(("lora", i, half), 1) for i in range(2) for half in (1, 0))
    return ([("scale", 0, 1)] + k[:-1] + r[:1] + k[-1:] + r[1:4] + [("factor", 1)] + normed[:2] + [("mix", 0, 1)] + normed[2:5] + r[4:]
            + normed[5:] + [("factor", 0), ("mix", 0, 0), ("scale", 0, 0)] + last0 + [("scale", 1, 1)] + own0
            + [("xn", 0), ("scale", 1, 0), ("hidden", 0)] + last1 + [("xput", 0)] + [("lw2", 0), ("la2", 0)] + own1 + [("scan", 0), ("hidden", 1), ("kk", 0)]
            + v + [("lg2", 0), ("kkss", 0), ("mix", 0, 2)] + g1 + [("kkb", 0)] + g0 + [("bonus", 0), ("at", 0), ("re", 0)])


def rwkv_order():
    out = first_tile()
    for j in range(KT):
        ahead = tile_ahead(j + 1) if j + 1 < KT else [f for m in range(GATES_IN) for f in parts(("gate2", m), 4)]
        last = parts(("glu", j + 1, 0), KT) if j + 1 < KT else []

        def slot(taps):
            got = [ahead.pop(0)] if ahead else []
            while ahead and ahead[0][0] != "part":
                got.append(ahead.pop(0))
            return got + [("conv", j, taps)]

        out += [("tok", j, 0), ("mb", j, 0), ("tok", j, 1), ("mb", j, 1), ("iy0", j, 0), ("iy0", j, 1)]
        if j:
            out.append(("gnm", j - 1))
        out += [("tok", j, 2), ("tok", j, 3), ("mk", j, 0), ("mk", j, 1), ("inv", j, 0, 0)]
        if j:
            out.append(("gnv", j - 1))
        out += [("akv", j, 0), ("akv", j, 1), ("inv", j, 1, 0), ("opv", j, 0), ("opv", j, 1)]
        for lv in range(1, LEVELS + 1):
            out += [("ip", j, 0, lv), ("ip", j, 1, lv)]
            if lv == 1 and j:
                out += [("gnb", j - 1), ("gnend", j - 1)]
            out += slot(2)
            out += [("iy", j, 0, lv), ("iy", j, 1, lv)] + slot(2)
            if lv == 2 and j:
                out.append(("aoput", j - 1))
            if lv < LEVELS:
                out += [("inv", j, 0, lv), ("inv", j, 1, lv)] + slot(2)
        out += [("tav", j, 0), ("tav", j, 1)] + slot(1) + [("rr", j, 0), ("rr", j, 1)] + slot(1)
        out += [("opa", j, 0), ("opa", j, 1)] + last[:1] + [("pt", j, 0), ("pt", j, 1)] + last[1:2] + [("qq", j, 0), ("qq", j, 1)]
        out += ahead + ([("re", j + 1)] if j + 1 < KT else [])
        for c in range(1, NCK - 1):
            out += [("st", j, c)] + last[1 + c:2 + c]
        out.append(("ost", j))
    gates = [f for m in range(GATES_IN, 16) for f in parts(("gate2", m), 1)]
    behind = [[("gnm", KT - 1)], [("gnv", KT - 1)], [("gnb", KT - 1), ("gnend", KT - 1)], [("aoput", KT - 1)], [("aoload", KT - 1)], []]
    behind += [[("aosplit", k), ("aosplit", k + 1)] for k in range(0, KT, 2)]
    for m, f in enumerate(gates):
        out += [f] + (behind[m] if m < len(behind) else [])
    return out


GATES_IN = 5
POOL_F = 6
KK_EPS = 1e-12
RKV_SLOT = {1: 0, 0: 1, 2: 0}
IN_BANKS = ("lw2", "la2", "lg2", "kkss", "bonus", "tok", "mb", "mk", "inv", "akv", "ip", "iy", "tav", "rr", "pt", "qq", "st", "gnm", "gnv", "kkb", "gnb")

BLOCKS = weight_blocks()
BLOCK_AT = {what: b for b, (_, what) in enumerate(BLOCKS)}
SPLIT_AT = {}
for _b, (_kind, _what) in enumerate(BLOCKS):
    if _kind == "split":
        SPLIT_AT[_what] = len(SPLIT_AT)
SPLITS = list(SPLIT_AT)


NSA_UNITS = [(h, qt, br) for h in range(H) for qt in range(TT) for br in range(3)]
MLA_UNITS = [(h, qt, None) for h in range(MH) for qt in range(TT)]
UNITS = {"nsa": NSA_UNITS, "mla": MLA_UNITS}
LAGS = {"nsa": (3, 5), "mla": (3, 5)}
PROBS = {tag: lag_t + 1 for tag, (lag_t, _) in LAGS.items()}
TURNED = {tag: lag_o - lag_t + 1 for tag, (lag_t, lag_o) in LAGS.items()}


def attention_order(tag):
    units, (lag_t, lag_o) = UNITS[tag], LAGS[tag]
    for i in range(len(units) + lag_o):
        if i < len(units):
            yield "S", i
        if 0 <= i - lag_t < len(units):
            yield "PT", i - lag_t
        if i >= lag_o:
            yield "O", i - lag_o


def bank_order():
    out = [("ss", "mix"), ("ada", 0), ("rb", "mix"), ("ada", 1)]
    for f in FRONT:
        if f[0] == "ck":
            if f[2] == CK_PARTS - 1:
                out += [("ckh", f[1], ht) for ht in range(2)]
        elif f[0] != "bkv":
            out.append(("rb", f[1]) if f[0] == "norm" else f)
    out += [(k, "nsa", u) for k, u in attention_order("nsa") if k != "O"]
    out += [("uq", h) for h in range(MH)] + [("uk", i) for i in range(MH // 2)] + [("uv", t) for t in range(TT)]
    out += [(k, "mla", u) for k, u in attention_order("mla") if k != "O"]
    out += [("gate", m) for m in range(9)] + [("ada", 4)] + [("gate", m) for m in range(9, 16)]
    for m in range(KT):
        out += [("on", m), ("om", m)] + ([("ada", 5)] if m == 0 else [])
    out += [("wo", m) for m in range(KT)]
    out += [("ss", "mlp"), ("rb", "mlp")] + [(f"fc{half}", 1, c, m) for half, c in mlp_order() for m in range(KT)]
    out += [("ss", "final"), ("ss", "mix2")]
    for f in rwkv_order():
        if f[0] == "part" and f[3] == KT:
            if f[1] == ("rkv", 0, 0):
                out += [("rb", "mix2"), ("rb", "final")]
            out.append(f[1])
        elif f[0] in IN_BANKS:
            out.append(f)
    pr = [("pr", m) for m in range(KT)]
    out += [("convmean",)] + pr[:2] + [("ss", "conv"), pr[2], ("rb", "conv")] + pr[3:] + [("pc", m) for m in range(KT)]
    out += [("wo2", m) for m in range(KT)]
    second = [(f"fc{half}", 2, c, m) for half, c in mlp_order() for m in range(KT)]
    out += [("ss", "ff2"), second[0], ("rb", "ff2")] + second[1:]
    return out + [("ss", "final2"), ("rb", "final2")]


BANK_ORDER = bank_order()
FILL = {name: n for n, name in enumerate(BANK_ORDER)}


def bank_places():
    bank, turn, used, at = {}, {}, [0] * NBANK, [0] * 4
    inside = set(f[1] if f[0] == "part" else f for f in rwkv_order())
    inside |= {(k, name) for k in ("ss", "rb") for name in ("final", "mix2")}
    for name in BANK_ORDER:
        if name[0] in ("S", "PT", "uq", "uk", "uv", "gate") or name == ("ada", 4):
            kind, base, n = 3, 0, NBANK - 1
        elif name not in inside:
            kind, base, n = 0, 0, NBANK
        elif name[0] in ("rkv", "glu", "gate2", "lora"):
            kind, base, n = 1, NBANK - 2, 2
        else:
            kind, base, n = 2, 0, NBANK - 2
        b = base + at[kind] % n
        at[kind] += 1
        bank[name], turn[name] = b, used[b]
        used[b] += 1
    return bank, turn


BANK, TURN = bank_places()
LAST_BESIDE = [name for name in BANK_ORDER[:FILL["S", "nsa", 0]] if BANK[name] == NBANK - 1][-1]


def obank(pair):
    return OBANK - pair % 2


BLOCK_LAST = {}
for _what in SPLITS:
    BLOCK_LAST[_what] = FILL[{"uq": lambda w: ("uq", 2 * w[1] + 1), "uk": lambda w: ("uk", MH // 2 - 1),
                              "uv": lambda w: ("uv", TT - 1), "nm": lambda w: ("om", w[1])}.get(_what[0], lambda w: w)(_what)]

NORMS = [("mix", KT), ("cq", 3), ("ckv", 2), ("mlp", KT), ("final", KT), ("mix2", KT), ("conv", KT), ("ff2", KT),
         ("final2", KT)]
SQ_AT = {}
for _name, _n in NORMS:
    for _k in range(_n if _name != "mix2" else 0):
        SQ_AT[_name, _k] = len(SQ_AT)
        if _name == "final":
            SQ_AT["mix2", _k] = len(SQ_AT)

SUM_OF = {"mlp": 0, "final": 0, "mix2": 1, "conv": 0, "ff2": 1, "final2": 0}
ADD_AT = {e: n for n, e in enumerate(e for e in SQ_AT if e[0] in SUM_OF and e[1])}
SQ_SLOTS = [e for e in SQ_AT if e[0] not in SUM_OF or e[1]]
SQ_SLOT = {e: n for n, e in enumerate(SQ_SLOTS)}

def split_order():
    out = [("mix", k) for k in range(KT)] + [("cq", k) for k in range(3)] + [("ckv", k) for k in range(2)]
    out += [("y", m) for m in range(KT)] + [("mlp", k) for k in range(KT)]
    out += [("hid", 1, c, m) for c in range(NCH) for m in range(KT)]
    out += [("early2", k) for k in range(KT)] + [("mix2", k) for k in range(KT)] + [("conv", k) for k in range(KT)]
    out += [("y2", m) for m in range(KT)] + [("early", k) for k in range(KT)] + [("ff2", k) for k in range(KT)]
    return out + [("hid", 2, c, m) for c in range(NCH) for m in range(KT)]


SPLIT_EVENTS = split_order()
EVENT = {name: n for n, name in enumerate(SPLIT_EVENTS)}
NTMP = 3
ADA_AT = {what: n for n, what in enumerate(what for _, what in BLOCKS if what[0] == "ada")}


def block1_constants():
    f = np.float32
    i = np.arange(P)[:, None]
    off = np.arange(S)[None, :] - (S - P)
    dist = (i - off).astype(f)
    seen = off <= i
    alibi = np.where(seen, dist, f(BIG)).astype(f)
    t = np.arange(S).reshape(TT, P).T[:, :, None]
    dc = (t - (np.arange(NC) * CS + CL - 1)).astype(f)
    cmpb = np.where(dc >= 0, dc, f(BIG)).astype(f)
    over = np.array([-DH ** -0.5 / SLOPES[2 * m + p // DH] for p in range(P) for m in range(H // 2)], f).reshape(P, H // 2)
    causal = np.where(seen, f(0), f(BIG)).astype(f)
    half = ROPE // 2
    inv = (f(10000.0) ** (-np.arange(half, dtype=f) / f(half))).astype(f)
    ang = (np.arange(S, dtype=f)[:, None] * inv[None, :]).astype(f)
    cos, sin = np.cos(ang).T.astype(f), np.sin(ang).T.astype(f)
    rope = np.zeros((P, S), f)
    rope[64:96] = np.concatenate([cos, cos])
    rope[96:128] = np.concatenate([-sin, sin])
    return {"eye_ones": np.concatenate([np.eye(P, dtype=f), np.ones((P, P), f), over], 1), "alibi": alibi,
            "cmpb": cmpb.reshape(P, TT * NC), "causal": causal, "rope": rope}


def rwkv_constants():
    i, t = np.arange(P)[:, None], np.arange(P)[None, :]
    same = i // CH == t // CH
    own = lambda m: np.where(i < CH, m[:, :CH], m[:, CH:])
    out = [own(i < t), same & (i <= t)]
    for lv in range(LEVELS + 1):
        b = 1 << lv
        joins = (i // (2 * b) == t // (2 * b)) & (i // b % 2 == 0) & (t // b % 2 == 1)
        out.append(own(joins if lv == 0 else joins.T))
    out.append(own(i == t))
    out.append(i // RN == t // RN)
    return np.concatenate(out, 1).astype(np.float32)


CONSTS = {"rw": (1 + LEVELS + 1 + 1) * CH + 2 * P, "eye_ones": 2 * P + H // 2, "alibi": S, "cmpb": TT * NC, "causal": S, "rope": S}


def build_program(nc, io):
    x_in, vec_in, w_in, out = io["x"], io["vec"], io["w"], io["out"]
    ctx = ExitStack()
    with ctx:
        def sb(name, shape, dt=F32, at=ctx):
            return at.enter_context(nc.sbuf_tensor(name, shape, dt))

        def sem(name):
            return ctx.enter_context(nc.semaphore(name))

        x = sb("x", [P, KT, S])
        vec = sb("vec", [P, NVEC])
        eye_ones = sb("eye_ones", [P, 2 * P + H // 2])
        eye, ones = eye_ones[:, 0:P], eye_ones[:, P:2 * P]
        over_slope = eye_ones[:, 2 * P:]
        raw = sb("raw", [P, NRAW, D])
        whi = sb("whi", [P, NHL, D], F32R)
        wlo = sb("wlo", [P, NHL, D], F32R)
        ah = sb("ah", [P, 2, KT, S], F32R)
        tmp = sb("tmp", [P, NTMP, S])
        sq = sb("sq", [P, 2, S])
        sq_sum = sb("sq_sum", [P, 2, S])
        rs = sb("rs", [P, 2 * TT + len(NORMS) + KT])
        mod = sb("mod", [P, 48])
        modg = sb("modg", [P, 2 * KT])
        psum = ctx.enter_context(nc.psum_tensor("psum", [P, 8, S], F32))

        mixer = ExitStack()
        oh = sb("oh", [P, 2, KT, S], F32R, mixer)
        with ExitStack() as at:
            cqh = sb("cqh", [P, 2, 5, S], F32R, at)
            zkr = sb("zkr", [P, S], F32, at)
            rope = sb("rope", [P, S], F32, at)
            causal = sb("causal", [P, S], F32, at)
            with ExitStack() as nsa:
                qT = sb("qT", [P, H // 2, S], F32, nsa)
                ksd = sb("ksd", [P, G, S], F32, nsa)
                kwd = sb("kwd", [P, G, S], F32, nsa)
                vtok = sb("vtok", [P, 2, TT, P], F32, nsa)
                kcT = sb("kcT", [P, G * NC], F32, nsa)
                vc = sb("vc", [P, G * DH], F32, nsa)
                gates = sb("gates", [P, TT, 32], F32, nsa)
                alibi = sb("alibi", [P, S], F32, nsa)
                cmpb = sb("cmpb", [P, TT, NC], F32, nsa)
                sm = sb("sm", [P, PROBS["nsa"], S], F32, nsa)
                pt = sb("pt", [P, TURNED["nsa"], S], F32, nsa)
                gT = zkr[0:32, :]
                stat = sb("stat", [P, PROBS["nsa"], 4], F32, nsa)
            with ExitStack() as mla:
                qcat = sb("qcat", [P, MH, S], F32, mla)
                kcat = sb("kcat", [P, MH, S], F32, mla)
                vm = sb("vm", [P, TT, MH * MV], F32, mla)
                sm2 = sb("sm2", [P, PROBS["mla"], S], F32, mla)
                rtmp = sq_sum[:, 0, :]
                stat2 = sb("stat2", [P, PROBS["mla"], 4], F32, mla)
        turned_nsa = [pt[:, i, :] for i in range(TURNED["nsa"])]
        turned_mla = [sq_sum[:, 0, :], sq_sum[:, 1, :], sq[:, 0, :]]
        with ExitStack() as at:
            yh = sb("yh", [P, 2, KT, S], F32R, at)
            sg = sb("sg", [P, 16, S], F32, at)
        mixer.close()
        with ExitStack() as at:
            kcd = sb("kcd", [P, 2, G, S], F32, at)
            bkv = sb("bkv", [P, 2, LP, G * NC], F32, at)
            hid = sb("hid", [P, 2, 2, G * NC], F32, at)
            vT = sb("vT", [P, 2, S], F32, at)
            zd = sb("zd", [P, 5, S], F32, at)
        with ExitStack() as at:
            taken = [0]

            def work(name, cols):
                taken[0] += cols
                return sb(name, [P, cols], F32, at)

            def both(name, cols):
                return [work(f"{name}{hh}", cols)[:, :].rearrange("p (t n) -> p t n", t=TT) for hh in range(2)]

            rw = work("rw", CONSTS["rw"])
            rkvp = work("rkvp", 2 * (S + 1))[:, :].rearrange("p (i s) -> p i s", i=2)
            rkv = work("rkv", 3 * S)[:, :].rearrange("p (i s) -> p i s", i=3)
            omu = work("omu", 48)
            lh = work("lh", 2 * S)[:, :].rearrange("p (i s) -> p i s", i=2)
            lwt = work("lwt", 4 * P)[:, :].rearrange("p (i n) -> p i n", i=2)
            arow = work("arow", 2 * S)[:, :].rearrange("p (t a n) -> p t a n", t=TT, a=2)
            bh, kh = work("bh", S), work("kh", S)
            ewall = work("ewall", NCK * (CH + 1))[:, :].rearrange("p (c n) -> p c n", c=NCK)
            ew, ewp = ewall[:, :, 1:], ewall[:, :, 0:CH]
            ewi = work("ewi", S)
            sw, cw, rate, kk = (work(n, S) for n in ("sw", "cw", "rate", "kk"))
            nrt, gnt = work("nrt", 2 * TT), work("gnt", 2 * TT)
            bv = work("bv", 2 * S)[:, :].rearrange("p (i s) -> p i s", i=2)
            gate = work("gate", 2 * S)[:, :].rearrange("p (i s) -> p i s", i=2)
            wc = work("wc", 2 * NCK)[:, :].rearrange("p (i c) -> p i c", i=2)
            ao = work("ao", 2 * S)[:, :].rearrange("p (k s) -> p k s", k=2)
            assert taken[0] <= 4 * KT * S
            ma, mr = both("ma", TT * CH), both("mr", TT * P)
            ka, kr = both("ka", TT * CH), both("kr", TT * P)
            ix, iy, ip = both("ix", TT * P), both("iy", TT * P), both("ip", TT * CH)
            iy2 = [m.rearrange("p t (c n) -> p t c n", c=2) for m in iy]
            ftok = work("ftok", 2 * S)[:, :].rearrange("p (t h a n) -> p t h a n", t=TT, h=2, a=2)
            tav = work("tav", 2 * S)[:, :].rearrange("p (t a h n) -> p t a h n", t=TT, a=2, h=2)
            btok, ktok, vtk = (work(n, S)[:, :].rearrange("p (t n) -> p t n", t=TT) for n in ("btok", "ktok", "vtk"))
            rp = work("rp", S)
            pts = work("pts", NCK * RN)[:, :].rearrange("p (c n) -> p c n", c=NCK)
            qs = work("qs", NCK * RN)[:, :].rearrange("p (c n) -> p c n", c=NCK)
            st = work("st", NCK * RN)[:, :].rearrange("p (c n) -> p c n", c=NCK)
            if taken[0] < 6 * KT * S:
                work("room", 6 * KT * S - taken[0])
            upad = work("upad", S + CONV - 1)
            sg_in = work("sg_in", GATES_IN * S)[:, :].rearrange("p (m s) -> p m s", m=GATES_IN)
            su = work("su", RN)
        usig, og, tf = tmp[:, 0, :], tmp[:, 1, :], tmp[:, 2, :]
        strict, incl = rw[:, 0:CH], rw[:, CH:CH + P]
        level = [rw[:, CH * (3 + lv):CH * (4 + lv)] for lv in range(LEVELS + 1)]
        own_eye = rw[:, CH * (4 + LEVELS):CH * (5 + LEVELS)]
        heads = rw[:, CH * (5 + LEVELS):CH * (5 + LEVELS) + P]
        with ExitStack() as at:
            with ExitStack() as before:
                aof = sb("aof", [P, KT, S], F32, before)
            coh = sb("coh", [P, 2, KT, S], F32R, at)
            aoh = sb("aoh", [P, 2, KT, S], F32R, at)
            sg2 = sb("sg2", [P, 16, S], F32, at)
        ao_kept = nc.dram_tensor("ao_kept", (KT, P, S), F32, kind="Internal").ap()
        x_kept = nc.dram_tensor("x_kept", (P, KT * S), F32, kind="Internal").ap()
        with ExitStack() as at:
            hidden = [sb(f"hidden{i}", [P, 2, KT, S], F32R, at) for i in range(2)]

        x_loaded, vec_loaded = sem("x_loaded"), sem("vec_loaded")
        const_loaded = {n: sem(f"{n}_loaded") for n in CONSTS}
        w_loaded = [sem(f"w_loaded{i}") for i in range(NRAW)]
        raw_used = sem("raw_used")
        hi_done, lo_done = sem("hi_done"), sem("lo_done")
        filled = sem("filled")
        emptied = [sem(f"emptied{i}") for i in range(NBANK)]
        dve_step, act_step = sem("dve_step"), sem("act_step")
        sq_ready, sq_used, sq_added = sem("sq_ready"), sem("sq_used"), sem("sq_added")
        root_done, rs_ready = sem("root_done"), sem("rs_ready")
        pre_split, hi_ready, hl_ready = sem("pre_split"), sem("hi_ready"), sem("hl_ready")
        ada_used = sem("ada_used")
        modg_ready = sem("modg_ready")
        bkv_ready = sem("bkv_ready")
        exp_done, p_ready, o_done = sem("exp_done"), sem("p_ready"), sem("o_done")
        o_hi, o_empty = sem("o_hi"), sem("o_empty")
        nope_done, rope_done, krot_done = sem("nope_done"), sem("rope_done"), sem("krot_done")
        early_used, factor_done = sem("early_used"), sem("factor_done")
        xn_ready = sem("xn_ready")
        zeros_done = sem("zeros_done")
        lora_scaled, lh_ready = sem("lora_scaled"), sem("lh_ready")
        lw_loaded = [sem(f"lw_loaded{i}") for i in range(2)]
        pool_f = sem("pool_f")
        mu_ready = sem("mu_ready")
        cw_ready, exp_ready = sem("cw_ready"), sem("exp_ready")
        kk0_ready, kksq_ready, nrm_ready = sem("kk0_ready"), sem("kksq_ready"), sem("nrm_ready")
        kmod_ready, rk_ready, at_ready = sem("kmod_ready"), sem("rk_ready"), sem("at_ready")
        iy0_done, pool_step = [sem(f"iy0_done{hh}") for hh in range(2)], sem("pool_step")
        opv_done, opa_done, ost_done, og_ready = sem("opv_done"), sem("opa_done"), sem("ost_done"), sem("og_ready")
        u_ready, kkroot_done, gnr_ready = sem("u_ready"), sem("kkroot_done"), sem("gnr_ready")
        ao_put, ao_back = [sem(f"ao_put{i}") for i in range(2)], sem("ao_back")
        gnsq_ready, gnroot_done, ao_done = sem("gnsq_ready"), sem("gnroot_done"), sem("ao_done")
        conv_done, cen_ready, convn_ready = sem("conv_done"), sem("cen_ready"), sem("convn_ready")
        ao_hi, ao_ready = sem("ao_hi"), sem("ao_ready")
        x_put, x_back = sem("x_put"), sem("x_back")
        stored = sem("stored")

        def bank(name):
            return psum[:, BANK[name], :]

        def wait_filled(eng, name):
            eng.wait_ge(filled, FILL[name] + 1)

        def wait_emptied(eng, name):
            eng.wait_ge(emptied[BANK[name]], TURN[name] + 1)

        def emptied_by(ins, name):
            ins.then_inc(emptied[BANK[name]], 1)

        def roots(name):
            return rs[:, TT:2 * TT] if name == "mix2" else rs[:, 0:TT]

        def vcol(name, k=0, n=1):
            return vec[:, VEC[name] + k:VEC[name] + k + n]

        def wait_loaded(eng, what):
            b = BLOCK_AT[what]
            eng.wait_ge(w_loaded[b % NRAW], 16 * (b // NRAW + 1))

        def raw_of(what):
            return raw[:, BLOCK_AT[what] % NRAW, :]

        def spare(i):
            return ftok.rearrange("p t h a n -> p (t h a n)") if i == 0 else tav.rearrange("p t a h n -> p (t a h n)")

        def ada_sum(s):
            return (sm, pt, sm, pt, sq, sq)[s][:, 0:2, :].rearrange("p a n -> p (a n)")

        def merge_gate(m):
            return (sg_in if m < GATES_IN else sg2)[:, m, :]

        def state(c):
            return qs[:, 0, :] if c == 1 else st[:, c, :]

        block = ctx.enter_context(nc.Block())

        @block.sync
        def _(sp):
            sp.dma_start(vec[:, :], vec_in).then_inc(vec_loaded, 16)
            sp.dma_start(x[:, :, :], x_in.rearrange("p (k s) -> p k s", k=KT)).then_inc(x_loaded, 16)
            sp.dma_start(eye_ones[:, :], io["eye_ones"]).then_inc(const_loaded["eye_ones"], 16)
            raws = 0
            for b, (kind, what) in enumerate(BLOCKS):
                if b >= NRAW:
                    old_kind, old = BLOCKS[b - NRAW]
                    if old_kind == "split":
                        sp.wait_ge(lo_done, SPLIT_AT[old] + 1)
                    elif old[0] == "ada":
                        sp.wait_ge(ada_used, ADA_AT[old] + 1)
                    elif old[0] == "ck" and old[2] < CK_PARTS - 1:
                        raws += 1
                        sp.wait_ge(raw_used, raws)
                    else:
                        wait_filled(sp, ("ckh", old[1], 1))
                sp.dma_start(raw[:, b % NRAW, :], w_in[b]).then_inc(w_loaded[b % NRAW], 16)
                if what == ("ada", 1, KT - 1):
                    for n, t in (("rope", rope), ("causal", causal), ("cmpb", cmpb), ("alibi", alibi)):
                        dst = {"cmpb": "p a b -> p (a b)"}.get(n)
                        sp.dma_start(t.rearrange(dst) if dst else t[:, :], io[n]).then_inc(const_loaded[n], 16)
            sp.wait_ge(xn_ready, 2 * KT)
            sp.dma_start(out.rearrange("p (k s) -> p k s", k=KT), x[:, :, :]).then_inc(stored, 16)
            sp.wait_ge(stored, 16)

        @block.gpsimd
        def _(pool):
            low = [0]

            def weights_ahead(n):
                while low[0] <= min(n, len(SPLITS) - 1):
                    s = low[0]
                    pool.wait_ge(hi_done, s + 1)
                    pool.tensor_tensor(wlo[:, s % NHL, :], raw_of(SPLITS[s]), whi[:, s % NHL, :].bitcast(F32),
                                       ALU.subtract).then_inc(lo_done, 1)
                    low[0] += 1

            weights_ahead(SPLIT_AT["rkv", 0, 1] - 1)
            weights_ahead(SPLIT_AT["rkv", 0, 1] + 1)
            wait_filled(pool, ("fc2", 1, NCH - 1, KT - 1))
            pool.memset(rkvp[:, :, 0:1], 0.0).then_inc(zeros_done, 1)
            pool.memset(upad[:, 0:CONV - 1], 0.0).then_inc(zeros_done, 1)
            pool.memset(ewall[:, :, 0:1], 1.0).then_inc(zeros_done, 1)
            weights_ahead(SPLIT_AT["rkv", 0, 1])
            for i in range(2):
                pool.memset(spare(i)[:, 0:1], 0.0).then_inc(zeros_done, 1)
            psteps = 0
            for f in rwkv_order():
                kind, j = f[0], f[1]
                n = POOL_F * j if kind != "part" else 0
                if kind == "part" and f[2] == 0:
                    weights_ahead(SPLIT_AT[f[1]] + 1)
                elif kind == "norm2":
                    e = EVENT["mix2", j]
                    pool.wait_ge(hi_ready, e + 1)
                    pool.tensor_tensor(ah[:, 1, j, :], tmp[:, e % NTMP, :], ah[:, 0, j, :].bitcast(F32), ALU.subtract).then_inc(hl_ready, 1)
                elif kind == "kk":
                    pool.wait_ge(kmod_ready, j + 1)
                    pool.wait_ge(exp_ready, 2 * j + 2)
                    if j:
                        wait_filled(pool, ("mk", j - 1, 1))
                    pool.tensor_tensor(kh[:, :], rkv[:, 1, :], ewi[:, :], ALU.mult).then_inc(pool_f, 1)
                    pool.wait_ge(pool_f, n + 1)
                    pool.tensor_tensor(cw[:, :].rearrange("p (c n) -> p c n", c=NCK), kh[:, :].rearrange("p (c n) -> p c n", c=NCK),
                                       ew[:, :, CH - 1:CH].to_broadcast([P, NCK, CH]), ALU.mult).then_inc(pool_f, 1)
                elif kind == "at":
                    wait_emptied(pool, ("kkb", j))
                    pool.tensor_tensor(rate[:, :], kk[:, :], rate[:, :], ALU.mult).then_inc(pool_f, 1)
                    pool.wait_ge(pool_f, n + 3)
                    if j:
                        wait_filled(pool, ("mb", j - 1, 1))
                    pool.tensor_tensor(bh[:, :], rate[:, :], ewi[:, :], ALU.mult).then_inc(pool_f, 1)
                    pool.wait_ge(pool_f, n + 4)
                    pool.wait_ge(cw_ready, j + 1)
                    pool.tensor_tensor(sw[:, :].rearrange("p (c n) -> p c n", c=NCK), bh[:, :].rearrange("p (c n) -> p c n", c=NCK),
                                       ew[:, :, CH - 1:CH].to_broadcast([P, NCK, CH]), ALU.mult).then_inc(pool_f, 1)
                elif kind == "re":
                    wait_emptied(pool, ("rkv", j, 0))
                    pool.wait_ge(exp_ready, 2 * j + 2)
                    if j:
                        wait_filled(pool, ("mk", j - 1, 1))
                        wait_emptied(pool, ("rr", j - 1, 1))
                        wait_emptied(pool, ("rr", j - 1, 0))
                    pool.tensor_tensor(arow[:, :, 1, :].rearrange("p t (c n) -> p t c n", c=2),
                                       rkv[:, 0, :].rearrange("p (t c n) -> p t c n", t=TT, c=2),
                                       ew.rearrange("p (t c) n -> p t c n", t=TT), ALU.mult).then_inc(pool_f, 1)
                elif kind == "iy0" and f[2] == 1:
                    wait_emptied(pool, ("mb", j, 1))
                    if j:
                        wait_filled(pool, ("tav", j - 1, 1))
                    pool.tensor_tensor(ip[1], ma[1], level[0].unsqueeze(1).to_broadcast([P, TT, CH]),
                                       ALU.mult).then_inc(pool_step, 1)
                    psteps += 1
                    pool.wait_ge(pool_step, psteps)
                    pool.tensor_tensor(iy2[1], ip[1].unsqueeze(2).to_broadcast([P, TT, 2, CH]),
                                       own_eye.unsqueeze(1).unsqueeze(1).to_broadcast([P, TT, 2, CH]), ALU.add).then_inc(iy0_done[1], 1)
            weights_ahead(len(SPLITS))

        @block.tensor
        def _(pe):
            fills = [0]

            def begin(name):
                assert FILL[name] == fills[0], (name, BANK_ORDER[fills[0]])
                fills[0] += 1
                free(name)

            def free(name):
                if TURN[name]:
                    pe.wait_ge(emptied[BANK[name]], TURN[name])

            def three(dst, w, wcols, a, k, first, last, a_moving=True):
                wh, wl = whi[:, w, wcols], wlo[:, w, wcols]
                h_, l_ = a[:, 0, k], a[:, 1, k]
                if a_moving:
                    pe.matmul(dst, wh, h_, start=first, stop=False)
                    pe.matmul(dst, wh, l_, start=False, stop=False)
                    return pe.matmul(dst, wl, h_, start=False, stop=last)
                pe.matmul(dst, h_, wh, start=first, stop=False)
                pe.matmul(dst, l_, wh, start=False, stop=False)
                return pe.matmul(dst, h_, wl, start=False, stop=last)

            def product(name, what, a, kts, col0=0, event=None):
                s = SPLIT_AT[what]
                pe.wait_ge(lo_done, s + 1)
                begin(name)
                for i, k in enumerate(kts):
                    if event is not None:
                        pe.wait_ge(hl_ready, EVENT[event + (i,)] + 1)
                    mm = three(bank(name), s % NHL, slice(col0 + i * P, col0 + i * P + P), a, k, i == 0, i == len(kts) - 1)
                mm.then_inc(filled, 1)

            def ada(s):
                begin(("ada", s))
                pe.wait_ge(ada_used, KT * (s + 1))
                for n in range(KT):
                    mm = pe.matmul(bank(("ada", s))[:, n:n + 1], ada_sum(s)[:, n * P:n * P + P], ones[:, 0:1], start=True, stop=True)
                mm.then_inc(filled, 1)

            def product_pair(names, a, event, lag=2):
                for name in names:
                    pe.wait_ge(lo_done, SPLIT_AT[name] + 1)
                    begin(name)
                for i in range(KT + lag):
                    if i < KT:
                        pe.wait_ge(hl_ready, EVENT[event + (i,)] + 1)
                    for name, k in zip(names, (i, i - lag)):
                        if 0 <= k < KT:
                            mm = three(bank(name), SPLIT_AT[name] % NHL, slice(k * P, k * P + P), a, k, k == 0, k == KT - 1)
                            if k == KT - 1:
                                mm.then_inc(filled, 1)

            def sum_squares(name):
                for k in range(dict(NORMS)[name]):
                    sum_step(name, k)

            def sum_step(name, k):
                n, last = SQ_AT[name, k], dict(NORMS)[name] - 1
                if k == 0:
                    free(("ss", name))
                pe.wait_ge(sq_ready, n + 1)
                at = SQ_SLOT[name, k] % 2
                for t in range(TT):
                    mm = pe.matmul(bank(("ss", name))[:, t:t + 1], sq[:, at, t * P:t * P + P], ones[:, 0:1],
                                   start=(k, t) == (0, 0), stop=k == last, skip_group_check=True)
                if k < last:
                    mm.then_inc(sq_used, 1)
                else:
                    assert FILL["ss", name] == fills[0], name
                    fills[0] += 1
                    mm.then_inc(filled, 1)

            def sum_total(name):
                begin(("ss", name))
                pe.wait_ge(sq_added, ADD_AT[name, KT - 1] + 1)
                for t in range(TT):
                    mm = pe.matmul(bank(("ss", name))[:, t:t + 1], sq_sum[:, SUM_OF[name], t * P:t * P + P], ones[:, 0:1],
                                   start=True, stop=True)
                mm.then_inc(filled, 1)

            def spread(name):
                begin(("rb", name))
                pe.wait_ge(rs_ready, [n for n, _ in NORMS].index(name) + 1)
                for t in range(TT):
                    mm = pe.matmul(bank(("rb", name))[:, t * P:t * P + P], roots(name)[:, t:t + 1].to_broadcast([P, P]), eye, start=True, stop=True)
                mm.then_inc(filled, 1)

            def attention(tag, units, at):
                base = {"nsa": 0, "mla": len(NSA_UNITS)}[tag]
                for kind, u in attention_order(tag):
                    h, qt, br = units[u]
                    probs, turned, scores, values = at
                    if kind == "S":
                        q, k, w = scores(h, qt, br)
                        begin(("S", tag, u))
                        pe.matmul(bank(("S", tag, u))[:, 0:w], q, k, start=True, stop=True).then_inc(filled, 1)
                    elif kind == "PT":
                        begin(("PT", tag, u))
                        pe.wait_ge(p_ready, base + u + 1)
                        for kt, (_, n) in enumerate(values(h, qt, br)):
                            mm = pe.transpose(bank(("PT", tag, u))[0:n, kt * P:kt * P + P],
                                              probs[:, u % PROBS[tag], kt * P:kt * P + n], eye)
                        mm.then_inc(filled, 1)
                    else:
                        wait_emptied(pe, ("PT", tag, u))
                        pair = base_pair[tag] + h // 2
                        if h % 2 == 0 and qt == 0 and br in (0, None):
                            if pair >= 2:
                                pe.wait_ge(o_empty, pair - 1)
                            elif pair == 1:
                                wait_emptied(pe, LAST_BESIDE)
                        rows = slice(64 * (h % 2), 64 * (h % 2) + 64)
                        vals = values(h, qt, br)
                        for kt, (v, n) in enumerate(vals):
                            mm = pe.matmul(psum[rows, obank(pair), qt * P:qt * P + P], v, turned[u % TURNED[tag]][0:n, kt * P:kt * P + P],
                                           start=br in (0, None) and kt == 0, stop=br in (2, None) and kt == len(vals) - 1)
                        mm.then_inc(o_done, 1)

            base_pair = {"nsa": 0, "mla": H // 2}

            def compressed_hidden(kv, q):
                if q == 0:
                    for ht in range(2):
                        free(("ckh", kv, ht))
                    pe.wait_ge(bkv_ready, kv + 1)
                wait_loaded(pe, ("ck", kv, q))
                w = raw_of(("ck", kv, q))
                for ht in range(2):
                    for i in range(4):
                        lp = 4 * q + i
                        mm = pe.matmul(bank(("ckh", kv, ht))[:, 0:G * NC], w[:, i * CHID + ht * P:i * CHID + ht * P + P],
                                       bkv[:, kv, lp, :], start=lp == 0, stop=lp == LP - 1)
                    if q == CK_PARTS - 1:
                        assert FILL["ckh", kv, ht] == fills[0]
                        fills[0] += 1
                        mm.then_inc(filled, 1)
                    elif ht == 1:
                        mm.then_inc(raw_used, 1)

            pe.wait_ge(vec_loaded, 16)
            pe.wait_ge(const_loaded["eye_ones"], 16)
            sum_squares("mix")
            ada(0)
            spread("mix")
            ada(1)
            for f in FRONT:
                kind = f[0]
                if f == Z_ORDER[0]:
                    product_pair(Z_ORDER[0:2], ah, ("mix",))
                elif kind == "z" and f != Z_ORDER[1]:
                    product(f, f, ah, range(KT))
                elif kind == "ada":
                    ada(f[1])
                elif kind == "ck":
                    compressed_hidden(*f[1:])
                elif kind == "ss":
                    sum_squares(f[1])
                elif kind == "norm":
                    spread(f[1])
                elif kind == "vt":
                    begin(f)
                    wait_emptied(pe, ("z", (7, 9)[f[1]]))
                    for t in range(TT):
                        mm = pe.transpose(bank(f)[:, t * P:t * P + P], vT[:, f[1], t * P:t * P + P], eye)
                    mm.then_inc(filled, 1)
                elif kind == "gt":
                    begin(f)
                    wait_emptied(pe, ("z", 10))
                    for t in range(TT):
                        mm = pe.transpose(bank(f)[:, t * 32:t * 32 + 32], gT[:, t * P:t * P + P], eye[0:32, 0:32])
                    mm.then_inc(filled, 1)
                elif kind == "kc":
                    begin(f)
                    for ht in range(2):
                        wait_emptied(pe, ("ckh", 0, ht))
                        mm = pe.matmul(bank(f)[:, 0:G * NC], vcol("w_ck2", ht * P, P), hid[:, 0, ht, :], start=ht == 0, stop=ht == 1)
                    mm.then_inc(filled, 1)
                elif kind == "vc":
                    begin(f)
                    for g in range(G):
                        for ht in range(2):
                            wait_emptied(pe, ("ckh", 1, ht))
                            mm = pe.matmul(bank(f)[0:NC, g * DH:g * DH + DH], hid[:, 1, ht, g * NC:g * NC + NC],
                                           vcol("w_cv2", ht * DH, DH), start=ht == 0, stop=ht == 1)
                    mm.then_inc(filled, 1)

            def nsa_scores(h, qt, br):
                rows = slice(64 * (h % 2), 64 * (h % 2) + 64)
                q = qT[rows, h // 2, qt * P:qt * P + P]
                if br == 0:
                    return q, kcT[rows, (h // HG) * NC:(h // HG) * NC + NC], NC
                return q, (ksd, kwd)[br - 1][rows, h // HG, 0:qt * P + P], qt * P + P

            def nsa_values(h, qt, br):
                g = h // HG
                if br == 0:
                    return [(vc[0:NC, g * DH:g * DH + DH], NC)]
                return [(vtok[:, br - 1, kt, g * DH:g * DH + DH], P) for kt in range(qt + 1)]

            for m in (0, 1, 2, 3, 6, 8):
                wait_emptied(pe, ("z", m))
            for n in (("vt", 0), ("vt", 1), ("kc",), ("vc",)):
                wait_emptied(pe, n)
            attention("nsa", NSA_UNITS, (sm, turned_nsa, nsa_scores, nsa_values))

            for h in range(MH):
                product(("uq", h), ("uq", h // 2), cqh, range(3), (h % 2) * 3 * P, event=("cq",) if h == 0 else None)
            for i in range(MH // 2):
                product(("uk", i), ("uk",), cqh, range(3, 5), i * 2 * P, event=("ckv",) if i == 0 else None)
            s = SPLIT_AT[("uv",)]
            pe.wait_ge(lo_done, s + 1)
            for t in range(TT):
                begin(("uv", t))
                for k in range(2):
                    mm = three(bank(("uv", t)), s % NHL, slice(k * S, k * S + S), cqh[:, :, :, t * P:t * P + P], 3 + k,
                               k == 0, k == 1, a_moving=False)
                mm.then_inc(filled, 1)

            def mla_scores(h, qt, br):
                return qcat[0:DQK, h, qt * P:qt * P + P], kcat[0:DQK, h, 0:qt * P + P], qt * P + P

            def mla_values(h, qt, br):
                return [(vm[:, kt, h * MV:h * MV + MV], P) for kt in range(qt + 1)]

            pe.wait_ge(rope_done, MH)
            pe.wait_ge(krot_done, 1)
            for i in range(MH // 2):
                wait_emptied(pe, ("uk", i))
            for t in range(TT):
                wait_emptied(pe, ("uv", t))
            attention("mla", MLA_UNITS, (sm2, turned_mla, mla_scores, mla_values))

            for m in range(16):
                product(("gate", m), ("gate", m), ah, range(KT))
                if m == 8:
                    ada(4)
            pe.wait_ge(o_empty, H // 2 + MH // 2)
            for m in range(KT):
                product(("on", m), ("nm", m), oh, range(4))
                product(("om", m), ("nm", m), oh, range(4, 8), col0=4 * P)
                if m == 0:
                    ada(5)
            for m in range(KT):
                product(("wo", m), ("wo", m), yh, range(KT), event=("y",) if m == 0 else None)
            sum_total("mlp")
            spread("mlp")

            def mlp(n, first, last):
                for half, c in mlp_order():
                    for m in range(KT):
                        if half == 1 and n == 2 and c == 0 and m <= EARLY:
                            if m == EARLY:
                                product(("fc1", n, c, m), ("fc1", n, c, m), ah, range(KT), event=first)
                        elif half == 1 and (c, m) == (0, 0):
                            product_pair([("fc1", n, c, 0), ("fc1", n, c, 1)], ah, first)
                        elif half == 1 and (n, c, m) != (1, 0, 1):
                            product(("fc1", n, c, m), ("fc1", n, c, m), ah, range(KT))
                        elif half == 1:
                            continue
                        else:
                            product(("fc2", n, c, m), ("fc2", n, c, m), hidden[c % 2], range(KT), event=("hid", n, c) if m == 0 else None)
                for name in last:
                    sum_total(name)

            mlp(1, ("mlp",), ())

            own_chunks = [(t, slice(CH * c, CH * c + CH)) for t in range(TT) for c in range(2)]
            for f in rwkv_order():
                kind, j = f[0], f[1]
                if kind == "part":
                    what, k0, k1 = f[1:]
                    n = SPLIT_AT[what]
                    if k0 == 0:
                        pe.wait_ge(lo_done, n + 1)
                        free(what)
                    for k in range(k0, k1):
                        if what == ("rkv", 0, 1):
                            pe.wait_ge(hl_ready, EVENT["early2", k] + 1)
                            if k == 4:
                                sum_total("final")
                                sum_total("mix2")
                        elif what == ("rkv", 0, 0) and k in (3, 6):
                            spread("mix2" if k == 3 else "final")
                        elif what == ("lora", 0, 1):
                            pe.wait_ge(hl_ready, EVENT["mix2", k] + 1)
                        mm = three(bank(what), n % NHL, slice(k * P, k * P + P), ah, k, k == 0, k == KT - 1)
                        if what == ("rkv", 0, 0) and k < KT - 1:
                            mm.then_inc(early_used, 1)
                    if k1 == KT:
                        assert FILL[what] == fills[0], (what, BANK_ORDER[fills[0]])
                        fills[0] += 1
                        mm.then_inc(filled, 1)
                    continue
                if kind in IN_BANKS:
                    begin(f)
                    b = bank(f)
                elif kind not in ("opv", "opa", "ost"):
                    continue
                if kind in ("lw2", "la2", "lg2"):
                    pe.wait_ge(lw_loaded[j % 2], 16 * (j // 2 + 1))
                    pe.wait_ge(lh_ready, 3 if kind == "lg2" else 2)
                    rows, cols, i = {"lw2": (slice(0, LORA), slice(0, P), 0), "la2": (slice(LORA, P), slice(0, P), 0),
                                     "lg2": (slice(0, P), slice(P, 2 * P), 1)}[kind]
                    mm = pe.matmul(b, lwt[rows, j % 2, cols], lh[rows, i, :], start=True, stop=True)
                elif kind == "kkss":
                    pe.wait_ge(kksq_ready, j + 1)
                    for t in range(TT):
                        mm = pe.matmul(b[:, 2 * t:2 * t + 2], sq[:, 0, t * P:t * P + P], heads[:, ::RN], start=True, stop=True)
                elif kind in ("kkb", "gnb"):
                    src = nrt if kind == "kkb" else gnt
                    pe.wait_ge(nrm_ready if kind == "kkb" else gnr_ready, j + 1)
                    for t in range(TT):
                        for hh in range(2):
                            mm = pe.matmul(b[RN * hh:RN * hh + RN, t * P:t * P + P],
                                           src[:, 2 * t + hh:2 * t + hh + 1].to_broadcast([P, RN]), eye, start=True, stop=True)
                elif kind == "bonus":
                    pe.wait_ge(rk_ready, j + 1)
                    mm = pe.matmul(b, heads, tf, start=True, stop=True)
                elif kind == "tok":
                    i = f[2]
                    if i == 0:
                        pe.wait_ge(at_ready, j + 1)
                    elif i < 3:
                        pe.wait_ge(pool_f, POOL_F * j + (5, 2)[i - 1])
                    for t in range(TT):
                        cols = slice(t * P, t * P + P)
                        src = (arow[:, t, 0, :], sw[:, cols], cw[:, cols], rkv[:, 2, cols])[i]
                        mm = pe.transpose(b[:, cols], src, eye)
                elif kind in ("mb", "mk"):
                    hh = f[2]
                    rows = slice(RN * hh, RN * hh + RN)
                    src = bh if kind == "mb" else kh
                    pe.wait_ge(at_ready, j + 1)
                    pe.wait_ge(pool_f, POOL_F * j + 6)
                    for t, own in own_chunks:
                        mm = pe.matmul(b[own, t * P:t * P + P], src[rows, t * P + own.start:t * P + own.stop],
                                       arow[rows, t, :, own], start=True, stop=True)
                elif kind == "inv":
                    hh, lv = f[2], f[3]
                    if lv == 0:
                        pe.wait_ge(iy0_done[hh], j + 1)
                    else:
                        wait_emptied(pe, ("iy", j, hh, lv))
                    for t in range(TT):
                        mm = pe.transpose(b[:, t * P:t * P + P], iy[hh][:, t, :], eye)
                elif kind == "akv":
                    hh = f[2]
                    wait_emptied(pe, ("mk", j, hh))
                    wait_emptied(pe, ("tok", j, 3))
                    for t, own in own_chunks:
                        mm = pe.matmul(b[own, t * RN:t * RN + RN], ka[hh][own, t, :], vtk[own, t, hh * RN:hh * RN + RN], start=True, stop=True)
                elif kind == "ip":
                    hh, lv = f[2], f[3]
                    wait_emptied(pe, ("inv", j, hh, lv - 1))
                    for t, own in own_chunks:
                        mm = pe.matmul(b[own, t * CH:t * CH + CH], ma[hh][own, t, :], ix[hh][own, t, own], start=True, stop=True)
                elif kind == "iy":
                    hh, lv = f[2], f[3]
                    wait_emptied(pe, ("ip", j, hh, lv))
                    for t, own in own_chunks:
                        mm = pe.matmul(b[own, t * CH:t * CH + CH], ip[hh][own, t, :], iy[hh][own, t, own], start=True, stop=True)
                elif kind == "tav":
                    hh = f[2]
                    wait_emptied(pe, ("iy", j, hh, LEVELS))
                    wait_emptied(pe, ("akv", j, hh))
                    for t, own in own_chunks:
                        mm = pe.matmul(b[own, t * P:t * P + P], iy[hh][own, t, own], ftok[own, t, hh, :, :].rearrange("p a n -> p (a n)"),
                                       start=True, stop=True)
                elif kind == "rr":
                    hh = f[2]
                    wait_emptied(pe, ("tav", j, hh))
                    for t in range(TT):
                        mm = pe.matmul(b[RN * hh:RN * hh + RN, t * P:t * P + P], tav[:, t, 0, hh, :], mr[hh][:, t, :],
                                       start=True, stop=True)
                elif kind == "opv":
                    hh = f[2]
                    wait_emptied(pe, ("mk", j, hh))
                    wait_emptied(pe, ("tok", j, 3))
                    if j:
                        pe.wait_ge(og_ready, j)
                    else:
                        pe.wait_ge(o_empty, H // 2 + MH // 2)
                    for t in range(TT):
                        mm = pe.matmul(psum[RN * hh:RN * hh + RN, OBANK, t * P:t * P + P], vtk[:, t, hh * RN:hh * RN + RN],
                                       kr[hh][:, t, :], start=t == 0, stop=False, skip_group_check=True)
                    mm.then_inc(opv_done, 1)
                elif kind == "opa":
                    hh = f[2]
                    wait_emptied(pe, ("tav", j, hh))
                    for t in range(TT):
                        mm = pe.matmul(psum[RN * hh:RN * hh + RN, OBANK, t * P:t * P + P], tav[:, t, 1, hh, :],
                                       mr[hh][:, t, :], start=False, stop=False, skip_group_check=True)
                    mm.then_inc(opa_done, 1)
                elif kind in ("pt", "qq"):
                    rows = slice(CH * f[2], CH * f[2] + CH)
                    for t in range(TT):
                        dst = [b[RN * hh:RN * hh + RN, t * RN:t * RN + RN] for hh in range(2)]
                        of = [slice(RN * hh, RN * hh + RN) for hh in range(2)]
                        for hh in range(2):
                            if kind == "pt":
                                mm = pe.matmul(dst[hh], tav[rows, t, 0, hh, :], btok[rows, t, of[hh]], start=True, stop=True)
                            else:
                                pe.matmul(dst[hh], btok[rows, t, of[hh]], tav[rows, t, 1, hh, :], start=True, stop=False)
                                mm = pe.matmul(dst[hh], ktok[rows, t, of[hh]], vtk[rows, t, of[hh]], start=False, stop=True)
                elif kind == "st":
                    c = f[2]
                    if c == 1:
                        for half in range(2):
                            wait_emptied(pe, ("pt", j, half))
                            wait_emptied(pe, ("qq", j, half))
                    else:
                        wait_emptied(pe, ("st", j, c - 1))
                    for hh in range(2):
                        rows = slice(RN * hh, RN * hh + RN)
                        mm = pe.matmul(b[rows, 0:RN], pts[rows, c, :], state(c)[rows, :], start=True, stop=True)
                elif kind == "ost":
                    wait_emptied(pe, ("st", j, NCK - 2))
                    wait_emptied(pe, ("rr", j, 0))
                    wait_emptied(pe, ("rr", j, 1))
                    for c in range(1, NCK):
                        for hh in range(2):
                            rows, cols = slice(RN * hh, RN * hh + RN), slice(c * CH, c * CH + CH)
                            mm = pe.matmul(psum[rows, OBANK, cols], state(c)[rows, :], rp[rows, cols], start=False, stop=True,
                                           skip_group_check=True)
                    mm.then_inc(ost_done, 1)
                elif kind == "gnm":
                    pe.wait_ge(og_ready, j + 1)
                    mm = pe.matmul(b, heads, og, start=True, stop=True)
                elif kind == "gnv":
                    pe.wait_ge(gnsq_ready, j + 1)
                    for t in range(TT):
                        mm = pe.matmul(b[:, 2 * t:2 * t + 2], sq[:, 1, t * P:t * P + P], heads[:, ::RN], start=True, stop=True)
                if kind in IN_BANKS:
                    mm.then_inc(filled, 1)
            begin(("convmean",))
            for k in range(KT):
                pe.wait_ge(conv_done, k + 1)
                mm = pe.matmul(bank(("convmean",)), ones, x[:, k, :], start=k == 0, stop=k == KT - 1)
            mm.then_inc(filled, 1)
            pe.wait_ge(ao_ready, KT)
            for m in range(KT):
                product(("pr", m), ("pr", m), aoh, range(KT))
                if m == 1:
                    sum_total("conv")
                elif m == 2:
                    spread("conv")
            for m in range(KT):
                product(("pc", m), ("pc", m), coh, range(KT), event=("conv",) if m == 0 else None)
            for m in range(KT):
                product(("wo2", m), ("wo2", m), ah, range(KT), event=("y2",) if m == 0 else None)
            for m in range(EARLY):
                what = ("fc1", 2, 0, m)
                pe.wait_ge(lo_done, SPLIT_AT[what] + 1)
                free(what)
                for k in range(KT):
                    if (m, k) == (0, 3):
                        sum_total("ff2")
                    if (m, k) == (1, 3):
                        spread("ff2")
                    if m == 0:
                        pe.wait_ge(hl_ready, EVENT["early", k] + 1)
                    mm = three(bank(what), SPLIT_AT[what] % NHL, slice(k * P, k * P + P), hidden[1], k, k == 0, k == KT - 1)
                assert FILL[what] == fills[0], what
                fills[0] += 1
                mm.then_inc(filled, 1)
            mlp(2, ("ff2",), ("final2",))
            spread("final2")

        @block.scalar
        def _(act):
            split = [0]

            def weights_ahead(n):
                while split[0] <= min(n, len(SPLITS) - 1):
                    s = split[0]
                    if SPLITS[s][0] == "lora":
                        act.wait_ge(lora_scaled, 1 + 2 * SPLITS[s][1] + (1 - SPLITS[s][2]))
                    else:
                        wait_loaded(act, SPLITS[s])
                    if s >= NHL:
                        act.wait_ge(filled, BLOCK_LAST[SPLITS[s - NHL]] + 1)
                    act.activation(whi[:, s % NHL, :], raw_of(SPLITS[s]), ACT.Copy).then_inc(hi_done, 1)
                    split[0] += 1

            def squares(name, src, wait):
                for k in range(dict(NORMS)[name]):
                    wait(k)
                    square(name, k, src[:, k, :])

            def square(name, k, src, scale=1.0):
                if name in SUM_OF and k == 0:
                    dst = sq_sum[:, SUM_OF[name], :]
                    for nm, _ in NORMS[:[nm for nm, _ in NORMS].index(name)]:
                        if SUM_OF.get(nm) == SUM_OF[name]:
                            wait_filled(act, ("ss", nm))
                else:
                    n = SQ_SLOT[name, k]
                    dst = sq[:, n % 2, :]
                    if n >= 2:
                        old = SQ_SLOTS[n - 2]
                        if old in ADD_AT:
                            act.wait_ge(sq_added, ADD_AT[old] + 1)
                        elif old[1] == dict(NORMS)[old[0]] - 1:
                            wait_filled(act, ("ss", old[0]))
                        else:
                            used = sum(1 for q, kk in SQ_SLOTS[:n - 1] if q not in SUM_OF and kk < dict(NORMS)[q] - 1)
                            act.wait_ge(sq_used, used)
                act.activation(dst, src, ACT.Square, scale=scale).then_inc(sq_ready, 1)

            def root(name):
                wait_emptied(act, ("ss", name))
                act.activation(roots(name), roots(name), ACT.Sqrt).then_inc(root_done, 1)

            def high(event, dst, bias=0.0):
                n = EVENT[event]
                act.wait_ge(pre_split, n + 1)
                act.activation(dst, tmp[:, n % NTMP, :], ACT.Identity, bias=bias).then_inc(hi_ready, 1)

            def empty(name, dst, src=None, **kw):
                wait_filled(act, name)
                emptied_by(act.activation(dst, bank(name) if src is None else src, kw.pop("func", ACT.Copy), **kw), name)

            act.wait_ge(x_loaded, 16)
            squares("mix", x, lambda k: None)
            root("mix")
            weights_ahead(NHL - 1)
            act.wait_ge(modg_ready, 1)
            for k in range(KT):
                high(("mix", k), ah[:, 0, k, :], bias=mod[:, k:k + 1])
            latent = {"cq": (0, 3), "ckv": (3, 2)}
            for f in FRONT:
                kind = f[0]
                if kind == "ss":
                    k0, n = latent[f[1]]
                    squares(f[1], zd[:, k0:k0 + n, :], lambda k: wait_emptied(act, ("z", 11 + k0 + k)))
                elif kind == "norm":
                    k0, n = latent[f[1]]
                    root(f[1])
                    for k in range(n):
                        high((f[1], k), cqh[:, 0, k0 + k, :])
                elif kind == "ck" and f[2] == CK_PARTS - 1:
                    for ht in range(2):
                        empty(("ckh", f[1], ht), hid[:, f[1], ht, :], bank(("ckh", f[1], ht))[:, 0:G * NC], func=ACT.Silu)
                elif kind == "kc":
                    empty(f, kcT[:, :], bank(f)[:, 0:G * NC])
                elif kind == "vc":
                    empty(f, vc[0:NC, :], bank(f)[0:NC, 0:G * DH])
                elif kind == "vt":
                    empty(f, vtok[:, f[1], :, :].rearrange("p t n -> p (t n)"))
                elif kind == "gt":
                    empty(f, gates[:, :, :].rearrange("p t n -> p (t n)"), bank(f)[:, 0:TT * 32])
                if kind != "z":
                    continue
                m = f[1]
                weights_ahead(min(SPLIT_AT[f] + 1, SPLIT_AT[Z_ORDER[-1]]))
                z = bank(f)
                if m < 4:
                    empty(f, qT[:, m, :], scale=over_slope[:, m:m + 1])
                elif m in (4, 5):
                    wait_filled(act, f)
                    for g in range(G):
                        rows = slice(64 * g, 64 * g + 64)
                        act.activation(kcd[0:64, m - 4, g, :], z[rows, :], ACT.Copy).then_inc(act_step, 1)
                        last = act.activation(kcd[64:128, m - 4, g, 0:S - 1], z[rows, 1:S], ACT.Copy)
                        if g < G - 1:
                            last.then_inc(act_step, 1)
                    emptied_by(last, f)
                elif m in (6, 8):
                    wait_filled(act, f)
                    dst = ksd if m == 6 else kwd
                    for g in range(G):
                        for half in range(2):
                            last = act.activation(dst[64 * half:64 * half + 64, g, :], z[64 * g:64 * g + 64, :], ACT.Copy)
                            if (g, half) != (G - 1, 1):
                                last.then_inc(act_step, 1)
                    emptied_by(last, f)
                elif m in (7, 9):
                    empty(f, vT[:, (m - 7) // 2, :])
                elif m == 10:
                    wait_filled(act, f)
                    act.activation(gT[:, :], z[0:32, :], ACT.Sigmoid).then_inc(act_step, 1)
                    emptied_by(act.activation(zkr[64:128, :], z[64:128, :], ACT.Copy), f)
                else:
                    empty(f, zd[:, m - 11, :])
            weights_ahead(SPLIT_AT["uq", 0] + 1)

            def attention(tag, units, probs, turned, st):
                base = {"nsa": 0, "mla": len(NSA_UNITS)}[tag]
                per_pair = 2 * TT * (3 if tag == "nsa" else 1)
                for kind, u in attention_order(tag):
                    if kind == "S":
                        h, qt, br = units[u]
                        w = NC if br == 0 else qt * P + P
                        wait_emptied(act, ("S", tag, u))
                        act.activation(probs[:, u % PROBS[tag], 0:w], probs[:, u % PROBS[tag], 0:w], ACT.Exp, bias=st[:, u % PROBS[tag], 0:1],
                                       scale=-1.0, accum_out=st[:, u % PROBS[tag], 1:2]).then_inc(exp_done, 1)
                    elif kind == "PT":
                        h, qt, br = units[u]
                        if u >= TURNED[tag]:
                            act.wait_ge(o_done, base + u - TURNED[tag] + 1)
                        if br == 0:
                            empty(("PT", tag, u), turned[u % TURNED[tag]][0:NC, 0:P], bank(("PT", tag, u))[0:NC, 0:P])
                        else:
                            empty(("PT", tag, u), turned[u % TURNED[tag]][:, 0:qt * P + P], bank(("PT", tag, u))[:, 0:qt * P + P])
                    elif (u + 1) % per_pair == 0:
                        act.wait_ge(o_done, base + u + 1)
                        pair = u // per_pair + (H // 2 if tag == "mla" else 0)
                        act.activation(oh[:, 0, pair, :], psum[:, obank(pair), :], ACT.Copy).then_inc(o_hi, 1)

            attention("nsa", NSA_UNITS, sm, turned_nsa, stat)
            for h in range(MH):
                weights_ahead(SPLIT_AT["uq", h // 2] + 1)
                wait_filled(act, ("uq", h))
                act.activation(qcat[0:NOPE, h, :], bank(("uq", h))[0:NOPE, :], ACT.Copy, scale=-DQK ** -0.5).then_inc(nope_done, 1)
            for i in range(MH // 2):
                weights_ahead(SPLIT_AT["uk",] + 1)
                wait_filled(act, ("uk", i))
                for half in range(2):
                    last = act.activation(kcat[0:NOPE, 2 * i + half, :], bank(("uk", i))[64 * half:64 * half + 64, :], ACT.Copy)
                    if half == 0:
                        last.then_inc(act_step, 1)
                emptied_by(last, ("uk", i))
            for t in range(TT):
                empty(("uv", t), vm[:, t, :])
            weights_ahead(SPLIT_AT["gate", 0] + 1)
            attention("mla", MLA_UNITS, sm2, turned_mla, stat2)
            for m in range(16):
                weights_ahead(SPLIT_AT["gate", m] + 1)
                empty(("gate", m), sg[:, m, :], func=ACT.Sigmoid)
            for m in range(KT):
                weights_ahead(SPLIT_AT["nm", m] + 1)
                high(("y", m), yh[:, 0, m, :])
            for m in range(KT):
                weights_ahead(SPLIT_AT["wo", m] + 1)
                if m == 0:
                    wait_filled(act, ("ada", 5))
                    at = 2 * TT + [n for n, _ in NORMS].index("mix")
                    wait_emptied(act, ("rb", "mix"))
                    act.activation(rs[:, at + 3:at + 4], rs[:, at:at + 1], ACT.Sqrt)
                else:
                    wait_emptied(act, ("wo", m - 1))
                    square("mlp", m - 1, x[:, m - 1, :])
            weights_ahead(SPLIT_AT["fc1", 1, 0, 1])
            wait_emptied(act, ("wo", KT - 1))
            square("mlp", KT - 1, x[:, KT - 1, :])
            root("mlp")
            for k in range(KT):
                high(("mlp", k), ah[:, 0, k, :], bias=mod[:, 24 + k:25 + k])

            def mlp(n, last):
                for half, c in mlp_order():
                    for m in range(KT):
                        what = (f"fc{half}", n, c, m)
                        weights_ahead(SPLIT_AT[what] + 1)
                        if half == 1:
                            e = EVENT["hid", n, c, m]
                            act.wait_ge(pre_split, e - 1)
                            empty(what, sq[:, e % 2, :], func=ACT.Relu)
                            if n == 1 or c or m >= EARLY:
                                weights_ahead(SPLIT_AT[what] + 2)
                            elif m == 1:
                                weights_ahead(SPLIT_AT[what] + EARLY + 1)
                            if c >= 2 and m == 0:
                                wait_filled(act, ("fc2", n, c - 2, KT - 1))
                            high(("hid", n, c, m), hidden[c % 2][:, 0, m, :])
                        elif c == NCH - 1 and m:
                            last(m - 1)
                last(KT - 1)

            def final_squares(k):
                wait_emptied(act, ("fc2", 1, NCH - 1, k))
                square("final", k, x[:, k, :])
                square("mix2", k, x[:, k, :], scale=vcol("g_final", k))
                high(("early2", k), ah[:, 0, k, :])

            def final2_squares(k):
                wait_emptied(act, ("fc2", 2, NCH - 1, k))
                square("final2", k, x[:, k, :])

            mlp(1, final_squares)
            weights_ahead(SPLIT_AT["rkv", 0, 1] + 1)
            root("final")
            root("mix2")

            wait_filled(act, ("fc2", 1, NCH - 1, KT - 1))
            act.dma_start(rw[:, :], io["rw"]).then_inc(const_loaded["rw"], 16)
            for j in range(2):
                act.dma_start(lwt[:, j, :], io["lw"][j]).then_inc(lw_loaded[j], 16)
            for f in rwkv_order():
                kind, j = f[0], f[1]
                if kind == "part":
                    what = f[1]
                    if f[2] == 0:
                        weights_ahead(SPLIT_AT[what] + 1)
                    if f[3] < KT or what[:1] + what[2:] in (("glu", 0), ("lora", 0)) or what in (("rkv", 0, 1), ("rkv", 0, 0)):
                        continue
                    if what[0] == "rkv":
                        j, i = what[1:]
                        old = {1: ("rkv", j - 1, 2), 0: ("rkv", j - 1, 0), 2: ("rkv", j, 1)}[i]
                        if old[1] >= 0:
                            wait_emptied(act, old)
                        wait_filled(act, what)
                        act.activation(rkvp[:, RKV_SLOT[i], 1:S + 1], bank(what), ACT.Copy, scale=vcol("mu_rkv_2", 8 * i + j)).then_inc(mu_ready, 1)
                    elif what[0] == "glu":
                        j = what[1]
                        if j:
                            wait_emptied(act, ("glu", j - 1, 0))
                        else:
                            act.wait_ge(hl_ready, EVENT["mix2", KT - 1] + 1)
                        empty(what, usig, func=ACT.Sigmoid)
                    elif what[0] == "lora":
                        act.wait_ge(zeros_done, 5)
                        empty(what, spare(what[1])[:, 1:S + 1])
                    else:
                        empty(what, merge_gate(what[1]), func=ACT.Sigmoid, bias=vcol("b_gate_2", what[1]))
                elif kind == "norm2":
                    if j < KT - 1:
                        act.wait_ge(early_used, j + 1)
                    else:
                        wait_filled(act, ("rkv", 0, 0))
                    high(("mix2", j), ah[:, 0, j, :])
                elif kind == "factor":
                    act.wait_ge(zeros_done, 1)
                    act.wait_ge(factor_done, 2 - j)
                    act.activation(rkvp[:, RKV_SLOT[j], 1:S + 1], bank(("rkv", 0, j)), ACT.Copy, scale=vcol("mu_rkv_2", 8 * j)).then_inc(mu_ready, 1)
                elif kind == "xput":
                    act.wait_ge(xn_ready, KT)
                    act.dma_start(x_kept, x[:, :, :].rearrange("p k s -> p (k s)")).then_inc(x_put, 16)
                elif kind == "hidden":
                    wait_emptied(act, ("lora", j, 0))
                    pre = (btok, ktok)[j].rearrange("p t n -> p (t n)")
                    if j == 0:
                        act.activation(lh[0:LORA, 0, :], pre[0:LORA, :], ACT.Tanh).then_inc(lh_ready, 1)
                        act.activation(lh[LORA:P, 0, :], pre[LORA:P, :], ACT.Copy).then_inc(lh_ready, 1)
                    else:
                        act.activation(lh[:, 1, :], pre, ACT.Sigmoid).then_inc(lh_ready, 1)
                elif kind == "lw2":
                    if j:
                        wait_filled(act, ("tok", j - 1, 1))
                    empty(f, sw[:, :], func=ACT.Sigmoid, bias=vcol("decay_w0_2", j))
                elif kind == "la2":
                    if j:
                        act.wait_ge(pool_f, POOL_F * (j - 1) + 4)
                    empty(f, rate[:, :], func=ACT.Sigmoid, bias=vcol("aaa_a0_2", j))
                elif kind == "lg2":
                    if j >= 2:
                        act.wait_ge(ao_done, j - 1)
                    empty(f, gate[:, j % 2, :])
                    if j + 2 < KT:
                        act.dma_start(lwt[:, j % 2, :], io["lw"][j + 2]).then_inc(lw_loaded[j % 2], 16)
                elif kind == "kk":
                    act.wait_ge(kk0_ready, j + 1)
                    if j == 0:
                        wait_filled(act, ("ss", "mix2"))
                    else:
                        wait_filled(act, ("kkss", j - 1))
                    act.activation(sq[:, 0, :], kk[:, :], ACT.Square).then_inc(kksq_ready, 1)
                    act.wait_ge(cw_ready, j + 1)
                    if j:
                        act.wait_ge(pool_f, POOL_F * j)
                        act.wait_ge(at_ready, j)
                    else:
                        act.wait_ge(zeros_done, 5)
                    act.activation(ewi[:, :], cw[:, :], ACT.Exp, scale=DECAY).then_inc(exp_ready, 1)
                    act.activation(ew, cw[:, :].rearrange("p (c n) -> p c n", c=NCK), ACT.Exp, scale=-DECAY).then_inc(exp_ready, 1)
                elif kind == "kkss":
                    wait_emptied(act, f)
                    act.activation(nrt[:, :], nrt[:, :], ACT.Sqrt).then_inc(kkroot_done, 1)
                elif kind == "tok":
                    if f[2] == 0:
                        empty(f, ftok[:, :, :, 0, :], bank(f).rearrange("p (t h n) -> p t h n", t=TT, h=2))
                    else:
                        empty(f, (btok, ktok, vtk)[f[2] - 1][:, :, :], bank(f).rearrange("p (t n) -> p t n", t=TT))
                elif kind == "inv":
                    empty(f, ix[f[2]], bank(f).rearrange("p (t n) -> p t n", t=TT))
                elif kind == "akv":
                    empty(f, ftok[:, :, f[2], 1, :], bank(f)[:, 0:TT * RN].rearrange("p (t n) -> p t n", t=TT))
                elif kind == "tav":
                    empty(f, tav[:, :, :, f[2], :], bank(f).rearrange("p (t a n) -> p t a n", t=TT, a=2))
                elif kind == "qq":
                    wait_filled(act, f)
                    if j:
                        wait_emptied(act, ("st", j - 1, NCK - 2))
                    emptied_by(act.activation(qs[:, f[2]::2, :], bank(f)[:, 0:TT * RN].rearrange("p (c n) -> p c n", c=TT), ACT.Copy), f)
                elif kind == "ost":
                    act.wait_ge(ost_done, j + 1)
                    if j:
                        act.wait_ge(ao_done, j)
                    else:
                        act.wait_ge(hl_ready, EVENT["mix2", KT - 1] + 1)
                    act.activation(og, psum[:, OBANK, :], ACT.Copy).then_inc(og_ready, 1)
                elif kind == "gnm":
                    wait_emptied(act, f)
                    act.activation(sq[:, 1, :], og, ACT.Square).then_inc(gnsq_ready, 1)
                elif kind == "gnv":
                    wait_emptied(act, f)
                    act.activation(gnt[:, :], gnt[:, :], ACT.Sqrt).then_inc(gnroot_done, 1)
                elif kind == "aoput":
                    act.wait_ge(ao_done, j + 1)
                    act.dma_start(ao_kept[j], ao[:, j % 2, :]).then_inc(ao_put[j % 2], 16)
                elif kind == "aoload":
                    for i in range(2):
                        act.wait_ge(ao_put[i], 16 * KT // 2)
                    act.dma_start(aof[:, :, :], ao_kept.rearrange("k p s -> p k s")).then_inc(ao_back, 16)
                elif kind == "aosplit":
                    act.wait_ge(ao_back, 16)
                    act.activation(aoh[:, 0, j, :], aof[:, j, :], ACT.Copy).then_inc(ao_hi, 1)
            weights_ahead(SPLIT_AT["pr", 1])
            for k in range(KT):
                if k < KT - 1:
                    act.wait_ge(cen_ready, k + 1)
                else:
                    wait_emptied(act, ("convmean",))
                square("conv", k, x[:, k, :])
                if k % 4 == 3:
                    weights_ahead(SPLIT_AT["pr", 2 + k // 4])
            root("conv")
            act.wait_ge(ao_ready, KT)
            for k in range(KT):
                n = EVENT["conv", k]
                act.wait_ge(convn_ready, k + 1)
                act.wait_ge(hl_ready, n - NTMP + 1)
                act.activation(tmp[:, n % NTMP, :], x[:, k, :], ACT.Silu, bias=vcol("conv_ln_b_2", k)).then_inc(pre_split, 1)
                high(("conv", k), coh[:, 0, k, :])
                weights_ahead(SPLIT_AT["pr", 4 + k // 2])
            act.wait_ge(pre_split, EVENT["conv", KT - 1] + 1)
            act.wait_ge(x_put, 16)
            act.dma_start(x[:, :, :].rearrange("p k s -> p (k s)"), x_kept).then_inc(x_back, 16)
            for m in range(KT):
                weights_ahead(SPLIT_AT["pc", m] + 1)
                high(("y2", m), ah[:, 0, m, :])
            for m in range(KT):
                weights_ahead(SPLIT_AT["wo2", m] + 1)
                if m:
                    wait_emptied(act, ("wo2", m - 1))
                    square("ff2", m - 1, x[:, m - 1, :])
                    high(("early", m - 1), hidden[1][:, 0, m - 1, :])
            weights_ahead(SPLIT_AT["fc1", 2, 0, 1])
            wait_emptied(act, ("wo2", KT - 1))
            square("ff2", KT - 1, x[:, KT - 1, :])
            high(("early", KT - 1), hidden[1][:, 0, KT - 1, :])
            root("ff2")
            weights_ahead(SPLIT_AT["fc1", 2, 0, 2])
            for k in range(KT):
                high(("ff2", k), ah[:, 0, k, :])
                if k in (1, 5):
                    weights_ahead(SPLIT_AT["fc1", 2, 0, 3 + k // 4])
            mlp(2, final2_squares)
            root("final2")

        @block.vector
        def _(dve):
            steps = [0]

            def step(ins):
                steps[0] += 1
                ins.then_inc(dve_step, 1)
                dve.wait_ge(dve_step, steps[0])

            def mean_square(name, n, eps=EPS):
                wait_filled(dve, ("ss", name))
                emptied_by(dve.tensor_scalar(rs[:, 0:TT], bank(("ss", name))[:, 0:TT], 1.0 / n, eps, ALU.mult, ALU.add), ("ss", name))

            def add_square(name, k):
                dve.wait_ge(sq_ready, SQ_AT[name, k] + 1)
                if k > 1:
                    dve.wait_ge(sq_added, ADD_AT[name, k - 1] + 1)
                total = sq_sum[:, SUM_OF[name], :]
                dve.tensor_tensor(total, total, sq[:, SQ_SLOT[name, k] % 2, :], ALU.add).then_inc(sq_added, 1)

            def inverse_root(name):
                dve.wait_ge(root_done, [n for n, _ in NORMS].index(name) + 1)
                dve.reciprocal(roots(name), roots(name)).then_inc(rs_ready, 1)

            def spread_used(name):
                c = 2 * TT + [n for n, _ in NORMS].index(name)
                emptied_by(dve.tensor_copy(rs[:, c:c + 1], bank(("rb", name))[:, 0:1]), ("rb", name))

            def low(event, dst_hi, dst_lo, bias=0.0):
                n = EVENT[event]
                dve.wait_ge(hi_ready, n + 1)
                dve.scalar_tensor_tensor(dst_lo, tmp[:, n % NTMP, :], bias, dst_hi.bitcast(F32), ALU.add,
                                         ALU.subtract).then_inc(hl_ready, 1)

            def slot(event):
                n = EVENT[event]
                if n >= NTMP:
                    dve.wait_ge(hl_ready, n - NTMP + 1)
                return tmp[:, n % NTMP, :]

            def normed(name, n, src, gain, dst, k0, tiles, bias=None, used=True):
                mean_square(name, n)
                inverse_root(name)
                normalize_tiles(name, src, gain, dst, k0, tiles, bias, used)

            def normalize_tiles(name, src, gain, dst, k0, tiles, bias=None, used=True):
                wait_filled(dve, ("rb", name))
                for k in range(tiles + 1):
                    if k < tiles:
                        dve.scalar_tensor_tensor(slot((name, k)), src[:, k, :], gain(k), bank(("rb", name)), ALU.mult,
                                                 ALU.mult).then_inc(pre_split, 1)
                    if k:
                        low((name, k - 1), dst[:, 0, k0 + k - 1, :], dst[:, 1, k0 + k - 1, :], bias(k - 1) if bias else 0.0)
                if used:
                    spread_used(name)

            def ada_take(s, k):
                what = ("ada", s, k)
                n = ADA_AT[what]
                wait_loaded(dve, what)
                if k == 0:
                    if s in (2, 3, 5):
                        wait_filled(dve, ("ada", {2: 0, 3: 1, 5: 4}[s]))
                    ins = dve.tensor_scalar(ada_sum(s), raw_of(what), vcol("c", k), None, ALU.mult)
                else:
                    dve.wait_ge(ada_used, n)
                    ins = dve.scalar_tensor_tensor(ada_sum(s), raw_of(what), vcol("c", k), ada_sum(s), ALU.mult, ALU.add)
                ins.then_inc(ada_used, 1)

            def ada_done(s):
                wait_filled(dve, ("ada", s))
                emptied_by(dve.tensor_tensor(mod[:, KT * s:KT * s + KT], bank(("ada", s))[:, 0:KT], vcol("b_ada", KT * s, KT), ALU.add),
                           ("ada", s))

            dve.wait_ge(vec_loaded, 16)
            for k in range(KT):
                ada_take(0, k)
            mean_square("mix", D)
            for k in range(KT):
                ada_take(1, k)
                if k == 2:
                    inverse_root("mix")
            ada_done(0)
            ada_done(1)
            wait_emptied(dve, ("ada", 1))
            dve.scalar_tensor_tensor(modg[:, 0:KT], mod[:, KT:2 * KT], 1.0, vcol("g_mix", 0, KT), ALU.add,
                                     ALU.mult).then_inc(modg_ready, 1)
            dve.wait_ge(modg_ready, 1)
            normalize_tiles("mix", x, lambda k: modg[:, k:k + 1], ah, 0, KT, lambda k: mod[:, k:k + 1])
            for f in FRONT:
                kind = f[0]
                if kind == "z":
                    ada_take(*ada_beside(f)[1:])
                elif kind == "ada":
                    ada_done(f[1])
                elif kind == "bkv":
                    kv = f[1]
                    wait_emptied(dve, ("z", 4 + kv))
                    for g in range(G):
                        for hi in range(2):
                            src = kcd[:, kv, g, hi * CS:hi * CS + NC * CS].rearrange("p (c r) -> p r c", r=CS)[:, ::2, :]
                            pe8 = vcol(("pe_ck", "pe_cv")[kv], 8 * hi, 8).unsqueeze(2).to_broadcast([P, 8, NC])
                            last = dve.tensor_tensor(bkv[:, kv, 8 * hi:8 * hi + 8, g * NC:g * NC + NC], src, pe8, ALU.add)
                            if (g, hi) != (G - 1, 1):
                                last.then_inc(dve_step, 1)
                                steps[0] += 1
                    last.then_inc(bkv_ready, 1)
                elif f == ("norm", "cq"):
                    normed("cq", QR, zd, lambda k: vcol("g_cq", k), cqh, 0, 3)
                elif f == ("norm", "ckv"):
                    normed("ckv", KVR, zd[:, 3:5, :], lambda k: vcol("g_ckv", k), cqh, 3, 2)

            def attention(tag, units, probs, st, bias, slope, gate):
                base = {"nsa": 0, "mla": len(NSA_UNITS)}[tag]
                per_pair = 2 * TT * (3 if tag == "nsa" else 1)

                def normalize(u):
                    h, qt, br = units[u]
                    w = NC if br == 0 else qt * P + P
                    dve.wait_ge(exp_done, base + u + 1)
                    total, inv = st[:, u % PROBS[tag], 1:2], st[:, u % PROBS[tag], 2:3]
                    if br == 0:
                        step(dve.tensor_scalar(total, total, 1e-30, None, ALU.max))
                    step(dve.reciprocal(inv, total))
                    pr = probs[:, u % PROBS[tag], 0:w]
                    if gate is None:
                        ins = dve.tensor_scalar(pr, pr, inv, None, ALU.mult)
                    else:
                        ins = dve.tensor_scalar(pr, pr, inv, gate(h, qt, br), ALU.mult, ALU.mult)
                    ins.then_inc(p_ready, 1)

                for kind, u in attention_order(tag):
                    h, qt, br = units[u]
                    if kind == "S":
                        w = NC if br == 0 else qt * P + P
                        wait_filled(dve, ("S", tag, u))
                        if u >= PROBS[tag]:
                            wait_filled(dve, ("PT", tag, u - PROBS[tag]))
                        emptied_by(dve.tensor_tensor_reduce(probs[:, u % PROBS[tag], 0:w], bank(("S", tag, u))[:, 0:w], bias(qt, br),
                                                            slope(h), 1e25, ALU.add, ALU.min, st[:, u % PROBS[tag], 0:1]), ("S", tag, u))
                        if u >= 1:
                            normalize(u - 1)
                        if u == len(units) - 1:
                            normalize(u)
                    elif kind == "O" and (u + 1) % per_pair == 0:
                        pair = u // per_pair + (H // 2 if tag == "mla" else 0)
                        dve.wait_ge(o_hi, pair + 1)
                        dve.tensor_tensor(oh[:, 1, pair, :], psum[:, obank(pair), :], oh[:, 0, pair, :].bitcast(F32),
                                          ALU.subtract).then_inc(o_empty, 1)

            def nsa_bias(qt, br):
                return cmpb[:, qt, :] if br == 0 else alibi[:, S - P - qt * P:S]

            for n in ("alibi", "cmpb", "causal", "rope"):
                dve.wait_ge(const_loaded[n], 16)
            wait_emptied(dve, ("gt",))
            attention("nsa", NSA_UNITS, sm, stat, nsa_bias, lambda h: SLOPES[h], lambda h, qt, br: gates[:, qt, br * H + h:br * H + h + 1])
            wait_emptied(dve, ("z", 10))
            step(dve.tensor_tensor(kcat[64:96, 0, :], zkr[64:96, :], rope[64:96, :], ALU.mult))
            step(dve.tensor_tensor(rtmp[64:96, :], zkr[96:128, :], rope[96:128, :], ALU.mult))
            step(dve.tensor_tensor(kcat[64:96, 0, :], kcat[64:96, 0, :], rtmp[64:96, :], ALU.add))
            dve.tensor_copy(kcat[64:96, 1:MH, :], kcat[64:96, 0:1, :].to_broadcast([32, MH - 1, S])).then_inc(krot_done, 1)
            for h in range(MH):
                wait_filled(dve, ("uq", h))
                q = bank(("uq", h))
                if h:
                    dve.wait_ge(rope_done, h)
                step(dve.scalar_tensor_tensor(qcat[64:96, h, :], q[64:96, :], -DQK ** -0.5, rope[64:96, :], ALU.mult, ALU.mult))
                dve.wait_ge(nope_done, h + 1)
                emptied_by(dve.scalar_tensor_tensor(rtmp[64:96, :], q[96:128, :], -DQK ** -0.5, rope[96:128, :], ALU.mult,
                                                    ALU.mult), ("uq", h))
                wait_emptied(dve, ("uq", h))
                dve.tensor_tensor(qcat[64:96, h, :], qcat[64:96, h, :], rtmp[64:96, :], ALU.add).then_inc(rope_done, 1)
            attention("mla", MLA_UNITS, sm2, stat2, lambda qt, br: causal[:, S - P - qt * P:S], lambda h: 1.0, None)
            for m in range(16):
                ada_take(4 + m // KT, m % KT)
                if m == 12:
                    ada_done(4)
            wait_emptied(dve, ("ada", 4))
            dve.scalar_tensor_tensor(modg[:, KT:2 * KT], mod[:, 32:40], 1.0, vcol("g_mlp", 0, KT), ALU.add,
                                     ALU.mult).then_inc(modg_ready, 1)
            for m in range(KT + 1):
                if m == 2:
                    ada_done(5)
                if m < KT:
                    wait_emptied(dve, ("gate", 8 + m))
                    wait_filled(dve, ("on", m))
                    emptied_by(dve.tensor_tensor(sg[:, m, :], bank(("on", m)), sg[:, m, :], ALU.mult), ("on", m))
                    wait_filled(dve, ("om", m))
                    emptied_by(dve.tensor_tensor(sg[:, 8 + m, :], bank(("om", m)), sg[:, 8 + m, :], ALU.mult), ("om", m))
                    wait_emptied(dve, ("on", m))
                    wait_emptied(dve, ("om", m))
                    dve.tensor_tensor(slot(("y", m)), sg[:, m, :], sg[:, 8 + m, :], ALU.add).then_inc(pre_split, 1)
                if m:
                    low(("y", m - 1), yh[:, 0, m - 1, :], yh[:, 1, m - 1, :])
            for m in range(KT):
                wait_filled(dve, ("wo", m))
                emptied_by(dve.scalar_tensor_tensor(x[:, m, :], bank(("wo", m)), mod[:, 16 + m:17 + m], x[:, m, :], ALU.mult,
                                                    ALU.add), ("wo", m))
                if m >= 2:
                    add_square("mlp", m - 1)
            add_square("mlp", KT - 1)
            dve.wait_ge(modg_ready, 2)
            normed("mlp", D, x, lambda k: modg[:, KT + k:KT + k + 1], ah, 0, KT, lambda k: mod[:, 24 + k:25 + k])

            def mlp(n, gate, last):
                for half, c in mlp_order():
                    for m in range(KT):
                        if half == 1:
                            what = ("fc1", n, c, m)
                            wait_emptied(dve, what)
                            e = EVENT["hid", n, c, m]
                            if n == 2 and c == 0 and m < EARLY:
                                step(dve.tensor_tensor(sq[:, e % 2, :], sq[:, e % 2, :], bank(("rb", "ff2")), ALU.mult))
                                if m == EARLY - 1:
                                    spread_used("ff2")
                            dve.tensor_tensor(slot(("hid", n, c, m)), sq[:, e % 2, :], sq[:, e % 2, :], ALU.mult).then_inc(pre_split, 1)
                            low(("hid", n, c, m), hidden[c % 2][:, 0, m, :], hidden[c % 2][:, 1, m, :])
                        else:
                            what = ("fc2", n, c, m)
                            wait_filled(dve, what)
                            if c:
                                wait_emptied(dve, ("fc2", n, c - 1, m))
                            if gate is None:
                                emptied_by(dve.tensor_tensor(x[:, m, :], bank(what), x[:, m, :], ALU.add), what)
                            else:
                                emptied_by(dve.scalar_tensor_tensor(x[:, m, :], bank(what), gate(m), x[:, m, :], ALU.mult,
                                                                    ALU.add), what)
                            if n == 1 and c == NCH - 1:
                                if m:
                                    low(("early2", m - 1), ah[:, 0, m - 1, :], ah[:, 1, m - 1, :])
                                into = slot(("early2", m))
                                wait_emptied(dve, what)
                                dve.tensor_scalar(into, x[:, m, :], gains2[:, m:m + 1], None, ALU.mult).then_inc(pre_split, 1)
                            for name in last if c == NCH - 1 and m >= 2 else ():
                                add_square(name, m - 1)
                for name in last:
                    add_square(name, KT - 1)
                if n == 1:
                    low(("early2", KT - 1), ah[:, 0, KT - 1, :], ah[:, 1, KT - 1, :])

            gains2 = rs[:, 2 * TT + len(NORMS):]
            step(dve.tensor_tensor(gains2, vcol("g_final", 0, KT), vcol("norm_mix_g_2", 0, KT), ALU.mult))
            mlp(1, lambda m: mod[:, 40 + m:41 + m], ("final", "mix2"))

            def normed_in_place(name, gain):
                mean_square(name, D)
                inverse_root(name)
                wait_filled(dve, ("rb", name))
                for k in range(KT):
                    dve.scalar_tensor_tensor(x[:, k, :], x[:, k, :], vcol(gain, k), bank(("rb", name)), ALU.mult, ALU.mult).then_inc(xn_ready, 1)
                spread_used(name)

            mean_square("final", D)
            inverse_root("final")
            dve.wait_ge(rs_ready, [n for n, _ in NORMS].index("final") + 1)
            wait_filled(dve, ("ss", "mix2"))
            step(dve.scalar_tensor_tensor(roots("mix2"), roots("final"), 1.0 / D, roots("final"), ALU.mult, ALU.mult))
            step(dve.tensor_tensor(roots("mix2"), bank(("ss", "mix2"))[:, 0:TT], roots("mix2"), ALU.mult))
            emptied_by(dve.tensor_scalar(roots("mix2"), roots("mix2"), EPS, None, ALU.add), ("ss", "mix2"))
            dve.wait_ge(root_done, [n for n, _ in NORMS].index("mix2") + 1)
            step(dve.reciprocal(roots("mix2"), roots("mix2")))
            dve.tensor_tensor(roots("mix2"), roots("mix2"), roots("final"), ALU.mult).then_inc(rs_ready, 1)

            dve.wait_ge(const_loaded["rw"], 16)
            taps = [0, CONV]

            def convolve(n):
                j, done = taps
                if (j, done) == (0, 0):
                    dve.wait_ge(x_put, 16)
                for w in range(done, min(done + n, CONV)):
                    src, tap, acc = upad[:, w:w + S], vcol("conv_w_2", 8 * w + j), x[:, j, :]
                    if w == 0:
                        ins = dve.tensor_scalar(acc, src, tap, vcol("conv_b_2", j), ALU.mult, ALU.add)
                    else:
                        ins = dve.scalar_tensor_tensor(acc, src, tap, acc, ALU.mult, ALU.add)
                    if w < CONV - 1:
                        step(ins)
                    else:
                        ins.then_inc(conv_done, 1)
                    taps[1] += 1

            dve.wait_ge(zeros_done, 5)
            step(dve.tensor_scalar(omu[:, 0:24], vcol("mu_rkv_2", 0, 24), -1.0, 1.0, ALU.mult, ALU.add))
            step(dve.tensor_scalar(omu[:, 24:48], vcol("mu_lora_2", 0, 24), -1.0, 1.0, ALU.mult, ALU.add))
            for f in rwkv_order():
                kind, j = f[0], f[1]
                if kind == "mix":
                    i = f[2]
                    n = (1, 0, 2).index(i)
                    what = ("rkv", j, i)
                    dve.wait_ge(mu_ready, 3 * j + n + 1)
                    if j:
                        dve.wait_ge(pool_f, POOL_F * j)
                        wait_emptied(dve, ("bonus", j - 1))
                        wait_filled(dve, ("tok", j - 1, 3))
                    emptied_by(dve.scalar_tensor_tensor(rkv[:, i, :], bank(what), omu[:, 8 * i + j:8 * i + j + 1], rkvp[:, RKV_SLOT[i], 0:S],
                                                        ALU.mult, ALU.add), what)
                elif kind == "factor":
                    if j == 1:
                        wait_filled(dve, ("rb", "mix2"))
                        step(dve.tensor_copy(sq[:, 0, :], bank(("rb", "mix2"))))
                    wait_filled(dve, ("rkv", 0, j))
                    b = bank(("rkv", 0, j))
                    dve.tensor_tensor(b, b, sq[:, 0, :], ALU.mult).then_inc(factor_done, 1)
                elif kind == "norm2":
                    dve.scalar_tensor_tensor(slot(("mix2", j)), x[:, j, :], gains2[:, j:j + 1], bank(("rb", "mix2")),
                                             ALU.mult, ALU.mult).then_inc(pre_split, 1)
                    if j == KT - 1:
                        spread_used("mix2")
                elif kind == "xn":
                    wait_filled(dve, ("rb", "final"))
                    for k in range(KT):
                        dve.scalar_tensor_tensor(x[:, k, :], x[:, k, :], vcol("g_final", k), bank(("rb", "final")), ALU.mult,
                                                 ALU.mult).then_inc(xn_ready, 1)
                    spread_used("final")
                elif kind == "scale":
                    i, last = j, f[2]
                    what = ("lora", i, last)
                    wait_loaded(dve, what)
                    w = raw_of(what).rearrange("p (k n) -> p k n", k=KT)
                    for q in ((0, 1), (2,))[i]:
                        cols = slice(0, P) if i else slice(q * LORA, q * LORA + LORA)
                        mu = vcol("mu_lora_2", 8 * q, 8) if last else omu[:, 24 + 8 * q:32 + 8 * q]
                        ins = dve.tensor_tensor(w[:, :, cols], w[:, :, cols],
                                                mu.unsqueeze(2).to_broadcast([P, KT, cols.stop - cols.start]), ALU.mult)
                        if (i, q) == (0, 0):
                            steps[0] += 1
                            ins.then_inc(dve_step, 1)
                    ins.then_inc(lora_scaled, 1)
                elif kind == "hidden":
                    wait_emptied(dve, ("lora", j, 1))
                    wait_filled(dve, ("lora", j, 0))
                    pre = (btok, ktok)[j].rearrange("p t n -> p (t n)")
                    emptied_by(dve.tensor_tensor(pre, bank(("lora", j, 0)), spare(j)[:, 0:S], ALU.add), ("lora", j, 0))
                elif kind == "scan":
                    wait_emptied(dve, ("lw2", j))
                    if j:
                        wait_filled(dve, ("tok", j - 1, 2))
                    for c in range(NCK):
                        cols = slice(c * CH, c * CH + CH)
                        last = dve.tensor_tensor_scan(cw[:, cols], ones[:, 0:CH], sw[:, cols], 0.0, ALU.mult, ALU.add)
                        if c < NCK - 1:
                            steps[0] += 1
                            last.then_inc(dve_step, 1)
                    last.then_inc(cw_ready, 1)
                elif kind == "kk":
                    wait_emptied(dve, ("la2", j))
                    wait_emptied(dve, ("rkv", j, 1))
                    wait_emptied(dve, ("rkv", j, 0))
                    if j:
                        dve.wait_ge(pool_f, POOL_F * (j - 1) + 3)
                        wait_filled(dve, ("bonus", j - 1))
                    dve.tensor_scalar(kk[:, :], rkv[:, 1, :], vcol("k_k_2", j), None, ALU.mult).then_inc(kk0_ready, 1)
                    step(dve.tensor_scalar(tf, rate[:, :], -1.0, vcol("k_a_2", j), ALU.add, ALU.mult))
                    dve.wait_ge(kk0_ready, j + 1)
                    dve.scalar_tensor_tensor(rkv[:, 1, :], tf, 1.0, rkv[:, 1, :], ALU.add, ALU.mult).then_inc(kmod_ready, 1)
                    dve.wait_ge(kmod_ready, j + 1)
                    dve.scalar_tensor_tensor(tf, rkv[:, 0, :], vcol("r_k_2", j), rkv[:, 1, :], ALU.mult, ALU.mult).then_inc(rk_ready, 1)
                elif kind == "kkss":
                    wait_filled(dve, f)
                    if j:
                        wait_filled(dve, ("kkb", j - 1))
                    emptied_by(dve.tensor_scalar(nrt[:, :], bank(f)[:, 0:2 * TT], KK_EPS * KK_EPS, None, ALU.max), f)
                    dve.wait_ge(kkroot_done, j + 1)
                    dve.reciprocal(nrt[:, :], nrt[:, :]).then_inc(nrm_ready, 1)
                elif kind == "kkb":
                    wait_filled(dve, f)
                    dve.wait_ge(kksq_ready, j + 1)
                    emptied_by(dve.tensor_tensor(kk[:, :], kk[:, :], bank(f), ALU.mult), f)
                    dve.wait_ge(exp_ready, 2 * j + 2)
                    step(dve.tensor_copy(wc[:, j % 2, :], ew[:, :, CH - 1]))
                elif kind == "at":
                    wait_emptied(dve, ("kkb", j))
                    if j:
                        wait_filled(dve, ("mk", j - 1, 1))
                    dve.scalar_tensor_tensor(arow[:, :, 0, :].rearrange("p t (c n) -> p t c n", c=2),
                                             kk[:, :].rearrange("p (t c n) -> p t c n", t=TT, c=2), -1.0,
                                             ewp.rearrange("p (t c) n -> p t c n", t=TT), ALU.mult, ALU.mult).then_inc(at_ready, 1)
                elif kind == "bonus":
                    wait_filled(dve, f)
                    wait_emptied(dve, ("rkv", j, 2))
                    emptied_by(dve.tensor_tensor(bv[:, j % 2, :], bank(f), rkv[:, 2, :], ALU.mult), f)
                elif kind == "part" and f[1][:1] + f[1][2:] == ("glu", 0) and f[3] == KT:
                    what = f[1]
                    j = what[1]
                    convolve(CONV)
                    taps[:] = [j, 0]
                    wait_emptied(dve, ("glu", j, 1))
                    wait_filled(dve, what)
                    if j == 0:
                        dve.wait_ge(zeros_done, 5)
                    else:
                        dve.wait_ge(conv_done, j)
                    emptied_by(dve.tensor_tensor(upad[:, CONV - 1:], bank(what), usig, ALU.mult), what)
                    wait_emptied(dve, what)
                elif kind == "conv":
                    convolve(f[2])
                elif kind == "iy0" and f[2] == 0:
                    wait_emptied(dve, ("mb", j, 0))
                    if j:
                        wait_filled(dve, ("tav", j - 1, 0))
                    step(dve.tensor_tensor(ip[0], ma[0], level[0].unsqueeze(1).to_broadcast([P, TT, CH]), ALU.mult))
                    dve.tensor_tensor(iy2[0], ip[0].unsqueeze(2).to_broadcast([P, TT, 2, CH]),
                                      own_eye.unsqueeze(1).unsqueeze(1).to_broadcast([P, TT, 2, CH]), ALU.add).then_inc(iy0_done[0], 1)
                elif kind in ("mb", "mk"):
                    wait_filled(dve, f)
                    if j:
                        dve.wait_ge(opa_done if kind == "mb" else opv_done, 2 * j - 1 + f[2])
                    own, both_chunks = ((ma, mr) if kind == "mb" else (ka, kr))
                    full = bank(f).rearrange("p (t n) -> p t n", t=TT)
                    steps[0] += 1
                    dve.tensor_tensor(own[f[2]], full[:, :, 0:CH], strict.unsqueeze(1).to_broadcast([P, TT, CH]), ALU.mult).then_inc(dve_step, 1)
                    for t in range(TT):
                        last = dve.tensor_tensor(both_chunks[f[2]][:, t, :].rearrange("p (c n) -> p c n", c=2),
                                                 full[:, t, CH:P].unsqueeze(1).to_broadcast([P, 2, CH]),
                                                 incl.rearrange("p (c n) -> p c n", c=2), ALU.mult)
                        if t < TT - 1:
                            steps[0] += 1
                            last.then_inc(dve_step, 1)
                    emptied_by(last, f)
                elif kind == "ip":
                    wait_filled(dve, f)
                    emptied_by(dve.tensor_tensor(ip[f[2]], bank(f)[:, 0:TT * CH].rearrange("p (t n) -> p t n", t=TT),
                                                 level[f[3]].unsqueeze(1).to_broadcast([P, TT, CH]), ALU.mult), f)
                elif kind == "iy":
                    wait_filled(dve, f)
                    if f[3] == 1:
                        dve.wait_ge(iy0_done[f[2]], j + 1)
                    else:
                        wait_emptied(dve, ("iy", j, f[2], f[3] - 1))
                    emptied_by(dve.tensor_tensor(iy2[f[2]], bank(f)[:, 0:TT * CH].rearrange("p (t n) -> p t n", t=TT)
                                                 .unsqueeze(2).to_broadcast([P, TT, 2, CH]), iy2[f[2]], ALU.add), f)
                elif kind == "rr":
                    hh = f[2]
                    rows = slice(RN * hh, RN * hh + RN)
                    wait_filled(dve, f)
                    dve.wait_ge(pool_f, POOL_F * j + 6)
                    if j:
                        dve.wait_ge(ost_done, j)
                    emptied_by(dve.tensor_tensor(rp[rows, :].rearrange("p (t n) -> p t n", t=TT),
                                                 bank(f)[rows, :].rearrange("p (t n) -> p t n", t=TT), arow[rows, :, 1, :], ALU.add), f)
                elif kind == "pt":
                    wait_filled(dve, f)
                    emptied_by(dve.tensor_copy(pts[:, f[2]::2, :], bank(f)[:, 0:TT * RN].rearrange("p (c n) -> p c n", c=TT)), f)
                elif kind == "st":
                    c = f[2]
                    if c == 1:
                        wait_emptied(dve, ("qq", j, 0))
                        wait_emptied(dve, ("qq", j, 1))
                        if j:
                            dve.wait_ge(ost_done, j)
                    dve.scalar_tensor_tensor(su[:, :], state(c), wc[:, j % 2, c:c + 1], qs[:, c, :], ALU.mult, ALU.add).then_inc(u_ready, 1)
                    dve.wait_ge(u_ready, (NCK - 2) * j + c)
                    wait_filled(dve, f)
                    emptied_by(dve.tensor_tensor(st[:, c + 1, :], bank(f)[:, 0:RN], su[:, :], ALU.add), f)
                    wait_emptied(dve, f)
                elif kind == "gnm":
                    wait_filled(dve, f)
                    emptied_by(dve.scalar_tensor_tensor(og, bank(f), -1.0 / RN, og, ALU.mult, ALU.add), f)
                elif kind == "gnv":
                    wait_filled(dve, f)
                    if j:
                        wait_filled(dve, ("gnb", j - 1))
                    emptied_by(dve.tensor_scalar(gnt[:, :], bank(f)[:, 0:2 * TT], 1.0 / RN, GN_EPS, ALU.mult, ALU.add), f)
                    dve.wait_ge(gnroot_done, j + 1)
                    dve.reciprocal(gnt[:, :], gnt[:, :]).then_inc(gnr_ready, 1)
                elif kind == "gnend":
                    wait_filled(dve, ("gnb", j))
                    emptied_by(dve.scalar_tensor_tensor(og, og, vcol("ln_x_g_2", j), bank(("gnb", j)), ALU.mult, ALU.mult), ("gnb", j))
                    wait_emptied(dve, ("gnb", j))
                    step(dve.scalar_tensor_tensor(og, og, vcol("ln_x_b_2", j), bv[:, j % 2, :], ALU.add, ALU.add))
                    if j >= 2:
                        dve.wait_ge(ao_put[j % 2], 16 * (j // 2))
                    dve.tensor_tensor(ao[:, j % 2, :], og, gate[:, j % 2, :], ALU.mult).then_inc(ao_done, 1)
                elif kind == "aosplit":
                    if j == 0:
                        convolve(CONV)
                    dve.wait_ge(ao_hi, j + 1)
                    dve.tensor_tensor(aoh[:, 1, j, :], aof[:, j, :], aoh[:, 0, j, :].bitcast(F32), ALU.subtract).then_inc(ao_ready, 1)
            wait_filled(dve, ("convmean",))
            for k in range(KT):
                if k == KT - 1:
                    dve.wait_ge(conv_done, KT)
                ins = dve.scalar_tensor_tensor(x[:, k, :], bank(("convmean",)), -1.0 / D, x[:, k, :], ALU.mult, ALU.add)
                if k < KT - 1:
                    ins.then_inc(cen_ready, 1)
                else:
                    emptied_by(ins, ("convmean",))
                if k >= 2:
                    add_square("conv", k - 1)
            add_square("conv", KT - 1)

            def gated(name, m):
                i = m if name == "pr" else 8 + m
                wait_emptied(dve, ("gate2", i))
                wait_filled(dve, (name, m))
                emptied_by(dve.tensor_tensor(merge_gate(i), bank((name, m)), merge_gate(i), ALU.mult), (name, m))

            for m in range(2):
                gated("pr", m)
            mean_square("conv", D, LN_EPS)
            inverse_root("conv")
            wait_filled(dve, ("rb", "conv"))
            for k in range(KT + 1):
                if k < KT:
                    dve.scalar_tensor_tensor(x[:, k, :], x[:, k, :], vcol("conv_ln_g_2", k), bank(("rb", "conv")), ALU.mult,
                                             ALU.mult).then_inc(convn_ready, 1)
                if k:
                    low(("conv", k - 1), coh[:, 0, k - 1, :], coh[:, 1, k - 1, :])
                if 2 <= k <= 4:
                    gated("pr", k)
            spread_used("conv")
            for m in range(5, KT):
                gated("pr", m)
            for m in range(KT + 1):
                if m < KT:
                    gated("pc", m)
                    wait_emptied(dve, ("pr", m))
                    wait_emptied(dve, ("pc", m))
                    dve.tensor_tensor(slot(("y2", m)), merge_gate(m), merge_gate(8 + m), ALU.add).then_inc(pre_split, 1)
                if m:
                    low(("y2", m - 1), ah[:, 0, m - 1, :], ah[:, 1, m - 1, :])
            dve.wait_ge(x_back, 16)
            for m in range(KT):
                wait_filled(dve, ("wo2", m))
                emptied_by(dve.tensor_tensor(x[:, m, :], bank(("wo2", m)), x[:, m, :], ALU.add), ("wo2", m))
                if m:
                    low(("early", m - 1), hidden[1][:, 0, m - 1, :], hidden[1][:, 1, m - 1, :])
                into = slot(("early", m))
                wait_emptied(dve, ("wo2", m))
                dve.tensor_scalar(into, x[:, m, :], vcol("norm_ff_g_2", m), None, ALU.mult).then_inc(pre_split, 1)
                if m >= 2:
                    add_square("ff2", m - 1)
            add_square("ff2", KT - 1)
            low(("early", KT - 1), hidden[1][:, 0, KT - 1, :], hidden[1][:, 1, KT - 1, :])
            normed("ff2", D, x, lambda k: vcol("norm_ff_g_2", k), ah, 0, KT, used=False)
            mlp(2, None, ("final2",))
            normed_in_place("final2", "norm_final_g_2")


def tiles_of(w):
    k, n = w.shape
    return w.reshape(k // P, P, n).transpose(1, 0, 2).reshape(P, -1)


def columns_of(v):
    return v.reshape(-1, P).T


def padded(a, n=D):
    return a if a.shape[1] == n else np.concatenate([a, np.zeros((P, n - a.shape[1]), a.dtype)], 1)


def block_of(what, w):
    kind = what[0]
    w_in = w["w_in"]
    if kind == "ada":
        return w["w_ada"][what[2] * P:what[2] * P + P, what[1] * D:what[1] * D + D]
    if kind == "z":
        m = what[1]
        if m < 10:
            return tiles_of(w_in[:, m * P:m * P + P])
        if m == 10:
            zero = np.zeros((D, 40), w_in.dtype)
            return tiles_of(np.concatenate([w_in[:, 1280:1304], zero, w_in[:, 1944:1976], w_in[:, 1960:1976],
                                            w_in[:, 1944:1960]], 1))
        return tiles_of(w_in[:, 1304 + (m - 11) * P:1304 + (m - 10) * P])
    if kind == "ck":
        src = w["w_ck1"] if what[1] == 0 else w["w_cv1"]
        return tiles_of(src[what[2] * S:what[2] * S + S])
    if kind == "uq":
        parts = []
        for h in (2 * what[1], 2 * what[1] + 1):
            q = w["w_uq"][:, h * DQK:h * DQK + DQK]
            parts.append(tiles_of(np.concatenate([q, q[:, NOPE + 16:], q[:, NOPE:NOPE + 16]], 1)))
        return padded(np.concatenate(parts, 1))
    if kind == "uk":
        return np.concatenate([tiles_of(w["w_uk"][:, i * P:i * P + P]) for i in range(MH // 2)], 1)
    if kind == "uv":
        return tiles_of(w["w_uv"])
    if kind == "gate":
        return tiles_of(w_in[:, 1976 + what[1] * P:1976 + what[1] * P + P])
    if kind == "nm":
        cols = slice(what[1] * P, what[1] * P + P)
        return np.concatenate([tiles_of(w["w_o_nsa"][:, cols]), tiles_of(w["w_o_mla"][:, cols])], 1)
    if kind == "wo":
        return tiles_of(w["w_out"][:, what[1] * P:what[1] * P + P])
    w2 = w["w_in_2"]
    if kind == "lora":
        return tiles_of(np.concatenate([w["decay_w1_2"], w["aaa_a1_2"]], 1) if what[1] == 0 else w["gate_g1_2"])
    if kind in ("rkv", "glu"):
        c0 = (0 if kind == "rkv" else 3 * D) + what[2] * D + what[1] * P
        return tiles_of(w2[:, c0:c0 + P])
    if kind == "gate2":
        return tiles_of(w2[:, 5 * D + what[1] * P:5 * D + what[1] * P + P])
    if kind in ("pr", "pc", "wo2"):
        src = w[{"pr": "w_rwkv_proj_2", "pc": "w_conv_proj_2", "wo2": "w_out_2"}[kind]]
        return tiles_of(src[:, what[1] * P:what[1] * P + P])
    _, n, c, m = what
    up, down = (w["w_fc1"], w["w_fc2"]) if n == 1 else (w["w_ff1_2"], w["w_ff2_2"])
    if kind == "fc1":
        return tiles_of(up[:, (c * KT + m) * P:(c * KT + m + 1) * P])
    return tiles_of(down[c * D:c * D + D, m * P:m * P + P])


def kernel(**inputs):
    import concourse.bacc as bacc
    from concourse.bass_utils import run_bass_kernel_spmd

    w = {n: np.asarray(a) for n, a in inputs.items()}
    w = {n: a[0] if a.ndim > 1 and a.shape[0] == 1 else a for n, a in w.items()}
    vecs = []
    for name in VEC:
        if name in ("pe_ck", "pe_cv"):
            vecs.append(w[name].reshape(LP, P).T)
        elif name == "w_ck2":
            vecs.append(tiles_of(np.concatenate([w[name], w[name]], 1)))
        elif name == "w_cv2":
            vecs.append(tiles_of(w[name]))
        elif name in ("mu_lora_2", "conv_w_2", "r_k_2"):
            vecs.append(columns_of(w[name].reshape(-1)))
        else:
            vecs.append(columns_of(w[name]))
    arrays = {
        "x": np.ascontiguousarray(tiles_of(w["x"].T)),
        "vec": np.ascontiguousarray(np.concatenate(vecs, 1)),
        "w": np.stack([block_of(what, w) for _, what in BLOCKS]),
    }
    both = np.concatenate([w["decay_w2_2"], w["aaa_a2_2"]], 0)
    arrays["lw"] = np.stack([np.concatenate([both[:, j * P:j * P + P], w["gate_g2_2"][:, j * P:j * P + P]], 1) for j in range(KT)])
    arrays.update({n: np.ascontiguousarray(a) for n, a in block1_constants().items()})
    arrays["rw"] = rwkv_constants()
    nc = bacc.Bacc("TRN2", target_bir_lowering=False, num_devices=1)
    io = {n: nc.dram_tensor(f"in_{n}", a.shape, F32, kind="ExternalInput").ap() for n, a in arrays.items()}
    io["out"] = nc.dram_tensor("out", (P, KT * S), F32, kind="ExternalOutput").ap()
    build_program(nc, io)
    r = run_bass_kernel_spmd(nc, [{f"in_{n}": a for n, a in arrays.items()}], core_ids=[0])
    got = np.asarray(r.results[0]["out"])
    return np.ascontiguousarray(got.reshape(P, KT, S).transpose(2, 1, 0).reshape(1, S, D))
```
